# Optimizing a Trainium2 kernel written in Bass

```python
import math
import jax, jax.numpy as jnp
from jax import lax
import numpy as np

D_MODEL = 1024
BATCH = 1
SEQ = 512
DEPTH = 1

CHUNK = 64
D_MIX = D_MODEL
FOX_HEADS = 8
FOX_HEAD_DIM = 64
FOX_WIDTH = FOX_HEADS * FOX_HEAD_DIM
HGRN_HEADS = 4
HGRN_HEAD_DIM = 128
HGRN_WIDTH = HGRN_HEADS * HGRN_HEAD_DIM
Q_BLOCK = 128
PEER_HEADS = 8
PEER_QUERY_DIM = 256
N_KEYS = 128
N_EXPERTS = N_KEYS * N_KEYS
PEER_TOPK = 16
PEER_TOKEN_BLOCK = 128
N_MOD = 6
EPS = 1e-6
SPLIT_SIZES = (FOX_WIDTH, FOX_WIDTH, FOX_WIDTH, FOX_HEADS,
               HGRN_WIDTH, HGRN_WIDTH, HGRN_WIDTH, HGRN_WIDTH)
D_IN = sum(SPLIT_SIZES)

kernel_name = "hybrid_fox_hgrn2_peer_block"

def _rmsnorm(x, g):
    x32 = x.astype(jnp.float32)
    y = x32 * lax.rsqrt(jnp.mean(x32 * x32, axis=-1, keepdims=True) + EPS)
    return (y * g.astype(jnp.float32)).astype(x.dtype)

def _forgetting_attention(q, k, v, logf):
    B, S, H, Dh = q.shape
    F = jnp.cumsum(logf, axis=1).transpose(0, 2, 1)
    scale = Dh ** -0.5
    outs = []
    for start in range(0, S, Q_BLOCK):
        end = start + Q_BLOCK
        qb, kb, vb = q[:, start:end], k[:, :end], v[:, :end]
        logits = (jnp.einsum('bqhd,bkhd->bhqk', qb, kb).astype(jnp.float32) * scale
                  + F[:, :, start:end, None] - F[:, :, None, :end])
        mask = (start + jnp.arange(Q_BLOCK))[:, None] >= jnp.arange(end)[None, :]
        p = jax.nn.softmax(jnp.where(mask[None, None], logits, -jnp.inf), axis=-1)
        outs.append(jnp.einsum('bhqk,bkhd->bqhd', p.astype(v.dtype), vb))
    return jnp.concatenate(outs, axis=1)

def _hgrn2_chunkwise(q, f, inp):
    B, S, H, Dk = q.shape
    Dv = inp.shape[-1]
    n = S // CHUNK
    f32 = jnp.float32

    def to_chunks(a):
        return a.astype(f32).reshape(B, n, CHUNK, H, a.shape[-1]).transpose(1, 0, 3, 2, 4)

    qc = to_chunks(q) * (Dk ** -0.5)
    kc = to_chunks(1.0 - f)
    lfc = to_chunks(jnp.log(f))
    ic = to_chunks(inp)
    tri = jnp.tril(jnp.ones((CHUNK, CHUNK), dtype=bool))

    def step(state, xs):
        q_, k_, i_, lf_ = xs
        A = jnp.cumsum(lf_, axis=2)
        o_inter = jnp.einsum('bhtk,bhkv->bhtv', q_ * jnp.exp(A), state)
        diff = A[:, :, :, None, :] - A[:, :, None, :, :]
        decay = jnp.exp(jnp.where(tri[:, :, None], diff, -jnp.inf))
        scores = jnp.einsum('bhtk,bhsk,bhtsk->bhts', q_, k_, decay)
        o_intra = jnp.einsum('bhts,bhsv->bhtv', scores, i_)
        A_last = A[:, :, -1:, :]
        new_state = (jnp.exp(A_last[:, :, 0, :])[..., None] * state
                     + jnp.einsum('bhsk,bhsv->bhkv', k_ * jnp.exp(A_last - A), i_))
        return new_state, o_inter + o_intra

    s0 = jnp.zeros((B, H, Dk, Dv), f32)
    _, o = lax.scan(step, s0, (qc, kc, ic, lfc))
    return o.transpose(1, 0, 3, 2, 4).reshape(B, S, H, Dv).astype(inp.dtype)

def _peer(h, w_q, sub_keys, u, v):
    B, S, D = h.shape
    T = B * S
    ht = h.reshape(T, D)
    q = (ht @ w_q).astype(jnp.float32).reshape(T, PEER_HEADS, 2, PEER_QUERY_DIM // 2)
    q = q * lax.rsqrt(jnp.mean(q * q, axis=-1, keepdims=True) + EPS)
    scores = jnp.einsum('thpd,hpnd->thpn', q, sub_keys.astype(jnp.float32))
    s_top, i_top = lax.top_k(scores, PEER_TOPK)
    cand = (s_top[:, :, 0, :, None] + s_top[:, :, 1, None, :]).reshape(T, PEER_HEADS, PEER_TOPK * PEER_TOPK)
    cand_idx = (i_top[:, :, 0, :, None] * N_KEYS + i_top[:, :, 1, None, :]).reshape(T, PEER_HEADS, PEER_TOPK * PEER_TOPK)
    best, pos = lax.top_k(cand, PEER_TOPK)
    idx = jnp.take_along_axis(cand_idx, pos, axis=-1)
    gate = jax.nn.softmax(best, axis=-1)
    E = PEER_HEADS * PEER_TOPK
    nblk = T // PEER_TOKEN_BLOCK

    def expert_block(args):
        xb, ib, gb = args
        a = jnp.einsum('td,ted->te', xb, u[ib])
        act = (gb * jax.nn.gelu(a.astype(jnp.float32), approximate=False)).astype(xb.dtype)
        return jnp.einsum('te,ted->td', act, v[ib])

    out = lax.map(expert_block, (ht.reshape(nblk, PEER_TOKEN_BLOCK, D),
                                 idx.reshape(nblk, PEER_TOKEN_BLOCK, E),
                                 gate.reshape(nblk, PEER_TOKEN_BLOCK, E)))
    return out.reshape(B, S, D)

def setup_inputs(seed: int = 0) -> dict:
    key = jax.random.key(seed)
    ks = jax.random.split(key, 17)
    nrm = jax.random.normal
    D = D_MODEL
    return {
        'x': nrm(ks[0], (BATCH, SEQ, D), jnp.float32),
        'c': nrm(ks[1], (BATCH, D), jnp.float32),
        'w_ada': nrm(ks[2], (DEPTH, D, N_MOD * D), jnp.float32) * (0.1 * D ** -0.5),
        'b_ada': nrm(ks[3], (DEPTH, N_MOD * D), jnp.float32) * 0.3,
        'pre_mix_g': 1.0 + 0.05 * nrm(ks[4], (DEPTH, D), jnp.float32),
        'post_mix_g': 1.0 + 0.05 * nrm(ks[5], (DEPTH, D), jnp.float32),
        'w_in': nrm(ks[6], (DEPTH, D, D_IN), jnp.float32) * D ** -0.5,
        'b_fox_f': 2.0 + 0.5 * nrm(ks[7], (DEPTH, FOX_HEADS), jnp.float32),
        'hgrn_gamma': 0.5 * nrm(ks[8], (DEPTH + 1, HGRN_WIDTH), jnp.float32),
        'hgrn_norm_g': 1.0 + 0.05 * nrm(ks[9], (DEPTH, HGRN_WIDTH), jnp.float32),
        'w_out': nrm(ks[10], (DEPTH, D_MIX, D), jnp.float32) * D_MIX ** -0.5,
        'pre_ffn_g': 1.0 + 0.05 * nrm(ks[11], (DEPTH, D), jnp.float32),
        'post_ffn_g': 1.0 + 0.05 * nrm(ks[12], (DEPTH, D), jnp.float32),
        'peer_w_q': nrm(ks[13], (DEPTH, D, PEER_HEADS * PEER_QUERY_DIM), jnp.float32) * D ** -0.5,
        'peer_sub_keys': nrm(ks[14], (DEPTH, PEER_HEADS, 2, N_KEYS, PEER_QUERY_DIM // 2), jnp.float32) * (PEER_QUERY_DIM // 2) ** -0.5,
        'peer_u': nrm(ks[15], (DEPTH, N_EXPERTS, D), jnp.float32) * D ** -0.5,
        'peer_v': nrm(ks[16], (DEPTH, N_EXPERTS, D), jnp.float32) * D ** -0.5,
    }

def reference(x, c, w_ada, b_ada, pre_mix_g, post_mix_g, w_in, b_fox_f, hgrn_gamma,
              hgrn_norm_g, w_out, pre_ffn_g, post_ffn_g, peer_w_q, peer_sub_keys,
              peer_u, peer_v):
    B, S, D = x.shape
    lower_bounds = jnp.cumsum(jax.nn.softmax(hgrn_gamma.astype(jnp.float32), axis=0), axis=0)
    cond = jax.nn.silu(c)
    split_idx = [int(s) for s in np.cumsum(SPLIT_SIZES)[:-1]]
    for l in range(DEPTH):
        mod = cond @ w_ada[l] + b_ada[l]
        shift_a, scale_a, gate_a, shift_f, scale_f, gate_f = [m[:, None, :] for m in jnp.split(mod, N_MOD, axis=-1)]

        h = _rmsnorm(x, pre_mix_g[l]) * (1.0 + scale_a) + shift_a
        proj = h @ w_in[l]
        fq, fk, fv, ff, hq, hf, hi, hg = jnp.split(proj, split_idx, axis=-1)

        logf = jax.nn.log_sigmoid(ff.astype(jnp.float32) + b_fox_f[l].astype(jnp.float32))
        shp_f = (B, S, FOX_HEADS, FOX_HEAD_DIM)
        o_fox = _forgetting_attention(fq.reshape(shp_f), fk.reshape(shp_f), fv.reshape(shp_f), logf)
        o_fox = o_fox.reshape(B, S, FOX_WIDTH)

        lb = lower_bounds[l]
        f = lb + (1.0 - lb) * jax.nn.sigmoid(hf.astype(jnp.float32))
        shp_h = (B, S, HGRN_HEADS, HGRN_HEAD_DIM)
        o_h = _hgrn2_chunkwise(hq.reshape(shp_h), f.reshape(shp_h), hi.reshape(shp_h))
        o_h = _rmsnorm(o_h, hgrn_norm_g[l].reshape(HGRN_HEADS, HGRN_HEAD_DIM)).reshape(B, S, HGRN_WIDTH)
        o_h = o_h * jax.nn.silu(hg)

        mix = jnp.concatenate([o_fox, o_h], axis=-1) @ w_out[l]
        x = x + gate_a * _rmsnorm(mix, post_mix_g[l])

        h2 = _rmsnorm(x, pre_ffn_g[l]) * (1.0 + scale_f) + shift_f
        y = _peer(h2, peer_w_q[l], peer_sub_keys[l], peer_u[l], peer_v[l])
        x = x + gate_f * _rmsnorm(y, post_ffn_g[l])
    return x


_drawn_inputs = setup_inputs


def setup_inputs(seed=0):
    import zlib

    import numpy as np

    out = dict(_drawn_inputs(seed))
    spreads = {}
    factors = {'post_ffn_g': 4.141}
    for name, (base, spread) in spreads.items():
        noise = np.random.default_rng([zlib.crc32(name.encode()), seed]).standard_normal(out[name].shape)
        drawn = base * np.exp(spread * noise) if base else spread * noise
        out[name] = __import__('jax').numpy.asarray(drawn.astype(out[name].dtype))
    for name, factor in factors.items():
        out[name] = (out[name] * factor).astype(out[name].dtype)
    return out
```

```python
from contextlib import ExitStack

import concourse.bass as bass
from concourse import mybir

P = 128
F32 = mybir.dt.float32
F32R = mybir.dt.float32r
I32 = mybir.dt.int32
U32 = mybir.dt.uint32
ALU = mybir.AluOpType
ACT = mybir.ActivationFunctionType
AX = mybir.AxisListType
MASKED = -3.0e38


def hybrid_block(nc, x_in, c_col, w_ada, b_ada_col, gains_col, rows, w_in, hgrn_rows, w_out,
                 w_q, keys_t, u_t, v_in, const_f, const_m, gate_map, out):
    S, D = x_in.shape
    NT = S // P
    KD = D // P
    W = 512
    FH, FD = 8, 64
    HH, HD = 4, 128
    PH, TOPK, NK = 8, 16, 128
    HP = 2 * PH
    SLOTS = PH * TOPK
    LEVELS = 8
    EPS = 1e-6
    GROUP = 4
    NGROUPS = NK // GROUP
    BATCH = 16
    QUAD = 4
    NB = P // BATCH
    QB = BATCH // QUAD
    OHR = 2
    FR = 4

    with ExitStack() as ctx:
        def sem(name):
            return ctx.enter_context(nc.semaphore(name))

        def sb(name, shape, dt=F32, where=ctx):
            return where.enter_context(nc.sbuf_tensor(name, shape, dt))

        bank = [ctx.enter_context(nc.psum_tensor(f"bank{i}", [P, W], F32)) for i in range(8)]

        x = sb("x", [P, NT, D])
        h2T = sb("h2T", [P, KD, S])
        hT = h2T
        gate_f = sb("gate_f", [P, D])
        ident = sb("ident", [P, P])
        iota = sb("iota", [P, P])
        eps = sb("eps", [P, 1])
        stat = sb("stat", [P, 4, NT])
        ones = sb("ones", [P, 1])

        mx = ExitStack()
        wring = sb("wring", [P, 2, KD, W], where=mx)
        cat = sb("cat", [P, NT, D], where=mx)
        fqk = sb("fqk", [P, 2, 4, S], where=mx)
        fqT, fkT = fqk[:, 0], fqk[:, 1]
        mix = fqk[:, :, :, :].rearrange("p a b c -> p (a b c)").rearrange("p (t d) -> p t d", t=NT)
        fv = sb("fv", [P, NT, 512], where=mx)
        hqk = sb("hqk", [P, 2 * HH, S], where=mx)
        hqT, hkT = hqk[:, 0:HH], hqk[:, HH:2 * HH]
        nFb = hqk
        hi = sb("hi", [P, NT, 512], where=mx)
        hg = sb("hg", [P, NT, 512], where=mx)
        logf = sb("logf", [P, NT, 512], where=mx)
        hk = sb("hk", [P, NT, 512], where=mx)
        gate_a = sb("gate_a", [P, D], where=mx)
        post_a = sb("post_a", [P, D], where=mx)
        post_f = sb("post_f", [P, D], where=mx)
        cond = sb("cond", [P, 2, KD], where=mx)
        wff = sb("wff", [P, KD, FH], where=mx)
        bada = sb("bada", [P, 48], where=mx)
        gains = sb("gains", [P, 2, KD], where=mx)
        shift = sb("shift", [P, 2, KD], where=mx)
        scale = sb("scale", [P, 2, KD], where=mx)
        gam = sb("gam", [P, 2, 512], where=mx)
        gmx = sb("gmx", [P, 512], where=mx)
        hng = sb("hng", [P, 512], where=mx)
        modt = sb("modt", [P, 2 * KD], where=mx)
        tri = sb("tri", [P, W + P], where=mx)
        lmask = sb("lmask", [P, LEVELS, P], I32, where=mx)
        ff = sb("ff", [P, 4, NT, FH], where=mx)
        fcol = sb("fcol", [P, NT, FH], where=mx)
        bfox = sb("bfox", [P, FH], where=mx)
        hss = sb("hss", [P, 2, NT, HH], where=mx)
        hx = ExitStack()
        AT = sb("AT", [P, 2, S], where=hx)
        dec = gam
        qe = sb("qe", [P, 2, S], where=hx)
        ke = sb("ke", [P, 2, S], where=hx)
        sc = sb("sc", [P, 2, S], where=hx)
        st = sb("st", [P, 2, 3, HD], where=hx)
        alast = sb("alast", [P, 2, NT], where=hx)
        hsq = gmx
        hx.close()
        fx = ExitStack()
        lg = sb("lg", [P, FR, S], where=fx)
        pr = sb("pr", [P, FR, S], where=fx)
        prT = logf
        rmax = sb("rmax", [P, NT, FH], where=fx)
        rsum = sb("rsum", [P, 2, NT, FH], where=fx)
        fx.close()
        mx.close()

        rt = ExitStack()
        wqring = sb("wqring", [P, 2, KD, W], where=rt)
        qsq = sb("qsq", [P, 2, S], where=rt)
        rt.close()
        stage = sb("stage", [P, NK, P], where=rt)
        qT = sb("qT", [P, HP, S], where=rt)
        keys = sb("keys", [P, HP, NK], where=rt)
        s1 = sb("s1", [P, HP, NK], where=rt)
        s2 = sb("s2", [P, HP, NK], where=rt)
        s3 = sb("s3", [P, HP, NK], where=rt)
        ohA = sb("ohA", [P, OHR * QUAD, NK], where=rt)
        ohB = sb("ohB", [P, OHR * QUAD, NK], where=rt)
        top = sb("top", [P, HP, TOPK], where=rt)
        topi = sb("topi", [P, HP, TOPK], U32, where=rt)
        topf = sb("topf", [P, HP, TOPK], where=rt)
        iota16 = iota[:, 0:TOPK]
        best = sb("best", [P, PH, TOPK], where=rt)
        pos = sb("pos", [P, 3, SLOTS], U32, where=rt)
        posf = sb("posf", [P, 2, SLOTS], where=rt)
        slot = sb("slot", [P, 3, SLOTS], where=rt)
        slotT = sb("slotT", [P, 3, P], where=rt)
        gsum = sb("gsum", [P, 2, PH], where=rt)
        rq = sb("rq", [P, 2, NT, HP], where=rt)
        rt.close()

        ex = ExitStack()
        hhi = sb("hhi", [P, KD, S], F32R, where=ex)
        hlo = sb("hlo", [P, KD, S], F32R, where=ex)
        uraw = sb("uraw", [P, GROUP, KD, P], where=ex)
        uhi = sb("uhi", [P, 2, KD, P], F32R, where=ex)
        ulo = sb("ulo", [P, 2, KD, P], F32R, where=ex)
        vraw = sb("vraw", [P, GROUP, D], where=ex)
        vhi = sb("vhi", [P, GROUP, D], F32R, where=ex)
        vlo = sb("vlo", [P, GROUP, D], F32R, where=ex)
        gmap = sb("gmap", [P, GROUP, S], where=ex)
        gel = sb("gel", [P, 2, S], where=ex)
        av = sb("av", [P, 2, S], where=ex)
        ahi = sb("ahi", [P, GROUP, S], F32R, where=ex)
        alo = sb("alo", [P, GROUP, S], F32R, where=ex)
        ex.close()
        acc = h2T[:, :, :].rearrange("p a b -> p (a b)").rearrange("p (t d) -> p t d", t=NT)
        n_lev = LEVELS - 1
        sqs = cat

        def number(jobs):
            return {job: n for n, job in enumerate(jobs)}

        a_jobs, d_jobs = [], []
        a_jobs += [("f", tt) for tt in range(NT)] + [("hq", h) for h in range(HH)]
        a_jobs += [("hk", h) for h in range(HH)] + [("hi", tt) for tt in range(NT)]
        a_jobs += [("suffix", c) for c in range(NT - 1)]
        for h in range(HH):
            a_jobs += [("A", h), ("side", h, 0), ("side", h, 1)]
            a_jobs += [("o", h - 1)] if h else []
            a_jobs += [("side", h, 2), ("side", h, 3)]
        a_jobs += [("o", HH - 1), ("fcol",)] + [("nF", h) for h in range(FH)]
        a_jobs += [("pT", n) for n in range(NT * FH)] + [("catT", k) for k in range(KD)]
        a_jobs += [("mix", half, tt) for half in range(2) for tt in range(NT)]
        a_jobs += [("q", n) for n in range(HP)]
        d_jobs += [("mod", 0)] + [("xT", k) for k in range(KD)] + [("ff",)]
        for h in range(HH):
            d_jobs += [("kv", h)] + [("level", h, lev) for lev in range(LEVELS)]
        d_jobs += [("gate_a", 0), ("gate_a", 1)] + [("logits", n) for n in range(NT * FH)]
        d_jobs += [("mod", 1), ("gate_f", 0), ("gate_f", 1)] + [("h2T", k) for k in range(KD)]
        a_job, d_job = number(a_jobs), number(d_jobs)
        A_BANKS, D_BANKS, O_BANKS = [0, 1, 2], [3, 4, 5], [6, 7]
        SCORE_BANKS, G_BANKS = [3, 4, 5, 6], [0, 1, 2, 7]
        UP_BANKS, Y_BANKS = [0, 1], [2, 3, 4, 5]

        def a_bank(job):
            return bank[A_BANKS[a_job[job] % 3]]

        def d_bank(job):
            return bank[D_BANKS[d_job[job] % 3]]

        w_loaded = [sem(f"w_loaded{i}") for i in range(2)]
        w_used = sem("w_used")
        small_loaded = sem("small_loaded")
        x_loaded = sem("x_loaded")
        keys_loaded = sem("keys_loaded")
        made = sem("made")
        cond_ready = sem("cond_ready")
        a_full = sem("a_full")
        a_done = sem("a_done")
        d_full = sem("d_full")
        d_done = sem("d_done")
        dve_chain = sem("dve_chain")
        act_chain = sem("act_chain")
        pool_chain = sem("pool_chain")
        sumsq_ready = sem("sumsq_ready")
        root_ready = sem("root_ready")
        xn_ready = sem("xn_ready")
        f_ready = sem("f_ready")
        logf_ready = sem("logf_ready")
        fz_ready = sem("fz_ready")
        fsoft_ready = sem("fsoft_ready")
        lff_ready = sem("lff_ready")
        kd_ready = sem("kd_ready")
        gam_ready = sem("gam_ready")
        game_ready = sem("game_ready")
        sc_zeroed = sem("sc_zeroed")
        diff_ready = sem("diff_ready")
        dec_ready = sem("dec_ready")
        qe_ready = sem("qe_ready")
        ke_ready = sem("ke_ready")
        alast_ready = sem("alast_ready")
        expA_ready = sem("expA_ready")
        qa_ready = sem("qa_ready")
        st_ready = sem("st_ready")
        hsq_ready = sem("hsq_ready")
        hsum_ready = sem("hsum_ready")
        hroot_ready = sem("hroot_ready")
        hcat_ready = sem("hcat_ready")
        mask_ready = sem("mask_ready")
        rmax_ready = sem("rmax_ready")
        pr_ready = sem("pr_ready")
        pv_done = sem("pv_done")
        fcat_ready = sem("fcat_ready")
        xmix_ready = sem("xmix_ready")
        qsq_ready = sem("qsq_ready")
        qss_done = sem("qss_done")
        qroot_ready = sem("qroot_ready")
        s_full = sem("s_full")
        s_done = sem("s_done")
        gmax_ready = sem("gmax_ready")
        gexp_ready = sem("gexp_ready")
        slot_ready = sem("slot_ready")
        slotT_full = sem("slotT_full")
        slotT_done = sem("slotT_done")
        onehot_ready = sem("onehot_ready")
        g_full = sem("g_full")
        g_done = sem("g_done")
        map_stored = sem("map_stored")
        routed = sem("routed")
        hhi_ready = sem("hhi_ready")
        hlo_ready = sem("hlo_ready")
        u_loaded = [sem(f"u_loaded{i}") for i in range(GROUP)]
        v_loaded = [sem(f"v_loaded{i}") for i in range(GROUP)]
        g_loaded = [sem(f"g_loaded{i}") for i in range(GROUP)]
        uhi_ready = sem("uhi_ready")
        ulo_ready = sem("ulo_ready")
        vhi_ready = sem("vhi_ready")
        vlo_ready = sem("vlo_ready")
        up_full = sem("up_full")
        gelu_ready = sem("gelu_ready")
        av_ready = sem("av_ready")
        ahi_ready = sem("ahi_ready")
        alo_ready = sem("alo_ready")
        y_full = sem("y_full")
        y_done = sem("y_done")
        out_ready = sem("out_ready")
        stored = sem("stored")

        FF = 3 * FH * FD
        HQ, HF, HI, HG = [FF + FH + i * 512 for i in range(4)]
        chunks = [(w_ada, n * W) for n in range(4)]
        chunks += [(w_in, n) for n in (HF, HQ, HI, 0, 512, 1024, HG)]
        chunks += [(w_ada, n * W) for n in (4, 5)]
        chunks += [(w_out, 0), (w_out, W)]
        chunks += [(w_ada, n * W) for n in range(6, 12)]
        N_MIX = len(chunks)
        chunks += [(w_q, n * W) for n in range(HP * P // W)]
        loads = [(cond[:, 0], c_col), (bada[:], b_ada_col), (gains[:], gains_col),
                 (gate_a[:], rows[0].partition_broadcast(P)), (gate_f[:], rows[1].partition_broadcast(P)),
                 (post_a[:], rows[2].partition_broadcast(P)), (post_f[:], rows[3].partition_broadcast(P)),
                 (gam[:, 0], hgrn_rows[0].partition_broadcast(P)),
                 (gam[:, 1], hgrn_rows[1].partition_broadcast(P)),
                 (hng[:], hgrn_rows[2].partition_broadcast(P)),
                 (bfox[:], hgrn_rows[3, 0:FH].partition_broadcast(P)),
                 (ident[:], const_f[:, 0:P]), (tri[:], const_f[:, P:2 * P + W]),
                 (iota[:], const_f[:, 2 * P + W:3 * P + W]), (lmask[:], const_m),
                 (wff[:], w_in[:, FF:FF + FH].rearrange("(k p) n -> p k n", p=P))]
        SMALL = 16 * len(loads)
        N_FOX = NT * FH

        block = ctx.enter_context(nc.Block())

        @block.sync
        def _(sp):
            for tt in range(NT):
                sp.dma_start(x[:, tt, :], x_in[tt * P:(tt + 1) * P, :]).then_inc(x_loaded, 16)
            for n, (w, c0) in enumerate(chunks):
                if n >= 2:
                    sp.wait_ge(w_used, n - 1)
                if n == N_MIX:
                    sp.wait_ge(d_done, d_job["h2T", KD - 1] + 1)
                ring = wring if n < N_MIX else wqring
                sp.dma_start(ring[:, n % 2], w[:, c0:c0 + W].rearrange("(k p) n -> p k n", p=P)
                             ).then_inc(w_loaded[n % 2], 16)
                if n == N_MIX:
                    sp.dma_start(keys[:], keys_t).then_inc(keys_loaded, 16)
            for tt in range(NT):
                sp.wait_ge(g_done, (tt + 1) * NB * QB + QB)
                sp.dma_start(gate_map[:, :, tt * P:(tt + 1) * P].rearrange("i j t -> j i t"),
                             stage[:]).then_inc(map_stored, 16)
            sp.wait_ge(routed, 1)
            sp.wait_ge(g_full, NT * NB * QB + OHR)
            sp.wait_ge(map_stored, 16 * NT)
            for k in range(GROUP):
                sp.dma_start(uraw[:, k], u_t[k]).then_inc(u_loaded[k], 16)
                sp.dma_start(vraw[:, k], v_in[k * P:(k + 1) * P, :]).then_inc(v_loaded[k], 16)
                sp.dma_start(gmap[:, k], gate_map[k]).then_inc(g_loaded[k], 16)
            with sp.Fori(1, NGROUPS) as g:
                for k in range(GROUP):
                    sp.wait_ge(ulo_ready, (g - 1) * GROUP + (k + 1))
                    sp.dma_start(uraw[:, k], u_t[bass.ds(g * GROUP + k, 1)].rearrange("a p c e -> p (a c) e")
                                 ).then_inc(u_loaded[k], 16)
                    sp.wait_ge(vlo_ready, (g - 1) * GROUP + (k + 1))
                    sp.dma_start(vraw[:, k], v_in[bass.ds((g * GROUP + k) * P, P), :]
                                 ).then_inc(v_loaded[k], 16)
                    sp.wait_ge(av_ready, (g - 1) * GROUP + (k + 1))
                    sp.dma_start(gmap[:, k], gate_map[bass.ds(g * GROUP + k, 1)].rearrange("a j t -> j (a t)")
                                 ).then_inc(g_loaded[k], 16)
            for tt in range(NT):
                sp.wait_ge(out_ready, tt + 1)
                sp.dma_start(out[tt * P:(tt + 1) * P, :], acc[:, tt, :]).then_inc(stored, 16)
            sp.wait_ge(stored, 16 * NT)

        @block.gpsimd
        def _(pool):
            for dst, src in loads:
                pool.dma_start(dst, src).then_inc(small_loaded, 16)
            pool.wait_ge(a_done, a_job["hk", HH - 1] + 1)
            for h in range(HH):
                for lev in range(1, LEVELS):
                    n = h * n_lev + lev - 1
                    pool.wait_ge(dec_ready, n + 1)
                    if n >= 2:
                        h2, l2 = divmod(n - 2, n_lev)
                        pool.wait_ge(d_full, d_job["level", h2, l2 + 1] + 1)
                    nc.gpsimd.tensor_tensor(ke[:, n % 2], hkT[:, h], dec[:, n % 2], ALU.mult
                                            ).then_inc(ke_ready, 1)
            for n in range(N_FOX):
                tt = n // FH
                pool.wait_ge(d_done, d_job["logits", n] + 1)
                blk = lg[:, n % FR, tt * P:(tt + 1) * P]
                nc.gpsimd.affine_select(out=blk, in_=blk, compare_op=ALU.is_ge, fill=MASKED, base=0,
                                        pattern=[[-1, P]], channel_multiplier=1).then_inc(mask_ready, 1)

        @block.scalar
        def _(act):
            chain = [0]

            def link(ins):
                chain[0] += 1
                ins.then_inc(act_chain, 1)
                act.wait_ge(act_chain, chain[0])

            def move(job, dst, func=ACT.Copy, cols=W, split=None, **kw):
                act.wait_ge(a_full, a_job[job] + 1)
                src = a_bank(job)[:, 0:cols]
                if split:
                    src = src.rearrange("p (c v) -> p c v", c=split)
                nc.scalar.activation(dst, src, func, **kw).then_inc(a_done, 1)

            def roots(n, src, dst):
                for tt in range(NT):
                    nc.scalar.activation(dst[:, tt, :], src[:, tt, :], ACT.Square,
                                         accum_out=stat[:, 0, tt:tt + 1]).then_inc(sumsq_ready, 1)
                act.wait_ge(sumsq_ready, (n + 1) * NT)
                nc.scalar.activation(stat[:, 1, :], stat[:, 0, :], ACT.Sqrt, bias=eps[:], scale=1.0 / D
                                     ).then_inc(root_ready, 1)

            act.wait_ge(small_loaded, SMALL)
            nc.scalar.activation(cond[:, 1], cond[:, 0], ACT.Silu).then_inc(cond_ready, 1)
            act.wait_ge(x_loaded, 16 * NT)
            act.wait_ge(made, 2)
            roots(0, x, sqs)
            act.wait_ge(gam_ready, 1)
            nc.scalar.activation(gam[:], gam[:], ACT.Exp).then_inc(game_ready, 1)
            for tt in range(NT):
                move(("f", tt), logf[:, tt, :], ACT.Sigmoid)
            for h in range(HH):
                move(("hq", h), hqT[:, h], scale=HD ** -0.5)
            act.wait_ge(fz_ready, 1)
            link(nc.scalar.activation(ff[:, 2], ff[:, 1], ACT.Exp, scale=-1.0))
            nc.scalar.activation(ff[:, 3], ff[:, 2], ACT.Ln, bias=ones[:]).then_inc(fsoft_ready, 1)
            act.wait_ge(f_ready, 1)
            nc.scalar.activation(logf[:], logf[:], ACT.Ln).then_inc(logf_ready, 1)
            for h in range(HH):
                move(("hk", h), hkT[:, h])
            for tt in range(NT):
                move(("hi", tt), hi[:, tt, :])
            for c in range(NT - 1):
                move(("suffix", c), cat[:, c, 0:512], ACT.Exp)

            def output_of(h):
                o_h = cat[:, :, 512 + h * HD:512 + (h + 1) * HD]
                move(("o", h), o_h, split=NT)
                act.wait_ge(a_done, a_job["o", h] + 1)
                if h:
                    act.wait_ge(hsum_ready, h)
                nc.scalar.activation(hsq[:].rearrange("p (c v) -> p c v", c=NT), o_h, ACT.Square
                                     ).then_inc(hsq_ready, 1)

            sides = [(fqT, ACT.Copy, FD ** -0.5), (fkT, ACT.Copy, 1.0), (fv, ACT.Copy, 1.0), (hg, ACT.Silu, 1.0)]
            for h in range(HH):
                if h:
                    act.wait_ge(diff_ready, h * n_lev)
                    act.wait_ge(expA_ready, h)
                move(("A", h), AT[:, 0])
                act.wait_ge(a_done, a_job["A", h] + 1)
                if h >= 2:
                    act.wait_ge(st_ready, h - 1)
                nc.scalar.activation(alast[:, h % 2], AT[:, 0].rearrange("p (c t) -> p c t", c=NT)[:, :, P - 1],
                                     ACT.Exp).then_inc(alast_ready, 1)
                dst, func, mul = sides[h]
                for j in range(NT):
                    move(("side", h, j), dst[:, j], func, scale=mul)
                    for lev in (2 * j + 1, 2 * j + 2):
                        if lev < LEVELS:
                            n = h * n_lev + lev - 1
                            act.wait_ge(diff_ready, n + 1)
                            link(nc.scalar.activation(dec[:, n % 2], dec[:, n % 2], ACT.Abs))
                            nc.scalar.activation(dec[:, n % 2], dec[:, n % 2], ACT.Exp, scale=-1.0
                                                 ).then_inc(dec_ready, 1)
                    if j == 1 and h:
                        output_of(h - 1)
                nc.scalar.activation(AT[:, 1], AT[:, 0], ACT.Exp).then_inc(expA_ready, 1)
            output_of(HH - 1)
            act.wait_ge(hsum_ready, HH)
            nc.scalar.activation(hss[:, 1], hss[:, 0], ACT.Sqrt, bias=eps[:], scale=1.0 / HD
                                 ).then_inc(hroot_ready, 1)
            move(("fcol",), fcol[:].rearrange("p t h -> p (t h)"), cols=NT * FH)
            act.wait_ge(hcat_ready, 1)
            for h in range(FH):
                move(("nF", h), nFb[:, h], scale=-1.0)
            for n in range(N_FOX):
                tt, h = divmod(n, FH)
                w = (tt + 1) * P
                act.wait_ge(rmax_ready, n + 1)
                nc.scalar.activation(pr[:, n % FR, 0:w], lg[:, n % FR, 0:w], ACT.Exp, bias=rmax[:, tt, h:h + 1],
                                     accum_out=rsum[:, 0, tt, h:h + 1]).then_inc(pr_ready, 1)
                if n >= FR:
                    act.wait_ge(pv_done, n - FR + 1)
                move(("pT", n), prT[:, n % FR, 0:w], cols=w)
            for k in range(KD):
                move(("catT", k), hT[:, k])
            for half in range(2):
                for tt in range(NT):
                    move(("mix", half, tt), mix[:, tt, half * W:(half + 1) * W])
            act.wait_ge(a_done, a_job["mix", 1, NT - 1] + 1)
            roots(1, mix, cat)
            act.wait_ge(xmix_ready, 1)
            roots(2, x, mix)
            act.wait_ge(d_done, d_job["h2T", KD - 1] + 1)
            for n in range(HP):
                move(("q", n), qT[:, n])
                act.wait_ge(a_done, a_job["q", n] + 1)
                if n >= 2:
                    act.wait_ge(qss_done, n - 1)
                nc.scalar.activation(qsq[:, n % 2], qT[:, n], ACT.Square).then_inc(qsq_ready, 1)
            act.wait_ge(qss_done, HP)
            nc.scalar.activation(rq[:, 0], bank[6][:, 0:NT * HP].rearrange("p (t n) -> p t n", t=NT), ACT.Sqrt,
                                 bias=eps[:], scale=1.0 / P).then_inc(qroot_ready, 1)
            act.sem_inc(g_done, QB)
            for tt in range(NT):
                act.wait_ge(gmax_ready, tt + 1)
                nc.scalar.activation(best[:], best[:], ACT.Exp).then_inc(gexp_ready, 1)
                if tt:
                    act.wait_ge(map_stored, 16 * tt)
                with act.Fori(0, NB) as bt:
                    for qd in range(QB):
                        act.wait_ge(g_full, bt * QB + (tt * NB * QB + qd + 1 + OHR))
                        dst = stage[:, :, bass.ds(bt * BATCH + qd * QUAD, QUAD)].rearrange("p i t -> p t i")
                        nc.scalar.activation(dst, bank[G_BANKS[qd]][:].rearrange("p (t i) -> p t i", t=QUAD),
                                             ACT.Copy).then_inc(g_done, 1)
            act.wait_ge(map_stored, 16 * NT)
            act.wait_ge(routed, 1)
            nc.scalar.activation(hhi[:], h2T[:], ACT.Copy).then_inc(hhi_ready, 1)

            def split_u(g, k):
                act.wait_ge(u_loaded[k], g * 16 + 16)
                if k >= 2:
                    act.wait_ge(up_full, g * GROUP + (k - 1))
                nc.scalar.activation(uhi[:, k % 2], uraw[:, k], ACT.Copy).then_inc(uhi_ready, 1)

            def split_v(g, k):
                act.wait_ge(v_loaded[k], g * 16 + 16)
                nc.scalar.activation(vhi[:, k], vraw[:, k], ACT.Copy).then_inc(vhi_ready, 1)

            def gelu(g, k):
                act.wait_ge(up_full, g * GROUP + (k + 1))
                nc.scalar.activation(gel[:, k % 2], bank[UP_BANKS[k % 2]][:], ACT.Gelu).then_inc(gelu_ready, 1)

            def split_a(g, k):
                act.wait_ge(av_ready, g * GROUP + (k + 1))
                nc.scalar.activation(ahi[:, k], av[:, k % 2], ACT.Copy).then_inc(ahi_ready, 1)

            with act.Fori(0, NGROUPS) as g:
                split_u(g, 0)
                split_u(g, 1)
                act.wait_ge(y_full, g * 8 + 1)
                split_v(g, 0)
                split_v(g, 1)
                for k in range(GROUP):
                    gelu(g, k)
                    if k + 2 < GROUP:
                        split_u(g, k + 2)
                    split_a(g, k)
                    if k + 2 < GROUP:
                        split_v(g, k + 2)
            act.wait_ge(y_done, 8 * NGROUPS + len(Y_BANKS))
            roots(3, acc, vraw)

        @block.vector
        def _(dve):
            chain = [0]

            def link(ins):
                chain[0] += 1
                ins.then_inc(dve_chain, 1)
                dve.wait_ge(dve_chain, chain[0])

            def full(job):
                dve.wait_ge(d_full, d_job[job] + 1)
                return d_bank(job)

            def mod_columns(i):
                b = full(("mod", i))
                link(nc.vector.tensor_tensor(modt[:], b[:, 0:2 * KD], bada[:, 24 * i:24 * i + 2 * KD], ALU.add))
                nc.vector.scalar_tensor_tensor(scale[:, i], modt[:, KD:2 * KD], 1.0, gains[:, i], ALU.add, ALU.mult)
                link(nc.vector.tensor_copy(shift[:, i], modt[:, 0:KD]))
                dve.sem_inc(d_done, 1)

            def gate_rows(name, gate, post):
                for half in range(2):
                    b = full((name, half))
                    cols = slice(half * W, (half + 1) * W)
                    link(nc.vector.tensor_tensor(gate[:, cols], gate[:, cols], b[:], ALU.add))
                    nc.vector.tensor_tensor(gate[:, cols], gate[:, cols], post[:, cols], ALU.mult
                                            ).then_inc(d_done, 1)

            def transposed(name, dst, i):
                for k in range(KD):
                    b = full((name, k))
                    nc.vector.tensor_scalar(dst[:, k], b[:], scale[:, i, k:k + 1], shift[:, i, k:k + 1],
                                            ALU.mult, ALU.add).then_inc(d_done, 1)

            nc.vector.memset(eps[:], EPS).then_inc(made, 1)
            nc.vector.memset(ones[:], 1.0).then_inc(made, 1)
            dve.wait_ge(small_loaded, SMALL)
            link(nc.vector.tensor_tensor(gmx[:], gam[:, 0], gam[:, 1], ALU.max))
            nc.vector.tensor_tensor(gam[:, 0], gam[:, 0], gmx[:], ALU.subtract)
            nc.vector.tensor_tensor(gam[:, 1], gam[:, 1], gmx[:], ALU.subtract).then_inc(gam_ready, 1)
            dve.wait_ge(game_ready, 1)
            link(nc.vector.tensor_tensor(gmx[:], gam[:, 0], gam[:, 1], ALU.add))
            link(nc.vector.reciprocal(gmx[:], gmx[:]))
            link(nc.vector.tensor_tensor(gam[:, 0], gam[:, 0], gmx[:], ALU.mult))
            link(nc.vector.tensor_scalar(gam[:, 1], gam[:, 0], -1.0, 1.0, ALU.mult, ALU.add))
            dve.wait_ge(root_ready, 1)
            link(nc.vector.reciprocal(stat[:, 2], stat[:, 1]))
            for tt in range(NT):
                nc.vector.tensor_scalar(cat[:, tt], x[:, tt], stat[:, 2, tt:tt + 1], None, ALU.mult
                                        ).then_inc(xn_ready, 1)
            mod_columns(0)
            transposed("xT", hT, 0)
            for tt in range(NT):
                dve.wait_ge(a_done, a_job["f", tt] + 1)
                link(nc.vector.tensor_tensor(logf[:, tt], logf[:, tt], gam[:, 1], ALU.mult))
                link(nc.vector.tensor_tensor(logf[:, tt], logf[:, tt], gam[:, 0], ALU.add))
                ins = nc.vector.tensor_scalar(hk[:, tt], logf[:, tt], -1.0, 1.0, ALU.mult, ALU.add)
            ins.then_inc(f_ready, 1)
            b = full(("ff",))
            link(nc.vector.tensor_tensor(ff[:, 0], b[:, 0:NT * FH].rearrange("p (t h) -> p t h", t=NT),
                                         bfox[:].unsqueeze(1).to_broadcast([P, NT, FH]), ALU.add))
            dve.sem_inc(d_done, 1)
            nc.vector.scalar_tensor_tensor(ff[:, 1], ff[:, 0], -1.0, ff[:, 0], ALU.mult, ALU.max).then_inc(fz_ready, 1)
            dve.wait_ge(fsoft_ready, 1)
            nc.vector.scalar_tensor_tensor(ff[:, 0], ff[:, 0], 0.0, ff[:, 3], ALU.min, ALU.subtract
                                           ).then_inc(lff_ready, 1)
            dve.wait_ge(a_done, a_job["hk", HH - 1] + 1)
            for c in range(NT - 1):
                dve.wait_ge(a_done, a_job["suffix", c] + 1)
                nc.vector.tensor_tensor(hk[:, c], hk[:, c], cat[:, c, 0:512], ALU.mult).then_inc(kd_ready, 1)

            def difference(h, lev):
                n = h * n_lev + lev - 1
                half = 1 << (lev - 1)
                a = AT[:, 0].rearrange("p (g u) -> p g u", u=2 * half)
                mid = a[:, :, half - 1:half].to_broadcast([P, S // (2 * half), 2 * half])
                if n >= 2:
                    dve.wait_ge(ke_ready, n - 1)
                nc.vector.tensor_tensor(dec[:, n % 2].rearrange("p (g u) -> p g u", u=2 * half), a, mid,
                                        ALU.subtract).then_inc(diff_ready, 1)

            def keep(h, lev):
                b = full(("level", h, lev))
                nc.vector.copy_predicated(sc[:, h % 2].rearrange("p (c t) -> p c t", c=NT),
                                          lmask[:, lev].unsqueeze(1).to_broadcast([P, NT, P]),
                                          b[:].rearrange("p (c t) -> p c t", c=NT)).then_inc(d_done, 1)

            def sum_squares(h):
                dve.wait_ge(hsq_ready, h + 1)
                nc.vector.tensor_reduce(hss[:, 0, :, h:h + 1].rearrange("p c o -> p (c o)"),
                                        hsq[:].rearrange("p (c v) -> p c v", c=NT), AX.X, ALU.add
                                        ).then_inc(hsum_ready, 1)

            for h in range(HH):
                dve.wait_ge(a_done, a_job["A", h] + 1)
                difference(h, 1)
                difference(h, 2)
                b = full(("kv", h))
                dve.wait_ge(alast_ready, h + 1)
                if h >= 2:
                    dve.wait_ge(a_full, a_job["o", h - 2] + 1)
                link(nc.vector.memset(sc[:, h % 2], 0.0))
                link(nc.vector.tensor_copy(st[:, h % 2, 0], b[:, 0:HD]))
                link(nc.vector.scalar_tensor_tensor(st[:, h % 2, 1], st[:, h % 2, 0], alast[:, h % 2, 1:2],
                                                    b[:, HD:2 * HD], ALU.mult, ALU.add))
                link(nc.vector.scalar_tensor_tensor(st[:, h % 2, 2], st[:, h % 2, 1], alast[:, h % 2, 2:3],
                                                    b[:, 2 * HD:3 * HD], ALU.mult, ALU.add))
                dve.sem_inc(d_done, 1)
                dve.sem_inc(st_ready, 1)
                keep(h, 0)
                for lev in range(1, LEVELS):
                    n = h * n_lev + lev - 1
                    dve.wait_ge(dec_ready, n + 1)
                    nc.vector.tensor_tensor(qe[:, n % 2], hqT[:, h], dec[:, n % 2], ALU.mult).then_inc(qe_ready, 1)
                    if lev + 2 < LEVELS:
                        dve.wait_ge(qe_ready, n + 1)
                        difference(h, lev + 2)
                    dve.wait_ge(d_done, d_job["level", h, lev - 1] + 1)
                    keep(h, lev)
                dve.wait_ge(expA_ready, h + 1)
                nc.vector.tensor_tensor(AT[:, 1], AT[:, 1], hqT[:, h], ALU.mult).then_inc(qa_ready, 1)
                if h:
                    sum_squares(h - 1)
            sum_squares(HH - 1)
            dve.wait_ge(hroot_ready, 1)
            link(nc.vector.reciprocal(hss[:, 0], hss[:, 1]))
            for c in range(NT):
                o_c = cat[:, c, 512:1024].rearrange("p (h v) -> p h v", h=HH)
                nc.vector.tensor_tensor(o_c, o_c, hss[:, 0, c].unsqueeze(2).to_broadcast([P, HH, HD]), ALU.mult)
                ins = nc.vector.tensor_tensor(hg[:, c], hg[:, c], hng[:], ALU.mult)
            link(ins)
            ins = nc.vector.tensor_tensor(cat[:, :, 512:1024], cat[:, :, 512:1024], hg[:], ALU.mult)
            ins.then_inc(hcat_ready, 1)
            gate_rows("gate_a", gate_a, post_a)

            def logits(n):
                tt, h = divmod(n, FH)
                w = (tt + 1) * P
                b = full(("logits", n))
                if n >= FR:
                    dve.wait_ge(pr_ready, n - FR + 1)
                nc.vector.scalar_tensor_tensor(lg[:, n % FR, 0:w], nFb[:, h, 0:w], fcol[:, tt, h:h + 1], b[:, 0:w],
                                               ALU.add, ALU.add).then_inc(d_done, 1)

            def fox_out(tt):
                dve.wait_ge(pv_done, (tt + 1) * FH)
                link(nc.vector.reciprocal(rsum[:, 1, tt], rsum[:, 0, tt]))
                nc.vector.tensor_tensor(cat[:, tt, 0:512].rearrange("p (h d) -> p h d", h=FH),
                                        bank[O_BANKS[tt % 2]][:].rearrange("p (h d) -> p h d", h=FH),
                                        rsum[:, 1, tt].unsqueeze(2).to_broadcast([P, FH, FD]), ALU.mult
                                        ).then_inc(fcat_ready, 1)

            dve.wait_ge(a_done, a_job["nF", FH - 1] + 1)
            logits(0)
            logits(1)
            for n in range(N_FOX):
                tt, h = divmod(n, FH)
                if n + 2 < N_FOX:
                    logits(n + 2)
                dve.wait_ge(mask_ready, n + 1)
                link(nc.vector.tensor_reduce(rmax[:, tt, h:h + 1], lg[:, n % FR, 0:(tt + 1) * P], AX.X, ALU.max))
                nc.vector.tensor_scalar(rmax[:, tt, h:h + 1], rmax[:, tt, h:h + 1], -1.0, None, ALU.mult
                                        ).then_inc(rmax_ready, 1)
                if tt and h == 3:
                    fox_out(tt - 1)
            fox_out(NT - 1)
            dve.wait_ge(root_ready, 2)
            link(nc.vector.reciprocal(stat[:, 2], stat[:, 1]))
            for tt in range(NT):
                ins = nc.vector.scalar_tensor_tensor(mix[:, tt], mix[:, tt], stat[:, 2, tt:tt + 1], gate_a[:],
                                                     ALU.mult, ALU.mult)
            link(ins)
            nc.vector.tensor_tensor(x[:], x[:], mix, ALU.add).then_inc(xmix_ready, 1)
            mod_columns(1)
            gate_rows("gate_f", gate_f, post_f)
            dve.wait_ge(root_ready, 3)
            link(nc.vector.reciprocal(stat[:, 2], stat[:, 1]))
            for tt in range(NT):
                nc.vector.tensor_scalar(cat[:, tt], x[:, tt], stat[:, 2, tt:tt + 1], None, ALU.mult
                                        ).then_inc(xn_ready, 1)
            transposed("h2T", h2T, 1)

            dve.wait_ge(qroot_ready, 1)
            link(nc.vector.reciprocal(rq[:, 1], rq[:, 0]))
            pairs = [s1, s2, s3]
            c1, c2, c3 = [s[:].rearrange("p n k -> p (n k)").rearrange("p (h a b) -> p h a b", h=PH, a=TOPK)
                          for s in pairs]
            f1, f3 = [s[:].rearrange("p n k -> p (n k)").rearrange("p (h c) -> p h c", h=PH) for s in (s1, s3)]
            halves = top[:].rearrange("p (h two) k -> p h two k", two=2)
            halvesf = topf[:].rearrange("p (h two) k -> p h two k", two=2)
            posk = pos[:, 0].rearrange("p (h k) -> p h k", h=PH)
            for tt in range(NT):
                for q4 in range(HP // 4):
                    dve.wait_ge(s_full, tt * (HP // 4) + (q4 + 1))
                    ns = slice(4 * q4, 4 * q4 + 4)
                    r4 = rq[:, 1, tt, ns]
                    nc.vector.tensor_tensor(s1[:, ns], bank[SCORE_BANKS[q4]][:].rearrange("p (n k) -> p n k", n=4),
                                            r4.unsqueeze(2).to_broadcast([P, 4, NK]), ALU.mult).then_inc(s_done, 1)
                dve.wait_ge(s_done, tt * (HP // 4) + HP // 4)
                for n in range(HP):
                    ins = nc.vector.max(top[:, n, 0:8], s1[:, n])
                link(ins)
                for n in range(HP):
                    nc.vector.max_index(topi[:, n, 0:8], top[:, n, 0:8], s1[:, n])
                    ins = nc.vector.match_replace(s2[:, n], top[:, n, 0:8], s1[:, n], MASKED)
                link(ins)
                for n in range(HP):
                    ins = nc.vector.max(top[:, n, 8:16], s2[:, n])
                link(ins)
                for n in range(HP):
                    ins = nc.vector.max_index(topi[:, n, 8:16], top[:, n, 8:16], s2[:, n])
                link(ins)
                nc.vector.tensor_copy(topf[:], topi[:])
                link(nc.vector.tensor_tensor(c3, halves[:, :, 0].unsqueeze(3).to_broadcast([P, PH, TOPK, TOPK]),
                                            halves[:, :, 1].unsqueeze(2).to_broadcast([P, PH, TOPK, TOPK]), ALU.add))
                for h in range(PH):
                    ins = nc.vector.max(best[:, h, 0:8], f3[:, h])
                link(ins)
                for h in range(PH):
                    nc.vector.max_index(posk[:, h, 0:8], best[:, h, 0:8], f3[:, h])
                    ins = nc.vector.match_replace(f1[:, h], best[:, h, 0:8], f3[:, h], MASKED)
                link(ins)
                for h in range(PH):
                    ins = nc.vector.max(best[:, h, 8:16], f1[:, h])
                link(ins)
                for h in range(PH):
                    nc.vector.max_index(posk[:, h, 8:16], best[:, h, 8:16], f1[:, h])
                link(nc.vector.tensor_copy(gsum[:, 0], best[:, :, 0]))
                nc.vector.tensor_tensor(best[:], best[:], gsum[:, 0].unsqueeze(2).to_broadcast([P, PH, TOPK]),
                                        ALU.subtract).then_inc(gmax_ready, 1)
                nc.vector.tensor_scalar(pos[:, 1], pos[:, 0], 4, None, ALU.logical_shift_right)
                link(nc.vector.tensor_scalar(pos[:, 2], pos[:, 0], TOPK - 1, None, ALU.bitwise_and))
                link(nc.vector.tensor_copy(posf[:], pos[:, 1:3]))
                for p, cp in ((0, c1), (1, c2)):
                    ins = nc.vector.tensor_tensor(
                        cp.rearrange("p h a b -> p (h a) b"), posf[:, p].unsqueeze(2).to_broadcast([P, SLOTS, TOPK]),
                        iota16.unsqueeze(1).to_broadcast([P, SLOTS, TOPK]), ALU.is_equal)
                link(ins)
                for p, cp in ((0, c1), (1, c2)):
                    ins = nc.vector.tensor_tensor(cp, cp, halvesf[:, :, p].unsqueeze(2).to_broadcast(
                        [P, PH, TOPK, TOPK]), ALU.mult)
                link(ins)
                for p, cp in ((0, c1), (1, c2)):
                    nc.vector.tensor_reduce(slot[:, p], cp.rearrange("p h a b -> p (h a) b"), AX.X, ALU.add)
                dve.wait_ge(gexp_ready, tt + 1)
                link(nc.vector.tensor_reduce(gsum[:, 0], best[:], AX.X, ALU.add))
                link(nc.vector.reciprocal(gsum[:, 1], gsum[:, 0]))
                nc.vector.tensor_tensor(slot[:, 2].rearrange("p (h k) -> p h k", h=PH), best[:],
                                        gsum[:, 1].unsqueeze(2).to_broadcast([P, PH, TOPK]), ALU.mult
                                        ).then_inc(slot_ready, 1)
                dve.wait_ge(slotT_full, tt + 1)
                nc.vector.tensor_copy(slotT[:].rearrange("p a t -> p (a t)"), bank[SCORE_BANKS[0]][:, 0:3 * P]
                                      ).then_inc(slotT_done, 1)
                dve.wait_ge(slotT_done, tt + 1)
                with dve.Fori(0, NB) as bt:
                    for qd in range(QB):
                        dve.wait_ge(g_full, tt * (NB * QB) + bt * QB + (qd + 1))
                        for j in range(QUAD):
                            o = (qd % OHR) * QUAD + j
                            t = bass.ds(bt * BATCH + (qd * QUAD + j), 1)
                            nc.vector.tensor_scalar(ohB[:, o], iota[:], slotT[:, 1, t], None, ALU.is_equal)
                            ins = nc.vector.tensor_scalar(ohA[:, o], iota[:], slotT[:, 0, t], slotT[:, 2, t],
                                                          ALU.is_equal, ALU.mult)
                        ins.then_inc(onehot_ready, 1)
            dve.sem_inc(routed, 1)

            dve.wait_ge(hhi_ready, 1)
            nc.vector.tensor_tensor(hlo[:], h2T[:], hhi[:].bitcast(F32), ALU.subtract).then_inc(hlo_ready, 1)
            dve.wait_ge(hlo_ready, 1)
            link(nc.vector.memset(h2T[:], 0.0))
            dve.sem_inc(y_done, len(Y_BANKS))

            def split_u(g, k):
                dve.wait_ge(uhi_ready, g * GROUP + (k + 1))
                nc.vector.tensor_tensor(ulo[:, k % 2], uraw[:, k], uhi[:, k % 2].bitcast(F32), ALU.subtract
                                        ).then_inc(ulo_ready, 1)

            def split_v(g, k):
                dve.wait_ge(vhi_ready, g * GROUP + (k + 1))
                nc.vector.tensor_tensor(vlo[:, k], vraw[:, k], vhi[:, k].bitcast(F32), ALU.subtract
                                        ).then_inc(vlo_ready, 1)

            def weigh(g, k):
                dve.wait_ge(gelu_ready, g * GROUP + (k + 1))
                dve.wait_ge(g_loaded[k], g * 16 + 16)
                nc.vector.tensor_tensor(av[:, k % 2], gel[:, k % 2], gmap[:, k], ALU.mult).then_inc(av_ready, 1)

            def split_a(g, k):
                dve.wait_ge(ahi_ready, g * GROUP + (k + 1))
                nc.vector.tensor_tensor(alo[:, k], av[:, k % 2], ahi[:, k].bitcast(F32), ALU.subtract
                                        ).then_inc(alo_ready, 1)

            def add_y(g, blk):
                dve.wait_ge(y_full, g * 8 + (blk + 2))
                a = acc[:, blk // 2, (blk % 2) * W:(blk % 2 + 1) * W]
                nc.vector.tensor_tensor(a, a, bank[Y_BANKS[blk % 4]][:], ALU.add).then_inc(y_done, 1)

            def experts(g, first):
                split_u(g, 0)
                split_u(g, 1)
                if not first:
                    for blk in range(4, 8):
                        add_y(g - 1, blk)
                split_v(g, 0)
                split_v(g, 1)
                for k in range(GROUP):
                    weigh(g, k)
                    if k + 2 < GROUP:
                        split_u(g, k + 2)
                    split_a(g, k)
                    if k + 2 < GROUP:
                        split_v(g, k + 2)
                for blk in range(4):
                    add_y(g, blk)

            experts(0, True)
            with dve.Fori(1, NGROUPS) as g:
                experts(g, False)
            for blk in range(4, 8):
                add_y(NGROUPS - 1, blk)
            dve.wait_ge(root_ready, 4)
            link(nc.vector.reciprocal(stat[:, 2], stat[:, 1]))
            for tt in range(NT):
                ins = nc.vector.scalar_tensor_tensor(acc[:, tt], acc[:, tt], stat[:, 2, tt:tt + 1], gate_f[:],
                                                     ALU.mult, ALU.mult)
            link(ins)
            for tt in range(NT):
                nc.vector.tensor_tensor(acc[:, tt], acc[:, tt], x[:, tt], ALU.add).then_inc(out_ready, 1)

        @block.tensor
        def _(pe):
            mm = nc.tensor.matmul

            def a_open(job):
                if a_job[job] >= 3:
                    pe.wait_ge(a_done, a_job[job] - 2)
                return a_bank(job)

            def d_open(job):
                if d_job[job] >= 3:
                    pe.wait_ge(d_done, d_job[job] - 2)
                return d_bank(job)

            chunk = [0]

            def weights():
                n = chunk[0]
                pe.wait_ge(w_loaded[n % 2], 16 * (n // 2 + 1))
                return (wring if n < N_MIX else wqring)[:, n % 2]

            def used(ins):
                ins.then_inc(w_used, 1)
                chunk[0] += 1

            def by_feature(w, b, m, src):
                for k in range(KD):
                    ins = mm(b[:], w[:, k, m * P:(m + 1) * P], src[:, k], start=k == 0, stop=k == KD - 1)
                return ins

            def by_token(w, b, tt, src):
                for k in range(KD):
                    ins = mm(b[:], src[:, k, tt * P:(tt + 1) * P], w[:, k], start=k == 0, stop=k == KD - 1)
                return ins

            def mod_columns(i):
                b = d_open(("mod", i))
                for ch in range(4):
                    w = weights()
                    for m in range(4):
                        for k in range(KD):
                            ins = mm(b[:, 4 * ch + m:4 * ch + m + 1], w[:, k, m * P:(m + 1) * P],
                                     cond[:, 1, k:k + 1], start=k == 0, stop=k == KD - 1)
                    if ch == 3:
                        ins.then_inc(d_full, 1)
                        pe.wait_ge(d_full, d_job["mod", i] + 1)
                        pe.sem_inc(w_used, 1)
                        chunk[0] += 1
                    else:
                        used(ins)

            def gate_rows(name):
                for half in range(2):
                    b = d_open((name, half))
                    w = weights()
                    for k in range(KD):
                        ins = mm(b[:], cond[:, 1, k:k + 1].to_broadcast([P, P]), w[:, k], start=k == 0, stop=k == KD - 1)
                    finish(ins, d_full, d_job[name, half] + 1)

            def finish(ins, full, n):
                ins.then_inc(full, 1)
                pe.wait_ge(full, n)
                pe.sem_inc(w_used, 1)
                chunk[0] += 1

            def transposes(b, src, n):
                for i in range(n):
                    ins = nc.tensor.transpose(b[:, i * P:(i + 1) * P], src(i), ident[:])
                return ins

            pe.wait_ge(small_loaded, SMALL)
            pe.wait_ge(cond_ready, 1)
            mod_columns(0)
            pe.wait_ge(xn_ready, NT)
            for k in range(KD):
                transposes(d_open(("xT", k)), lambda tt: cat[:, tt, k * P:(k + 1) * P], NT).then_inc(d_full, 1)
            pe.wait_ge(d_done, d_job["xT", KD - 1] + 1)
            w = weights()
            for tt in range(NT):
                ins = by_token(w, a_open(("f", tt)), tt, hT)
                if tt < NT - 1:
                    ins.then_inc(a_full, 1)
            finish(ins, a_full, a_job["f", NT - 1] + 1)
            w = weights()
            for h in range(HH):
                ins = by_feature(w, a_open(("hq", h)), h, hT)
                if h < HH - 1:
                    ins.then_inc(a_full, 1)
            finish(ins, a_full, a_job["hq", HH - 1] + 1)
            b = d_open(("ff",))
            for tt in range(NT):
                for k in range(KD):
                    ins = mm(b[:, tt * FH:(tt + 1) * FH], hT[:, k, tt * P:(tt + 1) * P], wff[:, k],
                             start=k == 0, stop=k == KD - 1)
            ins.then_inc(d_full, 1)
            pe.wait_ge(f_ready, 1)
            for h in range(HH):
                transposes(a_open(("hk", h)), lambda c: hk[:, c, h * HD:(h + 1) * HD], NT).then_inc(a_full, 1)
            w = weights()
            for tt in range(NT):
                ins = by_token(w, a_open(("hi", tt)), tt, hT)
                if tt < NT - 1:
                    ins.then_inc(a_full, 1)
            finish(ins, a_full, a_job["hi", NT - 1] + 1)
            pe.wait_ge(logf_ready, 1)
            for c in range(NT - 1):
                mm(a_open(("suffix", c))[:], tri[:, W:W + P], logf[:, c], start=True, stop=True).then_inc(a_full, 1)

            def output_of(h):
                b = a_open(("o", h))
                pe.wait_ge(d_done, d_job["level", h, LEVELS - 1] + 1)
                pe.wait_ge(st_ready, h + 1)
                pe.wait_ge(qa_ready, h + 1)
                for c in range(NT):
                    cs = slice(c * P, (c + 1) * P)
                    ins = mm(b[:, cs], sc[:, h % 2, cs], hi[:, c, h * HD:(h + 1) * HD], start=True, stop=c == 0)
                    if c:
                        ins = mm(b[:, cs], AT[:, 1, cs], st[:, h % 2, c - 1], start=False, stop=True)
                ins.then_inc(a_full, 1)

            for h in range(HH):
                hs = slice(h * HD, (h + 1) * HD)
                b = a_open(("A", h))
                for c in range(NT):
                    ins = mm(b[:, c * P:(c + 1) * P], logf[:, c, hs], tri[:, 0:P], start=True, stop=True)
                ins.then_inc(a_full, 1)
                b = d_open(("kv", h))
                pe.wait_ge(kd_ready, NT - 1)
                pe.wait_ge(a_done, a_job["hi", NT - 1] + 1)
                for c in range(NT - 1):
                    ins = mm(b[:, c * HD:(c + 1) * HD], hk[:, c, hs], hi[:, c, hs], start=True, stop=True)
                ins.then_inc(d_full, 1)
                w = weights()
                for j in range(NT):
                    b = a_open(("side", h, j))
                    ins = by_feature(w, b, j, hT) if h < 2 else by_token(w, b, j, hT)
                    if j < NT - 1:
                        ins.then_inc(a_full, 1)
                    else:
                        finish(ins, a_full, a_job["side", h, j] + 1)
                    if j == 1 and h:
                        output_of(h - 1)
                    for lev in (2 * j, 2 * j + 1):
                        b = d_open(("level", h, lev))
                        n = h * n_lev + lev - 1
                        if lev:
                            pe.wait_ge(qe_ready, n + 1)
                            pe.wait_ge(ke_ready, n + 1)
                        for c in range(NT):
                            cs = slice(c * P, (c + 1) * P)
                            ins = mm(b[:, cs], ke[:, n % 2, cs] if lev else hkT[:, h, cs],
                                     qe[:, n % 2, cs] if lev else hqT[:, h, cs], start=True, stop=True)
                        ins.then_inc(d_full, 1)
            output_of(HH - 1)
            gate_rows("gate_a")
            pe.wait_ge(lff_ready, 1)
            b = a_open(("fcol",))
            for tt in range(NT):
                for c in range(tt + 1):
                    ins = mm(b[:, tt * FH:(tt + 1) * FH], tri[:, 0:P] if c == tt else tri[:, P:2 * P], ff[:, 0, c],
                             start=c == 0, stop=c == tt)
            ins.then_inc(a_full, 1)
            for h in range(FH):
                b = a_open(("nF", h))
                for c in range(NT):
                    ins = mm(b[:, c * P:W], ff[:, 0, c, h:h + 1].to_broadcast([P, P]), tri[:, 0:W - c * P],
                             start=c == 0, stop=c == NT - 1)
                ins.then_inc(a_full, 1)

            def logits(n):
                tt, h = divmod(n, FH)
                ps = slice(FD * (h % 2), FD * (h % 2) + FD)
                mm(d_open(("logits", n))[:, 0:(tt + 1) * P], fqT[ps, h // 2, tt * P:(tt + 1) * P],
                   fkT[ps, h // 2, 0:(tt + 1) * P], start=True, stop=True).then_inc(d_full, 1)

            def values(n):
                tt, h = divmod(n, FH)
                pe.wait_ge(a_done, a_job["pT", n] + 1)
                if tt >= 2 and h == 0:
                    pe.wait_ge(fcat_ready, tt - 1)
                o = bank[O_BANKS[tt % 2]]
                for c in range(tt + 1):
                    ins = mm(o[:, h * FD:(h + 1) * FD], prT[:, n % FR, c * P:(c + 1) * P],
                             fv[:, c, h * FD:(h + 1) * FD], start=c == 0, stop=c == tt)
                ins.then_inc(pv_done, 1)

            for n in range(3):
                logits(n)
            for n in range(N_FOX):
                pe.wait_ge(pr_ready, n + 1)
                transposes(a_open(("pT", n)), lambda c: pr[:, n % FR, c * P:(c + 1) * P], n // FH + 1
                           ).then_inc(a_full, 1)
                if n + 3 < N_FOX:
                    logits(n + 3)
                if n:
                    values(n - 1)
            values(N_FOX - 1)
            pe.wait_ge(fcat_ready, NT)
            pe.wait_ge(hcat_ready, 1)
            for k in range(KD):
                transposes(a_open(("catT", k)), lambda tt: cat[:, tt, k * P:(k + 1) * P], NT).then_inc(a_full, 1)
            pe.wait_ge(a_done, a_job["catT", KD - 1] + 1)
            for half in range(2):
                w = weights()
                for tt in range(NT):
                    ins = by_token(w, a_open(("mix", half, tt)), tt, hT)
                    if tt < NT - 1:
                        ins.then_inc(a_full, 1)
                finish(ins, a_full, a_job["mix", half, NT - 1] + 1)
            mod_columns(1)
            gate_rows("gate_f")
            pe.wait_ge(xn_ready, 2 * NT)
            for k in range(KD):
                transposes(d_open(("h2T", k)), lambda tt: cat[:, tt, k * P:(k + 1) * P], NT).then_inc(d_full, 1)
            pe.wait_ge(d_done, d_job["h2T", KD - 1] + 1)

            def square_sums(n):
                pe.wait_ge(qsq_ready, n + 1)
                for tt in range(NT):
                    ins = mm(bank[6][:, tt * HP + n:tt * HP + n + 1], qsq[:, n % 2, tt * P:(tt + 1) * P], ones[:],
                             start=True, stop=True)
                ins.then_inc(qss_done, 1)

            for n in range(HP):
                if n % 4 == 0:
                    w = weights()
                ins = by_feature(w, a_open(("q", n)), n % 4, h2T)
                if n % 4 < 3:
                    ins.then_inc(a_full, 1)
                else:
                    finish(ins, a_full, a_job["q", n] + 1)
                if n:
                    square_sums(n - 1)
            square_sums(HP - 1)

            def scores(tt):
                for q4 in range(HP // 4):
                    if q4 == 0 and tt:
                        pe.wait_ge(slotT_done, tt)
                    elif tt:
                        pe.wait_ge(s_done, (tt - 1) * (HP // 4) + q4 + 1)
                    for n in range(4 * q4, 4 * q4 + 4):
                        ins = mm(bank[SCORE_BANKS[q4]][:, (n % 4) * NK:(n % 4 + 1) * NK],
                                 qT[:, n, tt * P:(tt + 1) * P], keys[:, n], start=True, stop=True)
                    ins.then_inc(s_full, 1)

            pe.wait_ge(keys_loaded, 16)
            pe.wait_ge(qroot_ready, 1)
            scores(0)
            pe.sem_inc(g_full, OHR)
            for tt in range(NT):
                pe.wait_ge(slot_ready, tt + 1)
                transposes(bank[SCORE_BANKS[0]], lambda a: slot[:, a], 3).then_inc(slotT_full, 1)
                if tt + 1 < NT:
                    scores(tt + 1)
                with pe.Fori(0, NB) as bt:
                    for qd in range(QB):
                        pe.wait_ge(onehot_ready, bt * QB + (tt * NB * QB + qd + 1))
                        pe.wait_ge(g_done, bt * QB + (tt * NB * QB + qd + 1))
                        for j in range(QUAD):
                            o = (qd % OHR) * QUAD + j
                            ins = mm(bank[G_BANKS[qd]][:, j * NK:(j + 1) * NK], ohB[:, o], ohA[:, o],
                                     start=True, stop=True)
                        ins.then_inc(g_full, 1)

            pe.wait_ge(g_done, NT * NB * QB + QB)
            pe.wait_ge(hlo_ready, 1)
            pe.sem_inc(y_full, 1)

            def up(g, k):
                pe.wait_ge(ulo_ready, g * GROUP + (k + 1))
                if k >= 2:
                    pe.wait_ge(gelu_ready, g * GROUP + (k - 1))
                b = bank[UP_BANKS[k % 2]]
                for c in range(KD):
                    mm(b[:], uhi[:, k % 2, c], hhi[:, c], start=c == 0, stop=False)
                    mm(b[:], uhi[:, k % 2, c], hlo[:, c], start=False, stop=False)
                    ins = mm(b[:], ulo[:, k % 2, c], hhi[:, c], start=False, stop=c == KD - 1)
                ins.then_inc(up_full, 1)

            def down(b, blk, k):
                ts = slice(blk // 2 * P, (blk // 2 + 1) * P)
                ds = slice(blk % 2 * W, (blk % 2 + 1) * W)
                mm(b[:], ahi[:, k, ts], vhi[:, k, ds], start=k == 0, stop=False)
                mm(b[:], ahi[:, k, ts], vlo[:, k, ds], start=False, stop=False)
                return mm(b[:], alo[:, k, ts], vhi[:, k, ds], start=False, stop=k == GROUP - 1)

            with pe.Fori(0, NGROUPS) as g:
                for k in range(GROUP):
                    up(g, k)
                pe.wait_ge(vlo_ready, g * GROUP + (GROUP - 1))
                pe.wait_ge(alo_ready, g * GROUP + (GROUP - 1))
                for blk in range(2):
                    pe.wait_ge(y_done, g * 8 + (blk + 1))
                    for k in range(GROUP - 1):
                        down(bank[Y_BANKS[blk]], blk, k)
                pe.wait_ge(vlo_ready, g * GROUP + GROUP)
                pe.wait_ge(alo_ready, g * GROUP + GROUP)
                for blk in range(2):
                    down(bank[Y_BANKS[blk]], blk, GROUP - 1).then_inc(y_full, 1)
                for blk in range(2, 8):
                    pe.wait_ge(y_done, g * 8 + (blk + 1))
                    for k in range(GROUP):
                        ins = down(bank[Y_BANKS[blk % 4]], blk, k)
                    ins.then_inc(y_full, 1)


def kernel(x, c, w_ada, b_ada, pre_mix_g, post_mix_g, w_in, b_fox_f, hgrn_gamma, hgrn_norm_g, w_out,
           pre_ffn_g, post_ffn_g, peer_w_q, peer_sub_keys, peer_u, peer_v):
    import concourse.bacc as _bacc
    import numpy as np
    from concourse.bass_utils import run_bass_kernel_spmd as _run

    D = x.shape[-1]
    S = x.shape[1]
    n_keys = peer_sub_keys.shape[3]

    def arr(a):
        return np.ascontiguousarray(np.asarray(a))

    def columns(v):
        return arr(np.asarray(v).reshape(-1, P).T)

    s = np.arange(P)
    const_f = np.concatenate([
        np.eye(P), (s[:, None] <= s[None, :]), np.ones((P, 3 * P)), (s[:, None] > s[None, :]),
        np.broadcast_to(s[None, :], (P, P))], axis=1).astype(np.float32)
    masks = [s[:, None] == s[None, :]]
    for lev in range(1, 8):
        half = 1 << (lev - 1)
        same = s[:, None] // (2 * half) == s[None, :] // (2 * half)
        masks.append(same & (s[:, None] % (2 * half) < half) & (s[None, :] % (2 * half) >= half))
    const_m = arr(np.stack(masks, axis=1).astype(np.int32))

    b = np.asarray(b_ada)[0].reshape(6, D)
    width = hgrn_gamma.shape[1]
    fox = np.concatenate([np.asarray(b_fox_f)[0], np.zeros(width - b_fox_f.shape[1], np.float32)])
    arrays = {
        "x_in": arr(np.asarray(x)[0]),
        "c_col": columns(np.asarray(c)[0]),
        "w_ada": arr(np.asarray(w_ada)[0]),
        "b_ada_col": columns(np.asarray(b_ada)[0]),
        "gains_col": arr(np.stack([columns(np.asarray(pre_mix_g)[0]), columns(np.asarray(pre_ffn_g)[0])], axis=1)),
        "rows": arr(np.stack([b[2], b[5], np.asarray(post_mix_g)[0], np.asarray(post_ffn_g)[0]])),
        "w_in": arr(np.asarray(w_in)[0]),
        "hgrn_rows": arr(np.concatenate([np.asarray(hgrn_gamma), np.asarray(hgrn_norm_g), fox[None]])),
        "w_out": arr(np.asarray(w_out)[0]),
        "w_q": arr(np.asarray(peer_w_q)[0]),
        "keys_t": arr(np.asarray(peer_sub_keys)[0].reshape(-1, n_keys, P).transpose(2, 0, 1)),
        "u_t": arr(np.asarray(peer_u)[0].reshape(n_keys, n_keys, D // P, P).transpose(0, 3, 2, 1)),
        "v_in": arr(np.asarray(peer_v)[0]),
        "const_f": const_f,
        "const_m": const_m,
    }
    nc = _bacc.Bacc("TRN2", target_bir_lowering=False, num_devices=1)
    args = [nc.dram_tensor(n, a.shape, mybir.dt.from_np(a.dtype), kind="ExternalInput").ap()
            for n, a in arrays.items()]
    gate_map = nc.dram_tensor("gate_map", (n_keys, P, S), F32, kind="Internal").ap()
    out = nc.dram_tensor("y_out", (S, D), F32, kind="ExternalOutput").ap()
    hybrid_block(nc, *args, gate_map, out)
    r = _run(nc, [arrays], core_ids=[0])
    return r.results[0]["y_out"].reshape(1, S, D)
```

```python
from contextlib import ExitStack

import concourse.bass as bass
from concourse import mybir

P = 128
F32 = mybir.dt.float32
F32R = mybir.dt.float32r
I32 = mybir.dt.int32
U32 = mybir.dt.uint32
ALU = mybir.AluOpType
ACT = mybir.ActivationFunctionType
AX = mybir.AxisListType
MASKED = -3.0e38


def hybrid_block(nc, x_in, c_col, w_ada, b_ada_col, gains_col, rows, w_in, hgrn_rows, w_out,
                 w_q, keys_t, u_t, v_in, const_f, const_m, gate_map, gelus, out):
    S, D = x_in.shape
    NT = S // P
    KD = D // P
    W = 512
    FH, FD = 8, 64
    HH, HD = 4, 128
    PH, TOPK, NK = 8, 16, 128
    HP = 2 * PH
    SLOTS = PH * TOPK
    LEVELS = 8
    EPS = 1e-6
    GROUP = 4
    QUAD = 4
    HALF = P // 2
    STEP = 2 * 4 * QUAD
    SQ = STEP // QUAD
    OHR = 4
    FR = 4

    plan, n = [("up", HP, 10)], HP + 10
    for tt in range(NT):
        plan.append(("slots", tt))
        for half in range(2):
            plan.append(("maps", tt, half, n))
            n += 2 * (HALF // STEP)
            ups = 4 if half == 0 else 10 if tt < NT - 1 else 0
            for part, count in ((0, min(ups, 2)), (1, max(ups - 2, 0))):
                plan.append(("store", 2 * tt + half, part))
                if count:
                    plan.append(("up", n, count))
                    n += count
    N_UP0 = n
    SPILLED = n - HP
    NF = (NK - SPILLED) // GROUP
    ND = SPILLED // GROUP
    assert SPILLED % GROUP == 0 and ND % 2 == 0 and NF >= 2

    with ExitStack() as ctx:
        def sem(name):
            return ctx.enter_context(nc.semaphore(name))

        def sb(name, shape, dt=F32, where=ctx):
            return where.enter_context(nc.sbuf_tensor(name, shape, dt))

        bank = [ctx.enter_context(nc.psum_tensor(f"bank{i}", [P, W], F32)) for i in range(8)]

        x = sb("x", [P, NT, D])
        h2T = sb("h2T", [P, KD, S])
        hT = h2T
        gate_f = sb("gate_f", [P, D])
        ident = sb("ident", [P, P])
        iota = sb("iota", [P, P])
        eps = sb("eps", [P, 1])
        stat = sb("stat", [P, 4, NT])
        ones = sb("ones", [P, 1])

        mx = ExitStack()
        wring = sb("wring", [P, 2, KD, W], where=mx)
        cat = sb("cat", [P, NT, D], where=mx)
        fqk = sb("fqk", [P, 2, 4, S], where=mx)
        fqT, fkT = fqk[:, 0], fqk[:, 1]
        mix = fqk[:, :, :, :].rearrange("p a b c -> p (a b c)").rearrange("p (t d) -> p t d", t=NT)
        fv = sb("fv", [P, NT, 512], where=mx)
        hqk = sb("hqk", [P, 2 * HH, S], where=mx)
        hqT, hkT = hqk[:, 0:HH], hqk[:, HH:2 * HH]
        nFb = hqk
        hi = sb("hi", [P, NT, 512], where=mx)
        hg = sb("hg", [P, NT, 512], where=mx)
        logf = sb("logf", [P, NT, 512], where=mx)
        hk = sb("hk", [P, NT, 512], where=mx)
        gate_a = sb("gate_a", [P, D], where=mx)
        post_a = sb("post_a", [P, D], where=mx)
        post_f = sb("post_f", [P, D], where=mx)
        cond = sb("cond", [P, 2, KD], where=mx)
        wff = sb("wff", [P, KD, FH], where=mx)
        bada = sb("bada", [P, 48], where=mx)
        gains = sb("gains", [P, 2, KD], where=mx)
        shift = sb("shift", [P, 2, KD], where=mx)
        scale = sb("scale", [P, 2, KD], where=mx)
        gam = sb("gam", [P, 2, 512], where=mx)
        gmx = sb("gmx", [P, 512], where=mx)
        hng = sb("hng", [P, 512], where=mx)
        modt = sb("modt", [P, 2 * KD], where=mx)
        tri = sb("tri", [P, W + P], where=mx)
        lmask = sb("lmask", [P, LEVELS, P], I32, where=mx)
        ff = sb("ff", [P, 4, NT, FH], where=mx)
        fcol = sb("fcol", [P, NT, FH], where=mx)
        bfox = sb("bfox", [P, FH], where=mx)
        hss = sb("hss", [P, 2, NT, HH], where=mx)
        hx = ExitStack()
        AT = sb("AT", [P, 2, S], where=hx)
        dec = gam
        qe = sb("qe", [P, 2, S], where=hx)
        ke = sb("ke", [P, 2, S], where=hx)
        sc = sb("sc", [P, 2, S], where=hx)
        st = sb("st", [P, 2, 3, HD], where=hx)
        alast = sb("alast", [P, 2, NT], where=hx)
        hsq = gmx
        hx.close()
        fx = ExitStack()
        lg = sb("lg", [P, FR, S], where=fx)
        pr = sb("pr", [P, FR, S], where=fx)
        prT = logf
        rmax = sb("rmax", [P, NT, FH], where=fx)
        rsum = sb("rsum", [P, 2, NT, FH], where=fx)
        fx.close()
        mx.close()

        up_mem = ExitStack()
        hhi = sb("hhi", [P, KD, S], F32R, where=up_mem)
        hlo = sb("hlo", [P, KD, S], F32R, where=up_mem)
        uraw = sb("uraw", [P, 2, KD, P], where=up_mem)
        uhi = sb("uhi", [P, 2, KD, P], F32R, where=up_mem)
        ulo = sb("ulo", [P, 2, KD, P], F32R, where=up_mem)

        rt = ExitStack()
        stage = sb("stage", [P, NK, HALF], where=rt)
        qsq = stage[:, :, :].rearrange("p i t -> p (i t)").rearrange("p (n s) -> p n s", s=S)[:, 0:2]
        qT = sb("qT", [P, HP, S], where=rt)
        s1 = sb("s1", [P, HP, NK], where=rt)
        s2 = sb("s2", [P, HP, NK], where=rt)
        s3 = sb("s3", [P, HP, NK], where=rt)
        ohA = sb("ohA", [P, OHR * QUAD, NK], where=rt)
        ohB = sb("ohB", [P, OHR * QUAD, NK], where=rt)
        top = sb("top", [P, HP, TOPK], where=rt)
        topi = sb("topi", [P, HP, TOPK], U32, where=rt)
        topf = sb("topf", [P, HP, TOPK], where=rt)
        iota16 = iota[:, 0:TOPK]
        best = sb("best", [P, PH, TOPK], where=rt)
        pos = sb("pos", [P, 3, SLOTS], U32, where=rt)
        posf = sb("posf", [P, 2, SLOTS], where=rt)
        slot = sb("slot", [P, 3, SLOTS], where=rt)
        slotT = sb("slotT", [P, 3, P], where=rt)
        gsum = sb("gsum", [P, 2, PH], where=rt)
        rq = sb("rq", [P, 2, NT, HP], where=rt)
        rt.close()
        keys = h2T[:, 0:4, :].rearrange("p a (b k) -> p (a b) k", k=NK)
        spill = h2T[:, 4:6]

        ex = ExitStack()
        vraw = sb("vraw", [P, GROUP, D], where=ex)
        gmap = sb("gmap", [P, GROUP // 2, S // HALF, 2, HALF], where=ex)
        gel = sb("gel", [P, GROUP, S], where=ex)
        av = sb("av", [P, 2, S], where=ex)
        sets = [[sb("vhi0", [P, GROUP, D], F32R, where=ex), sb("vlo0", [P, GROUP, D], F32R, where=ex),
                 sb("ahi0", [P, GROUP, S], F32R, where=ex), sb("alo0", [P, GROUP, S], F32R, where=ex)]]
        ex.close()
        up_mem.close()
        sets.append([sb("vhi1", [P, GROUP, D], F32R, where=up_mem), sb("vlo1", [P, GROUP, D], F32R, where=up_mem),
                     sb("ahi1", [P, GROUP, S], F32R, where=up_mem), sb("alo1", [P, GROUP, S], F32R, where=up_mem)])
        up_mem.close()
        acc = h2T[:, :, :].rearrange("p a b -> p (a b)").rearrange("p (t d) -> p t d", t=NT)
        n_lev = LEVELS - 1
        sqs = cat

        def number(jobs):
            return {job: n for n, job in enumerate(jobs)}

        a_jobs, d_jobs = [], []
        a_jobs += [("f", tt) for tt in range(NT)] + [("hq", h) for h in range(HH)]
        a_jobs += [("hk", h) for h in range(HH)] + [("hi", tt) for tt in range(NT)]
        a_jobs += [("suffix", c) for c in range(NT - 1)]
        for h in range(HH):
            a_jobs += [("A", h), ("side", h, 0), ("side", h, 1)]
            a_jobs += [("o", h - 1)] if h else []
            a_jobs += [("side", h, 2), ("side", h, 3)]
        a_jobs += [("o", HH - 1), ("fcol",)] + [("nF", h) for h in range(FH)]
        a_jobs += [("pT", n) for n in range(NT * FH)] + [("catT", k) for k in range(KD)]
        a_jobs += [("mix", half, tt) for half in range(2) for tt in range(NT)]
        d_jobs += [("mod", 0)] + [("xT", k) for k in range(KD)] + [("ff",)]
        for h in range(HH):
            d_jobs += [("kv", h)] + [("level", h, lev) for lev in range(LEVELS)]
        d_jobs += [("gate_a", 0), ("gate_a", 1)] + [("logits", n) for n in range(NT * FH)]
        d_jobs += [("mod", 1), ("gate_f", 0), ("gate_f", 1)] + [("h2T", k) for k in range(KD)]
        a_job, d_job = number(a_jobs), number(d_jobs)
        A_BANKS, D_BANKS, O_BANKS = [0, 1, 2], [3, 4, 5], [6, 7]
        SCORE_BANKS, SLOT_BANK, G_BANKS = [4, 5], 4, [2, 3, 6, 7]
        UP_BANKS, Y_BANKS = [0, 1], [2, 3, 4, 5]

        def a_bank(job):
            return bank[A_BANKS[a_job[job] % 3]]

        def d_bank(job):
            return bank[D_BANKS[d_job[job] % 3]]

        w_loaded = [sem(f"w_loaded{i}") for i in range(2)]
        w_used = sem("w_used")
        small_loaded = sem("small_loaded")
        x_loaded = sem("x_loaded")
        keys_loaded = sem("keys_loaded")
        made = sem("made")
        cond_ready = sem("cond_ready")
        a_full = sem("a_full")
        a_done = sem("a_done")
        d_full = sem("d_full")
        d_done = sem("d_done")
        dve_chain = sem("dve_chain")
        act_chain = sem("act_chain")
        pool_chain = sem("pool_chain")
        sumsq_ready = sem("sumsq_ready")
        root_ready = sem("root_ready")
        xn_ready = sem("xn_ready")
        f_ready = sem("f_ready")
        logf_ready = sem("logf_ready")
        fz_ready = sem("fz_ready")
        fsoft_ready = sem("fsoft_ready")
        lff_ready = sem("lff_ready")
        kd_ready = sem("kd_ready")
        gam_ready = sem("gam_ready")
        game_ready = sem("game_ready")
        sc_zeroed = sem("sc_zeroed")
        diff_ready = sem("diff_ready")
        dec_ready = sem("dec_ready")
        qe_ready = sem("qe_ready")
        ke_ready = sem("ke_ready")
        alast_ready = sem("alast_ready")
        expA_ready = sem("expA_ready")
        qa_ready = sem("qa_ready")
        st_ready = sem("st_ready")
        hsq_ready = sem("hsq_ready")
        hsum_ready = sem("hsum_ready")
        hroot_ready = sem("hroot_ready")
        hcat_ready = sem("hcat_ready")
        mask_ready = sem("mask_ready")
        rmax_ready = sem("rmax_ready")
        pr_ready = sem("pr_ready")
        pv_done = sem("pv_done")
        fcat_ready = sem("fcat_ready")
        xmix_ready = sem("xmix_ready")
        qsq_ready = sem("qsq_ready")
        qss_done = sem("qss_done")
        qroot_ready = sem("qroot_ready")
        s_full = sem("s_full")
        s_done = sem("s_done")
        gmax_ready = sem("gmax_ready")
        gexp_ready = sem("gexp_ready")
        slot_ready = sem("slot_ready")
        slotT_full = sem("slotT_full")
        slotT_done = sem("slotT_done")
        onehot_ready = sem("onehot_ready")
        g_full = sem("g_full")
        g_done = sem("g_done")
        map_stored = sem("map_stored")
        routed = sem("routed")
        hhi_ready = sem("hhi_ready")
        hlo_ready = sem("hlo_ready")
        q_ready = sem("q_ready")
        u_loaded = [sem(f"u_loaded{i}") for i in range(2)]
        v_loaded = [sem(f"v_loaded{i}") for i in range(GROUP)]
        g_loaded = [sem(f"g_loaded{i}") for i in range(GROUP // 2)]
        s_loaded = [sem(f"s_loaded{i}") for i in range(GROUP)]
        spilled = [sem(f"spilled{i}") for i in range(2)]
        uhi_ready = sem("uhi_ready")
        ulo_ready = sem("ulo_ready")
        vhi_ready = sem("vhi_ready")
        vlo_ready = sem("vlo_ready")
        up_full = sem("up_full")
        up_done = sem("up_done")
        av_ready = sem("av_ready")
        ahi_ready = sem("ahi_ready")
        alo_ready = sem("alo_ready")
        y_full = sem("y_full")
        y_done = sem("y_done")
        out_ready = sem("out_ready")
        stored = sem("stored")

        FF = 3 * FH * FD
        HQ, HF, HI, HG = [FF + FH + i * 512 for i in range(4)]
        chunks = [(w_ada, n * W) for n in range(4)]
        chunks += [(w_in, n) for n in (HF, HQ, HI, 0, 512, 1024, HG)]
        chunks += [(w_ada, n * W) for n in (4, 5)]
        chunks += [(w_out, 0), (w_out, W)]
        chunks += [(w_ada, n * W) for n in range(6, 12)]
        loads = [(cond[:, 0], c_col), (bada[:], b_ada_col), (gains[:], gains_col),
                 (gate_a[:], rows[0].partition_broadcast(P)), (gate_f[:], rows[1].partition_broadcast(P)),
                 (post_a[:], rows[2].partition_broadcast(P)), (post_f[:], rows[3].partition_broadcast(P)),
                 (gam[:, 0], hgrn_rows[0].partition_broadcast(P)),
                 (gam[:, 1], hgrn_rows[1].partition_broadcast(P)),
                 (hng[:], hgrn_rows[2].partition_broadcast(P)),
                 (bfox[:], hgrn_rows[3, 0:FH].partition_broadcast(P)),
                 (ident[:], const_f[:, 0:P]), (tri[:], const_f[:, P:2 * P + W]),
                 (iota[:], const_f[:, 2 * P + W:3 * P + W]), (lmask[:], const_m),
                 (wff[:], w_in[:, FF:FF + FH].rearrange("(k p) n -> p k n", p=P))]
        SMALL = 16 * len(loads)
        N_FOX = NT * FH

        block = ctx.enter_context(nc.Block())

        @block.sync
        def _(sp):
            for tt in range(NT):
                sp.dma_start(x[:, tt, :], x_in[tt * P:(tt + 1) * P, :]).then_inc(x_loaded, 16)
            for n, (w, c0) in enumerate(chunks):
                if n >= 2:
                    sp.wait_ge(w_used, n - 1)
                sp.dma_start(wring[:, n % 2], w[:, c0:c0 + W].rearrange("(k p) n -> p k n", p=P)
                             ).then_inc(w_loaded[n % 2], 16)
            sp.wait_ge(d_done, d_job["h2T", KD - 1] + 1)
            for n in range(HP):
                if n >= 2:
                    sp.wait_ge(ulo_ready, n - 1)
                sp.dma_start(uraw[:, n % 2], w_q[n]).then_inc(u_loaded[n % 2], 16)
                if n == 1:
                    sp.wait_ge(hlo_ready, KD)
                    sp.dma_start(keys, keys_t).then_inc(keys_loaded, 16)

            def load_u(n, par):
                sp.wait_ge(ulo_ready, n - 1)
                sp.dma_start(uraw[:, par], u_t[bass.ds(n - HP, 1)].rearrange("a p c e -> p (a c) e")
                             ).then_inc(u_loaded[par], 16)

            def store_gelu(n, par):
                sp.wait_ge(up_done, n + 1)
                sp.dma_start(gelus[bass.ds(n - HP, 1)].rearrange("a e t -> e (a t)"), spill[:, par]
                             ).then_inc(spilled[par], 16)

            for n in range(HP, HP + 4):
                load_u(n, n % 2)
            for what, *at in plan:
                if what == "up":
                    n0, count = at
                    with sp.Fori(0, count // 2) as i:
                        for par in range(2):
                            store_gelu(i * 2 + (n0 + par), par)
                            load_u(i * 2 + (n0 + par + 4), par)
                elif what == "maps":
                    tt, half, n0 = at
                    with sp.Fori(0, HALF // STEP) as i:
                        for par in range(2):
                            store_gelu(i * 2 + (n0 + par), par)
                            load_u(i * 2 + (n0 + par + 4), par)
                elif what == "store":
                    c, part = at
                    sp.wait_ge(g_done, (c + 1) * (HALF // QUAD) + len(G_BANKS))
                    tiles = slice(part * NK // 2, (part + 1) * NK // 2)
                    sp.dma_start(gate_map[c, :, tiles], stage[:, tiles]).then_inc(map_stored, 16)
            sp.wait_ge(routed, 1)
            sp.wait_ge(g_full, S // QUAD + OHR)
            sp.wait_ge(map_stored, 64 * NT)

            def load_v(tile, grp, k, first=False):
                if not first:
                    sp.wait_ge(vlo_ready, (grp - 1) * GROUP + (k + 1))
                sp.dma_start(vraw[:, k], v_in[bass.ds(tile * P, P), :]).then_inc(v_loaded[k], 16)
                if k % 2:
                    if not first:
                        sp.wait_ge(av_ready, (grp - 1) * GROUP + (k + 1))
                    sp.dma_start(gmap[:, k // 2].rearrange("p c i t -> p c (i t)"),
                                 gate_map[:, :, bass.ds(tile - 1, 2)].rearrange("c j i t -> j c (i t)")
                                 ).then_inc(g_loaded[k // 2], 16)

            for k in range(GROUP):
                load_v(SPILLED + k, 0, k, first=True)
            with sp.Fori(1, NF) as g:
                for k in range(GROUP):
                    load_u((g - 1) * GROUP + (N_UP0 + k + 4), k % 2)
                    load_v(g * GROUP + (SPILLED + k), g, k)
            with sp.Fori(0, ND) as g:
                for k in range(GROUP):
                    load_v(g * GROUP + k, g + NF, k)
                    sp.wait_ge(av_ready, (g + (NF - 1)) * GROUP + (k + 1))
                    sp.dma_start(gel[:, k], gelus[bass.ds(g * GROUP + k, 1)].rearrange("a e t -> e (a t)")
                                 ).then_inc(s_loaded[k], 16)
            for tt in range(NT):
                sp.wait_ge(out_ready, tt + 1)
                sp.dma_start(out[tt * P:(tt + 1) * P, :], acc[:, tt, :]).then_inc(stored, 16)
            sp.wait_ge(stored, 16 * NT)

        @block.gpsimd
        def _(pool):
            for dst, src in loads:
                pool.dma_start(dst, src).then_inc(small_loaded, 16)
            pool.wait_ge(a_done, a_job["hk", HH - 1] + 1)
            for h in range(HH):
                for lev in range(1, LEVELS):
                    n = h * n_lev + lev - 1
                    pool.wait_ge(dec_ready, n + 1)
                    if n >= 2:
                        h2, l2 = divmod(n - 2, n_lev)
                        pool.wait_ge(d_full, d_job["level", h2, l2 + 1] + 1)
                    nc.gpsimd.tensor_tensor(ke[:, n % 2], hkT[:, h], dec[:, n % 2], ALU.mult
                                            ).then_inc(ke_ready, 1)
            for n in range(N_FOX):
                tt = n // FH
                pool.wait_ge(d_done, d_job["logits", n] + 1)
                blk = lg[:, n % FR, tt * P:(tt + 1) * P]
                nc.gpsimd.affine_select(out=blk, in_=blk, compare_op=ALU.is_ge, fill=MASKED, base=0,
                                        pattern=[[-1, P]], channel_multiplier=1).then_inc(mask_ready, 1)

            def split_u(n, par):
                pool.wait_ge(uhi_ready, n + 1)
                nc.gpsimd.tensor_tensor(ulo[:, par], uraw[:, par], uhi[:, par].bitcast(F32), ALU.subtract
                                        ).then_inc(ulo_ready, 1)

            for n in range(HP + 2):
                split_u(n, n % 2)
            for what, *at in plan:
                if what == "up":
                    n0, count = at
                    with pool.Fori(0, count // 2) as i:
                        for par in range(2):
                            split_u(i * 2 + (n0 + par + 2), par)
                elif what == "maps":
                    tt, half, n0 = at
                    with pool.Fori(0, HALF // STEP) as i:
                        for par in range(2):
                            split_u(i * 2 + (n0 + par + 2), par)
            with pool.Fori(0, NF - 1) as g:
                for k in range(GROUP):
                    split_u(g * GROUP + (N_UP0 + k + 2), k % 2)
            for k in range(GROUP - 2):
                split_u((NF - 1) * GROUP + N_UP0 + k + 2, k % 2)

        @block.scalar
        def _(act):
            chain = [0]

            def link(ins):
                chain[0] += 1
                ins.then_inc(act_chain, 1)
                act.wait_ge(act_chain, chain[0])

            def move(job, dst, func=ACT.Copy, cols=W, split=None, **kw):
                act.wait_ge(a_full, a_job[job] + 1)
                src = a_bank(job)[:, 0:cols]
                if split:
                    src = src.rearrange("p (c v) -> p c v", c=split)
                nc.scalar.activation(dst, src, func, **kw).then_inc(a_done, 1)

            def roots(n, src, dst):
                for tt in range(NT):
                    nc.scalar.activation(dst[:, tt, :], src[:, tt, :], ACT.Square,
                                         accum_out=stat[:, 0, tt:tt + 1]).then_inc(sumsq_ready, 1)
                act.wait_ge(sumsq_ready, (n + 1) * NT)
                nc.scalar.activation(stat[:, 1, :], stat[:, 0, :], ACT.Sqrt, bias=eps[:], scale=1.0 / D
                                     ).then_inc(root_ready, 1)

            act.wait_ge(small_loaded, SMALL)
            nc.scalar.activation(cond[:, 1], cond[:, 0], ACT.Silu).then_inc(cond_ready, 1)
            act.wait_ge(x_loaded, 16 * NT)
            act.wait_ge(made, 2)
            roots(0, x, sqs)
            act.wait_ge(gam_ready, 1)
            nc.scalar.activation(gam[:], gam[:], ACT.Exp).then_inc(game_ready, 1)
            for tt in range(NT):
                move(("f", tt), logf[:, tt, :], ACT.Sigmoid)
            for h in range(HH):
                move(("hq", h), hqT[:, h], scale=HD ** -0.5)
            act.wait_ge(fz_ready, 1)
            link(nc.scalar.activation(ff[:, 2], ff[:, 1], ACT.Exp, scale=-1.0))
            nc.scalar.activation(ff[:, 3], ff[:, 2], ACT.Ln, bias=ones[:]).then_inc(fsoft_ready, 1)
            act.wait_ge(f_ready, 1)
            nc.scalar.activation(logf[:], logf[:], ACT.Ln).then_inc(logf_ready, 1)
            for h in range(HH):
                move(("hk", h), hkT[:, h])
            for tt in range(NT):
                move(("hi", tt), hi[:, tt, :])
            for c in range(NT - 1):
                move(("suffix", c), cat[:, c, 0:512], ACT.Exp)

            def output_of(h):
                o_h = cat[:, :, 512 + h * HD:512 + (h + 1) * HD]
                move(("o", h), o_h, split=NT)
                act.wait_ge(a_done, a_job["o", h] + 1)
                if h:
                    act.wait_ge(hsum_ready, h)
                nc.scalar.activation(hsq[:].rearrange("p (c v) -> p c v", c=NT), o_h, ACT.Square
                                     ).then_inc(hsq_ready, 1)

            sides = [(fqT, ACT.Copy, FD ** -0.5), (fkT, ACT.Copy, 1.0), (fv, ACT.Copy, 1.0), (hg, ACT.Silu, 1.0)]
            for h in range(HH):
                if h:
                    act.wait_ge(diff_ready, h * n_lev)
                    act.wait_ge(expA_ready, h)
                move(("A", h), AT[:, 0])
                act.wait_ge(a_done, a_job["A", h] + 1)
                if h >= 2:
                    act.wait_ge(st_ready, h - 1)
                nc.scalar.activation(alast[:, h % 2], AT[:, 0].rearrange("p (c t) -> p c t", c=NT)[:, :, P - 1],
                                     ACT.Exp).then_inc(alast_ready, 1)
                dst, func, mul = sides[h]
                for j in range(NT):
                    move(("side", h, j), dst[:, j], func, scale=mul)
                    for lev in (2 * j + 1, 2 * j + 2):
                        if lev < LEVELS:
                            n = h * n_lev + lev - 1
                            act.wait_ge(diff_ready, n + 1)
                            link(nc.scalar.activation(dec[:, n % 2], dec[:, n % 2], ACT.Abs))
                            nc.scalar.activation(dec[:, n % 2], dec[:, n % 2], ACT.Exp, scale=-1.0
                                                 ).then_inc(dec_ready, 1)
                    if j == 1 and h:
                        output_of(h - 1)
                nc.scalar.activation(AT[:, 1], AT[:, 0], ACT.Exp).then_inc(expA_ready, 1)
            output_of(HH - 1)
            act.wait_ge(hsum_ready, HH)
            nc.scalar.activation(hss[:, 1], hss[:, 0], ACT.Sqrt, bias=eps[:], scale=1.0 / HD
                                 ).then_inc(hroot_ready, 1)
            move(("fcol",), fcol[:].rearrange("p t h -> p (t h)"), cols=NT * FH)
            act.wait_ge(hcat_ready, 1)
            for h in range(FH):
                move(("nF", h), nFb[:, h], scale=-1.0)
            for n in range(N_FOX):
                tt, h = divmod(n, FH)
                w = (tt + 1) * P
                act.wait_ge(rmax_ready, n + 1)
                nc.scalar.activation(pr[:, n % FR, 0:w], lg[:, n % FR, 0:w], ACT.Exp, bias=rmax[:, tt, h:h + 1],
                                     accum_out=rsum[:, 0, tt, h:h + 1]).then_inc(pr_ready, 1)
                if n >= FR:
                    act.wait_ge(pv_done, n - FR + 1)
                move(("pT", n), prT[:, n % FR, 0:w], cols=w)
            for k in range(KD):
                move(("catT", k), hT[:, k])
            for half in range(2):
                for tt in range(NT):
                    move(("mix", half, tt), mix[:, tt, half * W:(half + 1) * W])
            act.wait_ge(a_done, a_job["mix", 1, NT - 1] + 1)
            roots(1, mix, cat)
            act.wait_ge(xmix_ready, 1)
            roots(2, x, mix)
            for k in range(KD):
                if k == 0:
                    act.wait_ge(d_done, d_job["h2T", KD - 1] + 1)
                nc.scalar.activation(hhi[:, k], h2T[:, k], ACT.Copy).then_inc(hhi_ready, 1)

            def split_u(n, par):
                act.wait_ge(u_loaded[par], (n - par) * 8 + 16)
                nc.scalar.activation(uhi[:, par], uraw[:, par], ACT.Copy).then_inc(uhi_ready, 1)

            split_u(0, 0)
            split_u(1, 1)
            for n in range(HP):
                act.wait_ge(up_full, n + 1)
                nc.scalar.activation(qT[:, n], bank[UP_BANKS[n % 2]][:], ACT.Copy).then_inc(up_done, 1)
                split_u(n + 2, n % 2)
                act.wait_ge(up_done, n + 1)
                if n >= 2:
                    act.wait_ge(qss_done, n - 1)
                nc.scalar.activation(qsq[:, n % 2], qT[:, n], ACT.Square).then_inc(qsq_ready, 1)
            act.wait_ge(qss_done, HP)
            nc.scalar.activation(rq[:, 0], bank[6][:, 0:NT * HP].rearrange("p (t n) -> p t n", t=NT), ACT.Sqrt,
                                 bias=eps[:], scale=1.0 / P).then_inc(qroot_ready, 1)
            act.wait_ge(qroot_ready, 1)
            act.sem_inc(g_done, len(G_BANKS))

            def gelu_spilled(n, par, first=False):
                act.wait_ge(up_full, n + 1)
                if not first:
                    act.wait_ge(spilled[par], (n - (HP + par)) * 8)
                nc.scalar.activation(spill[:, par], bank[UP_BANKS[par]][:], ACT.Gelu).then_inc(up_done, 1)
                split_u(n + 2, par)

            halves_done = 0
            for what, *at in plan:
                if what == "up":
                    n0, count = at
                    start = 0
                    if n0 == HP:
                        act.wait_ge(hlo_ready, KD)
                        gelu_spilled(HP, 0, first=True)
                        gelu_spilled(HP + 1, 1, first=True)
                        start = 1
                    with act.Fori(start, count // 2) as i:
                        for par in range(2):
                            gelu_spilled(i * 2 + (n0 + par), par)
                elif what == "slots":
                    act.wait_ge(gmax_ready, at[0] + 1)
                    nc.scalar.activation(best[:], best[:], ACT.Exp).then_inc(gexp_ready, 1)
                elif what == "maps":
                    tt, half, n0 = at
                    if halves_done:
                        act.wait_ge(map_stored, 32 * halves_done)
                    halves_done += 1
                    with act.Fori(0, HALF // STEP) as i:
                        for qd in range(SQ):
                            act.wait_ge(g_full, i * SQ + ((2 * tt + half) * (HALF // QUAD) + qd + 1 + OHR))
                            dst = stage[:, :, bass.ds(i * STEP + qd * QUAD, QUAD)].rearrange("p i t -> p t i")
                            nc.scalar.activation(dst, bank[G_BANKS[qd % 4]][:].rearrange("p (t i) -> p t i", t=QUAD),
                                                 ACT.Copy).then_inc(g_done, 1)
                            if qd % (SQ // 2) == SQ // 2 - 1:
                                par = qd // (SQ // 2)
                                gelu_spilled(i * 2 + (n0 + par), par)
            act.wait_ge(map_stored, 64 * NT)
            act.wait_ge(routed, 1)
            act.wait_ge(g_full, S // QUAD + OHR)

            def split_v(grp, k, which):
                act.wait_ge(v_loaded[k], grp * 16 + 16)
                nc.scalar.activation(sets[which][0][:, k], vraw[:, k], ACT.Copy).then_inc(vhi_ready, 1)

            def split_a(grp, k, which):
                act.wait_ge(av_ready, grp * GROUP + (k + 1))
                nc.scalar.activation(sets[which][2][:, k], av[:, k % 2], ACT.Copy).then_inc(ahi_ready, 1)

            def fused(g, last):
                for k in range(GROUP):
                    n = g * GROUP + (N_UP0 + k)
                    act.wait_ge(up_full, n + 1)
                    nc.scalar.activation(gel[:, k], bank[UP_BANKS[k % 2]][:], ACT.Gelu).then_inc(up_done, 1)
                    if not last or k + 2 < GROUP:
                        split_u(n + 2, k % 2)
                    if k == 0:
                        act.wait_ge(y_full, g * 8 + 1)
                    split_v(g, k, 0)
                    split_a(g, k, 0)

            with act.Fori(0, NF - 1) as g:
                fused(g, False)
            fused(NF - 1, True)

            def second_only(grp, which, guard=True):
                for k in range(GROUP):
                    if k == 0 and guard:
                        act.wait_ge(y_full, (grp - 1) * 8 + 1)
                    split_v(grp, k, which)
                    split_a(grp, k, which)

            with act.Fori(0, ND // 2) as i:
                second_only(i * 2 + NF, 1)
                second_only(i * 2 + (NF + 1), 0)
            act.wait_ge(y_done, 8 * (NF + ND) + len(Y_BANKS))
            roots(3, acc, vraw)

        @block.vector
        def _(dve):
            chain = [0]

            def link(ins):
                chain[0] += 1
                ins.then_inc(dve_chain, 1)
                dve.wait_ge(dve_chain, chain[0])

            def full(job):
                dve.wait_ge(d_full, d_job[job] + 1)
                return d_bank(job)

            def mod_columns(i):
                b = full(("mod", i))
                link(nc.vector.tensor_tensor(modt[:], b[:, 0:2 * KD], bada[:, 24 * i:24 * i + 2 * KD], ALU.add))
                nc.vector.scalar_tensor_tensor(scale[:, i], modt[:, KD:2 * KD], 1.0, gains[:, i], ALU.add, ALU.mult)
                link(nc.vector.tensor_copy(shift[:, i], modt[:, 0:KD]))
                dve.sem_inc(d_done, 1)

            def gate_rows(name, gate, post):
                for half in range(2):
                    b = full((name, half))
                    cols = slice(half * W, (half + 1) * W)
                    link(nc.vector.tensor_tensor(gate[:, cols], gate[:, cols], b[:], ALU.add))
                    nc.vector.tensor_tensor(gate[:, cols], gate[:, cols], post[:, cols], ALU.mult
                                            ).then_inc(d_done, 1)

            def transposed(name, dst, i):
                for k in range(KD):
                    b = full((name, k))
                    nc.vector.tensor_scalar(dst[:, k], b[:], scale[:, i, k:k + 1], shift[:, i, k:k + 1],
                                            ALU.mult, ALU.add).then_inc(d_done, 1)

            nc.vector.memset(eps[:], EPS).then_inc(made, 1)
            nc.vector.memset(ones[:], 1.0).then_inc(made, 1)
            dve.wait_ge(small_loaded, SMALL)
            link(nc.vector.tensor_tensor(gmx[:], gam[:, 0], gam[:, 1], ALU.max))
            nc.vector.tensor_tensor(gam[:, 0], gam[:, 0], gmx[:], ALU.subtract)
            nc.vector.tensor_tensor(gam[:, 1], gam[:, 1], gmx[:], ALU.subtract).then_inc(gam_ready, 1)
            dve.wait_ge(game_ready, 1)
            link(nc.vector.tensor_tensor(gmx[:], gam[:, 0], gam[:, 1], ALU.add))
            link(nc.vector.reciprocal(gmx[:], gmx[:]))
            link(nc.vector.tensor_tensor(gam[:, 0], gam[:, 0], gmx[:], ALU.mult))
            link(nc.vector.tensor_scalar(gam[:, 1], gam[:, 0], -1.0, 1.0, ALU.mult, ALU.add))
            dve.wait_ge(root_ready, 1)
            link(nc.vector.reciprocal(stat[:, 2], stat[:, 1]))
            for tt in range(NT):
                nc.vector.tensor_scalar(cat[:, tt], x[:, tt], stat[:, 2, tt:tt + 1], None, ALU.mult
                                        ).then_inc(xn_ready, 1)
            mod_columns(0)
            transposed("xT", hT, 0)
            for tt in range(NT):
                dve.wait_ge(a_done, a_job["f", tt] + 1)
                link(nc.vector.tensor_tensor(logf[:, tt], logf[:, tt], gam[:, 1], ALU.mult))
                link(nc.vector.tensor_tensor(logf[:, tt], logf[:, tt], gam[:, 0], ALU.add))
                ins = nc.vector.tensor_scalar(hk[:, tt], logf[:, tt], -1.0, 1.0, ALU.mult, ALU.add)
            ins.then_inc(f_ready, 1)
            b = full(("ff",))
            link(nc.vector.tensor_tensor(ff[:, 0], b[:, 0:NT * FH].rearrange("p (t h) -> p t h", t=NT),
                                         bfox[:].unsqueeze(1).to_broadcast([P, NT, FH]), ALU.add))
            dve.sem_inc(d_done, 1)
            nc.vector.scalar_tensor_tensor(ff[:, 1], ff[:, 0], -1.0, ff[:, 0], ALU.mult, ALU.max).then_inc(fz_ready, 1)
            dve.wait_ge(fsoft_ready, 1)
            nc.vector.scalar_tensor_tensor(ff[:, 0], ff[:, 0], 0.0, ff[:, 3], ALU.min, ALU.subtract
                                           ).then_inc(lff_ready, 1)
            dve.wait_ge(a_done, a_job["hk", HH - 1] + 1)
            for c in range(NT - 1):
                dve.wait_ge(a_done, a_job["suffix", c] + 1)
                nc.vector.tensor_tensor(hk[:, c], hk[:, c], cat[:, c, 0:512], ALU.mult).then_inc(kd_ready, 1)

            def difference(h, lev):
                n = h * n_lev + lev - 1
                half = 1 << (lev - 1)
                a = AT[:, 0].rearrange("p (g u) -> p g u", u=2 * half)
                mid = a[:, :, half - 1:half].to_broadcast([P, S // (2 * half), 2 * half])
                if n >= 2:
                    dve.wait_ge(ke_ready, n - 1)
                nc.vector.tensor_tensor(dec[:, n % 2].rearrange("p (g u) -> p g u", u=2 * half), a, mid,
                                        ALU.subtract).then_inc(diff_ready, 1)

            def keep(h, lev):
                b = full(("level", h, lev))
                nc.vector.copy_predicated(sc[:, h % 2].rearrange("p (c t) -> p c t", c=NT),
                                          lmask[:, lev].unsqueeze(1).to_broadcast([P, NT, P]),
                                          b[:].rearrange("p (c t) -> p c t", c=NT)).then_inc(d_done, 1)

            def sum_squares(h):
                dve.wait_ge(hsq_ready, h + 1)
                nc.vector.tensor_reduce(hss[:, 0, :, h:h + 1].rearrange("p c o -> p (c o)"),
                                        hsq[:].rearrange("p (c v) -> p c v", c=NT), AX.X, ALU.add
                                        ).then_inc(hsum_ready, 1)

            for h in range(HH):
                dve.wait_ge(a_done, a_job["A", h] + 1)
                difference(h, 1)
                difference(h, 2)
                b = full(("kv", h))
                dve.wait_ge(alast_ready, h + 1)
                if h >= 2:
                    dve.wait_ge(a_full, a_job["o", h - 2] + 1)
                link(nc.vector.memset(sc[:, h % 2], 0.0))
                link(nc.vector.tensor_copy(st[:, h % 2, 0], b[:, 0:HD]))
                link(nc.vector.scalar_tensor_tensor(st[:, h % 2, 1], st[:, h % 2, 0], alast[:, h % 2, 1:2],
                                                    b[:, HD:2 * HD], ALU.mult, ALU.add))
                link(nc.vector.scalar_tensor_tensor(st[:, h % 2, 2], st[:, h % 2, 1], alast[:, h % 2, 2:3],
                                                    b[:, 2 * HD:3 * HD], ALU.mult, ALU.add))
                dve.sem_inc(d_done, 1)
                dve.sem_inc(st_ready, 1)
                keep(h, 0)
                for lev in range(1, LEVELS):
                    n = h * n_lev + lev - 1
                    dve.wait_ge(dec_ready, n + 1)
                    nc.vector.tensor_tensor(qe[:, n % 2], hqT[:, h], dec[:, n % 2], ALU.mult).then_inc(qe_ready, 1)
                    if lev + 2 < LEVELS:
                        dve.wait_ge(qe_ready, n + 1)
                        difference(h, lev + 2)
                    dve.wait_ge(d_done, d_job["level", h, lev - 1] + 1)
                    keep(h, lev)
                dve.wait_ge(expA_ready, h + 1)
                nc.vector.tensor_tensor(AT[:, 1], AT[:, 1], hqT[:, h], ALU.mult).then_inc(qa_ready, 1)
                if h:
                    sum_squares(h - 1)
            sum_squares(HH - 1)
            dve.wait_ge(hroot_ready, 1)
            link(nc.vector.reciprocal(hss[:, 0], hss[:, 1]))
            for c in range(NT):
                o_c = cat[:, c, 512:1024].rearrange("p (h v) -> p h v", h=HH)
                nc.vector.tensor_tensor(o_c, o_c, hss[:, 0, c].unsqueeze(2).to_broadcast([P, HH, HD]), ALU.mult)
                ins = nc.vector.tensor_tensor(hg[:, c], hg[:, c], hng[:], ALU.mult)
            link(ins)
            ins = nc.vector.tensor_tensor(cat[:, :, 512:1024], cat[:, :, 512:1024], hg[:], ALU.mult)
            ins.then_inc(hcat_ready, 1)
            gate_rows("gate_a", gate_a, post_a)

            def logits(n):
                tt, h = divmod(n, FH)
                w = (tt + 1) * P
                b = full(("logits", n))
                if n >= FR:
                    dve.wait_ge(pr_ready, n - FR + 1)
                nc.vector.scalar_tensor_tensor(lg[:, n % FR, 0:w], nFb[:, h, 0:w], fcol[:, tt, h:h + 1], b[:, 0:w],
                                               ALU.add, ALU.add).then_inc(d_done, 1)

            def fox_out(tt):
                dve.wait_ge(pv_done, (tt + 1) * FH)
                link(nc.vector.reciprocal(rsum[:, 1, tt], rsum[:, 0, tt]))
                nc.vector.tensor_tensor(cat[:, tt, 0:512].rearrange("p (h d) -> p h d", h=FH),
                                        bank[O_BANKS[tt % 2]][:].rearrange("p (h d) -> p h d", h=FH),
                                        rsum[:, 1, tt].unsqueeze(2).to_broadcast([P, FH, FD]), ALU.mult
                                        ).then_inc(fcat_ready, 1)

            dve.wait_ge(a_done, a_job["nF", FH - 1] + 1)
            logits(0)
            logits(1)
            for n in range(N_FOX):
                tt, h = divmod(n, FH)
                if n + 2 < N_FOX:
                    logits(n + 2)
                dve.wait_ge(mask_ready, n + 1)
                link(nc.vector.tensor_reduce(rmax[:, tt, h:h + 1], lg[:, n % FR, 0:(tt + 1) * P], AX.X, ALU.max))
                nc.vector.tensor_scalar(rmax[:, tt, h:h + 1], rmax[:, tt, h:h + 1], -1.0, None, ALU.mult
                                        ).then_inc(rmax_ready, 1)
                if tt and h == 3:
                    fox_out(tt - 1)
            fox_out(NT - 1)
            dve.wait_ge(root_ready, 2)
            link(nc.vector.reciprocal(stat[:, 2], stat[:, 1]))
            for tt in range(NT):
                ins = nc.vector.scalar_tensor_tensor(mix[:, tt], mix[:, tt], stat[:, 2, tt:tt + 1], gate_a[:],
                                                     ALU.mult, ALU.mult)
            link(ins)
            nc.vector.tensor_tensor(x[:], x[:], mix, ALU.add).then_inc(xmix_ready, 1)
            mod_columns(1)
            gate_rows("gate_f", gate_f, post_f)
            dve.wait_ge(root_ready, 3)
            link(nc.vector.reciprocal(stat[:, 2], stat[:, 1]))
            for tt in range(NT):
                nc.vector.tensor_scalar(cat[:, tt], x[:, tt], stat[:, 2, tt:tt + 1], None, ALU.mult
                                        ).then_inc(xn_ready, 1)
            transposed("h2T", h2T, 1)

            for k in range(KD):
                dve.wait_ge(hhi_ready, k + 1)
                nc.vector.tensor_tensor(hlo[:, k], h2T[:, k], hhi[:, k].bitcast(F32), ALU.subtract
                                        ).then_inc(hlo_ready, 1)

            dve.wait_ge(qroot_ready, 1)
            link(nc.vector.reciprocal(rq[:, 1], rq[:, 0]))
            pairs = [s1, s2, s3]
            c1, c2, c3 = [s[:].rearrange("p n k -> p (n k)").rearrange("p (h a b) -> p h a b", h=PH, a=TOPK)
                          for s in pairs]
            f1, f3 = [s[:].rearrange("p n k -> p (n k)").rearrange("p (h c) -> p h c", h=PH) for s in (s1, s3)]
            halves = top[:].rearrange("p (h two) k -> p h two k", two=2)
            halvesf = topf[:].rearrange("p (h two) k -> p h two k", two=2)
            posk = pos[:, 0].rearrange("p (h k) -> p h k", h=PH)

            def take_scores(tt):
                for q4 in range(HP // 4):
                    dve.wait_ge(s_full, tt * (HP // 4) + (q4 + 1))
                    ns = slice(4 * q4, 4 * q4 + 4)
                    nc.vector.tensor_tensor(s1[:, ns], bank[SCORE_BANKS[q4 % 2]][:].rearrange("p (n k) -> p n k", n=4),
                                            rq[:, 1, tt, ns].unsqueeze(2).to_broadcast([P, 4, NK]), ALU.mult
                                            ).then_inc(s_done, 1)
                dve.wait_ge(s_done, (tt + 1) * (HP // 4))

            take_scores(0)
            for tt in range(NT):
                for n in range(HP):
                    ins = nc.vector.max(top[:, n, 0:8], s1[:, n])
                link(ins)
                for n in range(HP):
                    nc.vector.max_index(topi[:, n, 0:8], top[:, n, 0:8], s1[:, n])
                    ins = nc.vector.match_replace(s2[:, n], top[:, n, 0:8], s1[:, n], MASKED)
                link(ins)
                for n in range(HP):
                    ins = nc.vector.max(top[:, n, 8:16], s2[:, n])
                link(ins)
                for n in range(HP):
                    ins = nc.vector.max_index(topi[:, n, 8:16], top[:, n, 8:16], s2[:, n])
                link(ins)
                nc.vector.tensor_copy(topf[:], topi[:])
                link(nc.vector.tensor_tensor(c3, halves[:, :, 0].unsqueeze(3).to_broadcast([P, PH, TOPK, TOPK]),
                                            halves[:, :, 1].unsqueeze(2).to_broadcast([P, PH, TOPK, TOPK]), ALU.add))
                for h in range(PH):
                    ins = nc.vector.max(best[:, h, 0:8], f3[:, h])
                link(ins)
                for h in range(PH):
                    nc.vector.max_index(posk[:, h, 0:8], best[:, h, 0:8], f3[:, h])
                    ins = nc.vector.match_replace(f1[:, h], best[:, h, 0:8], f3[:, h], MASKED)
                link(ins)
                for h in range(PH):
                    ins = nc.vector.max(best[:, h, 8:16], f1[:, h])
                link(ins)
                for h in range(PH):
                    nc.vector.max_index(posk[:, h, 8:16], best[:, h, 8:16], f1[:, h])
                link(nc.vector.tensor_copy(gsum[:, 0], best[:, :, 0]))
                nc.vector.tensor_tensor(best[:], best[:], gsum[:, 0].unsqueeze(2).to_broadcast([P, PH, TOPK]),
                                        ALU.subtract).then_inc(gmax_ready, 1)
                nc.vector.tensor_scalar(pos[:, 1], pos[:, 0], 4, None, ALU.logical_shift_right)
                link(nc.vector.tensor_scalar(pos[:, 2], pos[:, 0], TOPK - 1, None, ALU.bitwise_and))
                link(nc.vector.tensor_copy(posf[:], pos[:, 1:3]))
                for p, cp in ((0, c1), (1, c2)):
                    ins = nc.vector.tensor_tensor(
                        cp.rearrange("p h a b -> p (h a) b"), posf[:, p].unsqueeze(2).to_broadcast([P, SLOTS, TOPK]),
                        iota16.unsqueeze(1).to_broadcast([P, SLOTS, TOPK]), ALU.is_equal)
                link(ins)
                for p, cp in ((0, c1), (1, c2)):
                    ins = nc.vector.tensor_tensor(cp, cp, halvesf[:, :, p].unsqueeze(2).to_broadcast(
                        [P, PH, TOPK, TOPK]), ALU.mult)
                link(ins)
                for p, cp in ((0, c1), (1, c2)):
                    nc.vector.tensor_reduce(slot[:, p], cp.rearrange("p h a b -> p (h a) b"), AX.X, ALU.add)
                dve.wait_ge(gexp_ready, tt + 1)
                link(nc.vector.tensor_reduce(gsum[:, 0], best[:], AX.X, ALU.add))
                link(nc.vector.reciprocal(gsum[:, 1], gsum[:, 0]))
                nc.vector.tensor_tensor(slot[:, 2].rearrange("p (h k) -> p h k", h=PH), best[:],
                                        gsum[:, 1].unsqueeze(2).to_broadcast([P, PH, TOPK]), ALU.mult
                                        ).then_inc(slot_ready, 1)
                dve.wait_ge(slotT_full, tt + 1)
                nc.vector.tensor_copy(slotT[:].rearrange("p a t -> p (a t)"), bank[SLOT_BANK][:, 0:3 * P]
                                      ).then_inc(slotT_done, 1)
                dve.wait_ge(slotT_done, tt + 1)
                if tt + 1 < NT:
                    take_scores(tt + 1)
                for half in range(2):
                    with dve.Fori(0, HALF // STEP) as i:
                        for qd in range(SQ):
                            dve.wait_ge(g_full, i * SQ + ((2 * tt + half) * (HALF // QUAD) + qd + 1))
                            o = (qd % OHR) * QUAD
                            ts = bass.ds(i * STEP + (half * HALF + qd * QUAD), QUAD)
                            nc.vector.tensor_tensor(ohB[:, o:o + QUAD], iota[:].unsqueeze(1).to_broadcast([P, QUAD, P]),
                                                    slotT[:, 1, ts].unsqueeze(2).to_broadcast([P, QUAD, P]),
                                                    ALU.is_equal)
                            for j in range(QUAD):
                                t = bass.ds(i * STEP + (half * HALF + qd * QUAD + j), 1)
                                ins = nc.vector.tensor_scalar(ohA[:, o + j], iota[:], slotT[:, 0, t],
                                                              slotT[:, 2, t], ALU.is_equal, ALU.mult)
                            ins.then_inc(onehot_ready, 1)
            dve.wait_ge(onehot_ready, S // QUAD)
            dve.sem_inc(routed, 1)

            for par in range(2):
                dve.wait_ge(spilled[par], SPILLED * 8)
            dve.wait_ge(s_full, NT * (HP // 4))
            link(nc.vector.memset(h2T[:], 0.0))
            dve.sem_inc(y_done, len(Y_BANKS))
            dve.wait_ge(g_full, S // QUAD + OHR)
            dve.wait_ge(map_stored, 64 * NT)

            def weigh(grp, k):
                dve.wait_ge(g_loaded[k // 2], grp * 16 + 16)
                nc.vector.tensor_tensor(av[:, k % 2].rearrange("p (c t) -> p c t", t=HALF),
                                        gel[:, k].rearrange("p (c t) -> p c t", t=HALF),
                                        gmap[:, k // 2, :, k % 2], ALU.mult).then_inc(av_ready, 1)

            def split_v(grp, k, which):
                hi_, lo_ = sets[which][0:2]
                dve.wait_ge(vhi_ready, grp * GROUP + (k + 1))
                nc.vector.tensor_tensor(lo_[:, k], vraw[:, k], hi_[:, k].bitcast(F32), ALU.subtract
                                        ).then_inc(vlo_ready, 1)

            def split_a(grp, k, which):
                hi_, lo_ = sets[which][2:4]
                dve.wait_ge(ahi_ready, grp * GROUP + (k + 1))
                nc.vector.tensor_tensor(lo_[:, k], av[:, k % 2], hi_[:, k].bitcast(F32), ALU.subtract
                                        ).then_inc(alo_ready, 1)

            def add_y(grp, blk):
                dve.wait_ge(y_full, grp * 8 + (blk + 2))
                a = acc[:, blk // 2, (blk % 2) * W:(blk % 2 + 1) * W]
                nc.vector.tensor_tensor(a, a, bank[Y_BANKS[blk % 4]][:], ALU.add).then_inc(y_done, 1)

            def fused(g, first):
                if not first:
                    for blk in range(4, 8):
                        add_y(g - 1, blk)
                for k in range(GROUP):
                    dve.wait_ge(up_done, g * GROUP + (N_UP0 + k + 1))
                    weigh(g, k)
                    split_v(g, k, 0)
                    split_a(g, k, 0)
                for blk in range(4):
                    add_y(g, blk)

            def second_only(g, grp, which, blocks):
                for k in range(GROUP):
                    dve.wait_ge(s_loaded[k], g * 16 + 16)
                    weigh(grp, k)
                    split_v(grp, k, which)
                    split_a(grp, k, which)
                    for blk in blocks[k]:
                        add_y(grp - 1, blk)

            fused(0, True)
            with dve.Fori(1, NF) as g:
                fused(g, False)
            second_only(0, NF, 1, [[4], [5], [6], [7]])
            second_only(1, NF + 1, 0, [[0, 1], [2, 3], [4, 5], [6, 7]])
            with dve.Fori(1, ND // 2) as i:
                second_only(i * 2, i * 2 + NF, 1, [[0, 1], [2, 3], [4, 5], [6, 7]])
                second_only(i * 2 + 1, i * 2 + (NF + 1), 0, [[0, 1], [2, 3], [4, 5], [6, 7]])
            for blk in range(8):
                add_y(NF + ND - 1, blk)
            dve.wait_ge(root_ready, 4)
            link(nc.vector.reciprocal(stat[:, 2], stat[:, 1]))
            for tt in range(NT):
                ins = nc.vector.scalar_tensor_tensor(acc[:, tt], acc[:, tt], stat[:, 2, tt:tt + 1], gate_f[:],
                                                     ALU.mult, ALU.mult)
            link(ins)
            for tt in range(NT):
                nc.vector.tensor_tensor(acc[:, tt], acc[:, tt], x[:, tt], ALU.add).then_inc(out_ready, 1)

        @block.tensor
        def _(pe):
            mm = nc.tensor.matmul

            def a_open(job):
                if a_job[job] >= 3:
                    pe.wait_ge(a_done, a_job[job] - 2)
                return a_bank(job)

            def d_open(job):
                if d_job[job] >= 3:
                    pe.wait_ge(d_done, d_job[job] - 2)
                return d_bank(job)

            chunk = [0]

            def weights():
                n = chunk[0]
                pe.wait_ge(w_loaded[n % 2], 16 * (n // 2 + 1))
                return wring[:, n % 2]

            def used(ins):
                ins.then_inc(w_used, 1)
                chunk[0] += 1

            def by_feature(w, b, m, src):
                for k in range(KD):
                    ins = mm(b[:], w[:, k, m * P:(m + 1) * P], src[:, k], start=k == 0, stop=k == KD - 1)
                return ins

            def by_token(w, b, tt, src):
                for k in range(KD):
                    ins = mm(b[:], src[:, k, tt * P:(tt + 1) * P], w[:, k], start=k == 0, stop=k == KD - 1)
                return ins

            def mod_columns(i):
                b = d_open(("mod", i))
                for ch in range(4):
                    w = weights()
                    for m in range(4):
                        for k in range(KD):
                            ins = mm(b[:, 4 * ch + m:4 * ch + m + 1], w[:, k, m * P:(m + 1) * P],
                                     cond[:, 1, k:k + 1], start=k == 0, stop=k == KD - 1)
                    if ch == 3:
                        ins.then_inc(d_full, 1)
                        pe.wait_ge(d_full, d_job["mod", i] + 1)
                        pe.sem_inc(w_used, 1)
                        chunk[0] += 1
                    else:
                        used(ins)

            def gate_rows(name):
                for half in range(2):
                    b = d_open((name, half))
                    w = weights()
                    for k in range(KD):
                        ins = mm(b[:], cond[:, 1, k:k + 1].to_broadcast([P, P]), w[:, k], start=k == 0, stop=k == KD - 1)
                    finish(ins, d_full, d_job[name, half] + 1)

            def finish(ins, full, n):
                ins.then_inc(full, 1)
                pe.wait_ge(full, n)
                pe.sem_inc(w_used, 1)
                chunk[0] += 1

            def transposes(b, src, n):
                for i in range(n):
                    ins = nc.tensor.transpose(b[:, i * P:(i + 1) * P], src(i), ident[:])
                return ins

            pe.wait_ge(small_loaded, SMALL)
            pe.wait_ge(cond_ready, 1)
            mod_columns(0)
            pe.wait_ge(xn_ready, NT)
            for k in range(KD):
                transposes(d_open(("xT", k)), lambda tt: cat[:, tt, k * P:(k + 1) * P], NT).then_inc(d_full, 1)
            pe.wait_ge(d_done, d_job["xT", KD - 1] + 1)
            w = weights()
            for tt in range(NT):
                ins = by_token(w, a_open(("f", tt)), tt, hT)
                if tt < NT - 1:
                    ins.then_inc(a_full, 1)
            finish(ins, a_full, a_job["f", NT - 1] + 1)
            w = weights()
            for h in range(HH):
                ins = by_feature(w, a_open(("hq", h)), h, hT)
                if h < HH - 1:
                    ins.then_inc(a_full, 1)
            finish(ins, a_full, a_job["hq", HH - 1] + 1)
            b = d_open(("ff",))
            for tt in range(NT):
                for k in range(KD):
                    ins = mm(b[:, tt * FH:(tt + 1) * FH], hT[:, k, tt * P:(tt + 1) * P], wff[:, k],
                             start=k == 0, stop=k == KD - 1)
            ins.then_inc(d_full, 1)
            pe.wait_ge(f_ready, 1)
            for h in range(HH):
                transposes(a_open(("hk", h)), lambda c: hk[:, c, h * HD:(h + 1) * HD], NT).then_inc(a_full, 1)
            w = weights()
            for tt in range(NT):
                ins = by_token(w, a_open(("hi", tt)), tt, hT)
                if tt < NT - 1:
                    ins.then_inc(a_full, 1)
            finish(ins, a_full, a_job["hi", NT - 1] + 1)
            pe.wait_ge(logf_ready, 1)
            for c in range(NT - 1):
                mm(a_open(("suffix", c))[:], tri[:, W:W + P], logf[:, c], start=True, stop=True).then_inc(a_full, 1)

            def output_of(h):
                b = a_open(("o", h))
                pe.wait_ge(d_done, d_job["level", h, LEVELS - 1] + 1)
                pe.wait_ge(st_ready, h + 1)
                pe.wait_ge(qa_ready, h + 1)
                for c in range(NT):
                    cs = slice(c * P, (c + 1) * P)
                    ins = mm(b[:, cs], sc[:, h % 2, cs], hi[:, c, h * HD:(h + 1) * HD], start=True, stop=c == 0)
                    if c:
                        ins = mm(b[:, cs], AT[:, 1, cs], st[:, h % 2, c - 1], start=False, stop=True)
                ins.then_inc(a_full, 1)

            for h in range(HH):
                hs = slice(h * HD, (h + 1) * HD)
                b = a_open(("A", h))
                for c in range(NT):
                    ins = mm(b[:, c * P:(c + 1) * P], logf[:, c, hs], tri[:, 0:P], start=True, stop=True)
                ins.then_inc(a_full, 1)
                b = d_open(("kv", h))
                pe.wait_ge(kd_ready, NT - 1)
                pe.wait_ge(a_done, a_job["hi", NT - 1] + 1)
                for c in range(NT - 1):
                    ins = mm(b[:, c * HD:(c + 1) * HD], hk[:, c, hs], hi[:, c, hs], start=True, stop=True)
                ins.then_inc(d_full, 1)
                w = weights()
                for j in range(NT):
                    b = a_open(("side", h, j))
                    ins = by_feature(w, b, j, hT) if h < 2 else by_token(w, b, j, hT)
                    if j < NT - 1:
                        ins.then_inc(a_full, 1)
                    else:
                        finish(ins, a_full, a_job["side", h, j] + 1)
                    if j == 1 and h:
                        output_of(h - 1)
                    for lev in (2 * j, 2 * j + 1):
                        b = d_open(("level", h, lev))
                        n = h * n_lev + lev - 1
                        if lev:
                            pe.wait_ge(qe_ready, n + 1)
                            pe.wait_ge(ke_ready, n + 1)
                        for c in range(NT):
                            cs = slice(c * P, (c + 1) * P)
                            ins = mm(b[:, cs], ke[:, n % 2, cs] if lev else hkT[:, h, cs],
                                     qe[:, n % 2, cs] if lev else hqT[:, h, cs], start=True, stop=True)
                        ins.then_inc(d_full, 1)
            output_of(HH - 1)
            gate_rows("gate_a")
            pe.wait_ge(lff_ready, 1)
            b = a_open(("fcol",))
            for tt in range(NT):
                for c in range(tt + 1):
                    ins = mm(b[:, tt * FH:(tt + 1) * FH], tri[:, 0:P] if c == tt else tri[:, P:2 * P], ff[:, 0, c],
                             start=c == 0, stop=c == tt)
            ins.then_inc(a_full, 1)
            for h in range(FH):
                b = a_open(("nF", h))
                for c in range(NT):
                    ins = mm(b[:, c * P:W], ff[:, 0, c, h:h + 1].to_broadcast([P, P]), tri[:, 0:W - c * P],
                             start=c == 0, stop=c == NT - 1)
                ins.then_inc(a_full, 1)

            def logits(n):
                tt, h = divmod(n, FH)
                ps = slice(FD * (h % 2), FD * (h % 2) + FD)
                mm(d_open(("logits", n))[:, 0:(tt + 1) * P], fqT[ps, h // 2, tt * P:(tt + 1) * P],
                   fkT[ps, h // 2, 0:(tt + 1) * P], start=True, stop=True).then_inc(d_full, 1)

            def values(n):
                tt, h = divmod(n, FH)
                pe.wait_ge(a_done, a_job["pT", n] + 1)
                if tt >= 2 and h == 0:
                    pe.wait_ge(fcat_ready, tt - 1)
                o = bank[O_BANKS[tt % 2]]
                for c in range(tt + 1):
                    ins = mm(o[:, h * FD:(h + 1) * FD], prT[:, n % FR, c * P:(c + 1) * P],
                             fv[:, c, h * FD:(h + 1) * FD], start=c == 0, stop=c == tt)
                ins.then_inc(pv_done, 1)

            for n in range(3):
                logits(n)
            for n in range(N_FOX):
                pe.wait_ge(pr_ready, n + 1)
                transposes(a_open(("pT", n)), lambda c: pr[:, n % FR, c * P:(c + 1) * P], n // FH + 1
                           ).then_inc(a_full, 1)
                if n + 3 < N_FOX:
                    logits(n + 3)
                if n:
                    values(n - 1)
            values(N_FOX - 1)
            pe.wait_ge(fcat_ready, NT)
            pe.wait_ge(hcat_ready, 1)
            for k in range(KD):
                transposes(a_open(("catT", k)), lambda tt: cat[:, tt, k * P:(k + 1) * P], NT).then_inc(a_full, 1)
            pe.wait_ge(a_done, a_job["catT", KD - 1] + 1)
            for half in range(2):
                w = weights()
                for tt in range(NT):
                    ins = by_token(w, a_open(("mix", half, tt)), tt, hT)
                    if tt < NT - 1:
                        ins.then_inc(a_full, 1)
                finish(ins, a_full, a_job["mix", half, NT - 1] + 1)
            mod_columns(1)
            gate_rows("gate_f")
            pe.wait_ge(xn_ready, 2 * NT)
            for k in range(KD):
                transposes(d_open(("h2T", k)), lambda tt: cat[:, tt, k * P:(k + 1) * P], NT).then_inc(d_full, 1)
            pe.wait_ge(hlo_ready, KD)

            def up(n, par):
                pe.wait_ge(ulo_ready, n + 1)
                if not isinstance(n, int) or n >= 2:
                    pe.wait_ge(up_done, n - 1)
                b = bank[UP_BANKS[par]]
                for c in range(KD):
                    mm(b[:], uhi[:, par, c], hhi[:, c], start=c == 0, stop=False)
                    mm(b[:], uhi[:, par, c], hlo[:, c], start=False, stop=False)
                    ins = mm(b[:], ulo[:, par, c], hhi[:, c], start=False, stop=c == KD - 1)
                ins.then_inc(up_full, 1)

            def square_sums(n):
                pe.wait_ge(qsq_ready, n + 1)
                for tt in range(NT):
                    ins = mm(bank[6][:, tt * HP + n:tt * HP + n + 1], qsq[:, n % 2, tt * P:(tt + 1) * P], ones[:],
                             start=True, stop=True)
                ins.then_inc(qss_done, 1)

            for n in range(HP):
                up(n, n % 2)
                if n:
                    square_sums(n - 1)
            square_sums(HP - 1)

            def scores(tt):
                if tt:
                    pe.wait_ge(slotT_done, tt)
                for q4 in range(HP // 4):
                    done = tt * (HP // 4) + q4 - 1
                    if done > 0:
                        pe.wait_ge(s_done, done)
                    for n in range(4 * q4, 4 * q4 + 4):
                        ins = mm(bank[SCORE_BANKS[q4 % 2]][:, (n % 4) * NK:(n % 4 + 1) * NK],
                                 qT[:, n, tt * P:(tt + 1) * P], keys[:, n], start=True, stop=True)
                    ins.then_inc(s_full, 1)

            pe.wait_ge(keys_loaded, 16)
            scores(0)
            pe.sem_inc(g_full, OHR)
            for what, *at in plan:
                if what == "up":
                    n0, count = at
                    with pe.Fori(0, count // 2) as i:
                        for par in range(2):
                            up(i * 2 + (n0 + par), par)
                elif what == "slots":
                    tt, = at
                    pe.wait_ge(slot_ready, tt + 1)
                    transposes(bank[SLOT_BANK], lambda a: slot[:, a], 3).then_inc(slotT_full, 1)
                    if tt + 1 < NT:
                        scores(tt + 1)
                elif what == "maps":
                    tt, half, n0 = at
                    with pe.Fori(0, HALF // STEP) as i:
                        for qd in range(SQ):
                            idx = i * SQ + ((2 * tt + half) * (HALF // QUAD) + qd)
                            pe.wait_ge(onehot_ready, idx + 1)
                            pe.wait_ge(g_done, idx + 1)
                            for j in range(QUAD):
                                o = (qd % OHR) * QUAD + j
                                ins = mm(bank[G_BANKS[qd % 4]][:, j * NK:(j + 1) * NK], ohB[:, o], ohA[:, o],
                                         start=True, stop=True)
                            ins.then_inc(g_full, 1)
                            if qd % (SQ // 2) == SQ // 2 - 1:
                                par = qd // (SQ // 2)
                                up(i * 2 + (n0 + par), par)

            pe.sem_inc(y_full, 1)

            def down(b, blk, k, which):
                vhi, vlo, ahi, alo = sets[which]
                ts = slice(blk // 2 * P, (blk // 2 + 1) * P)
                ds = slice(blk % 2 * W, (blk % 2 + 1) * W)
                mm(b[:], ahi[:, k, ts], vhi[:, k, ds], start=k == 0, stop=False)
                mm(b[:], ahi[:, k, ts], vlo[:, k, ds], start=False, stop=False)
                return mm(b[:], alo[:, k, ts], vhi[:, k, ds], start=False, stop=k == GROUP - 1)

            def second(grp, which):
                pe.wait_ge(vlo_ready, grp * GROUP + (GROUP - 1))
                pe.wait_ge(alo_ready, grp * GROUP + (GROUP - 1))
                for blk in range(2):
                    pe.wait_ge(y_done, grp * 8 + (blk + 1))
                    for k in range(GROUP - 1):
                        down(bank[Y_BANKS[blk]], blk, k, which)
                pe.wait_ge(vlo_ready, grp * GROUP + GROUP)
                pe.wait_ge(alo_ready, grp * GROUP + GROUP)
                for blk in range(2):
                    down(bank[Y_BANKS[blk]], blk, GROUP - 1, which).then_inc(y_full, 1)
                for blk in range(2, 8):
                    pe.wait_ge(y_done, grp * 8 + (blk + 1))
                    for k in range(GROUP):
                        ins = down(bank[Y_BANKS[blk % 4]], blk, k, which)
                    ins.then_inc(y_full, 1)

            with pe.Fori(0, NF) as g:
                for k in range(GROUP):
                    up(g * GROUP + (N_UP0 + k), k % 2)
                second(g, 0)
            with pe.Fori(0, ND // 2) as i:
                second(i * 2 + NF, 1)
                second(i * 2 + (NF + 1), 0)


def kernel(x, c, w_ada, b_ada, pre_mix_g, post_mix_g, w_in, b_fox_f, hgrn_gamma, hgrn_norm_g, w_out,
           pre_ffn_g, post_ffn_g, peer_w_q, peer_sub_keys, peer_u, peer_v):
    import concourse.bacc as _bacc
    import numpy as np
    from concourse.bass_utils import run_bass_kernel_spmd as _run

    D = x.shape[-1]
    S = x.shape[1]
    n_keys = peer_sub_keys.shape[3]

    def arr(a):
        return np.ascontiguousarray(np.asarray(a))

    def columns(v):
        return arr(np.asarray(v).reshape(-1, P).T)

    s = np.arange(P)
    const_f = np.concatenate([
        np.eye(P), (s[:, None] <= s[None, :]), np.ones((P, 3 * P)), (s[:, None] > s[None, :]),
        np.broadcast_to(s[None, :], (P, P))], axis=1).astype(np.float32)
    masks = [s[:, None] == s[None, :]]
    for lev in range(1, 8):
        half = 1 << (lev - 1)
        same = s[:, None] // (2 * half) == s[None, :] // (2 * half)
        masks.append(same & (s[:, None] % (2 * half) < half) & (s[None, :] % (2 * half) >= half))
    const_m = arr(np.stack(masks, axis=1).astype(np.int32))

    b = np.asarray(b_ada)[0].reshape(6, D)
    width = hgrn_gamma.shape[1]
    fox = np.concatenate([np.asarray(b_fox_f)[0], np.zeros(width - b_fox_f.shape[1], np.float32)])
    arrays = {
        "x_in": arr(np.asarray(x)[0]),
        "c_col": columns(np.asarray(c)[0]),
        "w_ada": arr(np.asarray(w_ada)[0]),
        "b_ada_col": columns(np.asarray(b_ada)[0]),
        "gains_col": arr(np.stack([columns(np.asarray(pre_mix_g)[0]), columns(np.asarray(pre_ffn_g)[0])], axis=1)),
        "rows": arr(np.stack([b[2], b[5], np.asarray(post_mix_g)[0], np.asarray(post_ffn_g)[0]])),
        "w_in": arr(np.asarray(w_in)[0]),
        "hgrn_rows": arr(np.concatenate([np.asarray(hgrn_gamma), np.asarray(hgrn_norm_g), fox[None]])),
        "w_out": arr(np.asarray(w_out)[0]),
        "w_q": arr(np.asarray(peer_w_q)[0].reshape(D // P, P, -1, P).transpose(2, 1, 0, 3)),
        "keys_t": arr(np.asarray(peer_sub_keys)[0].reshape(-1, n_keys, P).transpose(2, 0, 1)),
        "u_t": arr(np.asarray(peer_u)[0].reshape(n_keys, n_keys, D // P, P).transpose(0, 3, 2, 1)),
        "v_in": arr(np.asarray(peer_v)[0]),
        "const_f": const_f,
        "const_m": const_m,
    }
    nc = _bacc.Bacc("TRN2", target_bir_lowering=False, num_devices=1)
    args = [nc.dram_tensor(n, a.shape, mybir.dt.from_np(a.dtype), kind="ExternalInput").ap()
            for n, a in arrays.items()]
    gate_map = nc.dram_tensor("gate_map", (8, P, n_keys, S // 8), F32, kind="Internal").ap()
    gelus = nc.dram_tensor("gelus", (n_keys, P, S), F32, kind="Internal").ap()
    out = nc.dram_tensor("y_out", (S, D), F32, kind="ExternalOutput").ap()
    hybrid_block(nc, *args, gate_map, gelus, out)
    r = _run(nc, [arrays], core_ids=[0])
    return r.results[0]["y_out"].reshape(1, S, D)
```

```python
from contextlib import ExitStack

import concourse.bass as bass
from concourse import mybir

P = 128
F32 = mybir.dt.float32
F32R = mybir.dt.float32r
I32 = mybir.dt.int32
U32 = mybir.dt.uint32
ALU = mybir.AluOpType
ACT = mybir.ActivationFunctionType
AX = mybir.AxisListType
MASKED = -3.0e38


def hybrid_block(nc, x_in, c_col, w_ada, b_ada_col, gains_col, rows, w_in, hgrn_rows, w_out,
                 w_q, keys_t, u_t, v_in, const_f, const_m, gate_map, gelus, out):
    S, D = x_in.shape
    NT = S // P
    KD = D // P
    W = 512
    FH, FD = 8, 64
    HH, HD = 4, 128
    PH, TOPK, NK = 8, 16, 128
    HP = 2 * PH
    SLOTS = PH * TOPK
    LEVELS = 8
    EPS = 1e-6
    GROUP = 4
    QUAD = 4
    HALF = P // 2
    STEP = 2 * 4 * QUAD
    SQ = STEP // QUAD
    OHR = 4
    FR = 4

    plan, n = [("up", HP, 8)], HP + 8
    for tt in range(NT):
        for item, count in (("exp", 2), ("slots", 2)):
            plan += [(item, tt), ("up", n, count)]
            n += count
        for half in range(2):
            plan.append(("maps", tt, half, n))
            n += 2 * (HALF // STEP)
            ups = 4 if half == 0 else 8 if tt < NT - 1 else 0
            first = int((tt, half) == (NT - 1, 1))
            for part, count in ((first, min(ups, 2)), (1 - first, max(ups - 2, 0))):
                plan.append(("store", 2 * tt + half, part))
                if count:
                    plan.append(("up", n, count))
                    n += count
    N_UP0 = n
    SPILLED = n - HP
    NF = (NK - SPILLED) // GROUP
    ND = SPILLED // GROUP
    assert SPILLED % GROUP == 0 and ND % 2 == 0 and NF >= 2

    with ExitStack() as ctx:
        def sem(name):
            return ctx.enter_context(nc.semaphore(name))

        def sb(name, shape, dt=F32, where=ctx):
            return where.enter_context(nc.sbuf_tensor(name, shape, dt))

        bank = [ctx.enter_context(nc.psum_tensor(f"bank{i}", [P, W], F32)) for i in range(8)]

        x = sb("x", [P, NT, D])
        h2T = sb("h2T", [P, KD, S])
        hT = h2T
        gate_f = sb("gate_f", [P, D])
        ident = sb("ident", [P, P])
        iota = sb("iota", [P, P])
        eps = sb("eps", [P, 1])
        stat = sb("stat", [P, 2, 3, NT])
        ones = sb("ones", [P, P])

        mx = ExitStack()
        fv = sb("fv", [P, NT, 512], where=mx)
        hqk = sb("hqk", [P, 2 * HH, S], where=mx)
        hqT, hkT = hqk[:, 0:HH], hqk[:, HH:2 * HH]
        nFb = hqk
        hi = sb("hi", [P, NT, 512], where=mx)
        hg = sb("hg", [P, NT, 512], where=mx)
        logf = sb("logf", [P, NT, 512], where=mx)
        hk = sb("hk", [P, NT, 512], where=mx)
        wring = sb("wring", [P, 2, KD, W], where=mx)
        cat = sb("cat", [P, NT, D], where=mx)
        fqk = sb("fqk", [P, 2, 4, S], where=mx)
        fqT, fkT = fqk[:, 0], fqk[:, 1]
        mix = fqk[:, :, :, :].rearrange("p a b c -> p (a b c)").rearrange("p (t d) -> p t d", t=NT)
        gate_a = sb("gate_a", [P, D], where=mx)
        post_a = sb("post_a", [P, D], where=mx)
        post_f = sb("post_f", [P, D], where=mx)
        cond = sb("cond", [P, 2, KD], where=mx)
        wff = sb("wff", [P, KD, FH], where=mx)
        bada = sb("bada", [P, 48], where=mx)
        gains = sb("gains", [P, 2, KD], where=mx)
        shift = sb("shift", [P, 2, KD], where=mx)
        scale = sb("scale", [P, 2, KD], where=mx)
        gam = sb("gam", [P, 2, 512], where=mx)
        gmx = sb("gmx", [P, 512], where=mx)
        hng = sb("hng", [P, 512], where=mx)
        modt = sb("modt", [P, 2 * KD], where=mx)
        tri = sb("tri", [P, W + P], where=mx)
        lmask = sb("lmask", [P, LEVELS, P], I32, where=mx)
        ff = sb("ff", [P, 4, NT, FH], where=mx)
        fcol = sb("fcol", [P, NT, FH], where=mx)
        bfox = sb("bfox", [P, FH], where=mx)
        hss = sb("hss", [P, 2, NT, HH], where=mx)
        ada = [hqk[:], fqk[:, :, :, :].rearrange("p a b s -> p (a b) s"), h2T[:], wring[:, 0]]
        part0 = fv
        hx = ExitStack()
        AT = sb("AT", [P, 2, S], where=hx)
        dec = gam
        qe = sb("qe", [P, 2, S], where=hx)
        ke = sb("ke", [P, 2, S], where=hx)
        sc = sb("sc", [P, 2, S], where=hx)
        st = sb("st", [P, 2, 3, HD], where=hx)
        alast = sb("alast", [P, 2, NT], where=hx)
        hsq = gmx
        hx.close()
        fx = ExitStack()
        lg = sb("lg", [P, FR, S], where=fx)
        pr = sb("pr", [P, FR, S], where=fx)
        prT = logf
        rmax = sb("rmax", [P, NT, FH], where=fx)
        rsum = sb("rsum", [P, 2, NT, FH], where=fx)
        fx.close()
        mx.close()

        up_mem = ExitStack()
        hhi = sb("hhi", [P, KD, S], F32R, where=up_mem)
        hlo = sb("hlo", [P, KD, S], F32R, where=up_mem)
        uraw = sb("uraw", [P, 2, KD, P], where=up_mem)
        uhi = sb("uhi", [P, 2, KD, P], F32R, where=up_mem)
        ulo = sb("ulo", [P, 2, KD, P], F32R, where=up_mem)

        rt = ExitStack()
        stage = sb("stage", [P, NK, HALF], where=rt)
        qsq = stage[:, :, :].rearrange("p i t -> p (i t)").rearrange("p (n s) -> p n s", s=S)[:, 0:2]
        qT = sb("qT", [P, HP, S], where=rt)
        s1 = sb("s1", [P, HP, NK], where=rt)
        s2 = sb("s2", [P, HP, NK], where=rt)
        s3 = sb("s3", [P, HP, NK], where=rt)
        ohA = sb("ohA", [P, OHR * QUAD, NK], where=rt)
        ohB = sb("ohB", [P, OHR * QUAD, NK], where=rt)
        top = sb("top", [P, HP, TOPK], where=rt)
        topi = sb("topi", [P, HP, TOPK], U32, where=rt)
        topf = sb("topf", [P, HP, TOPK], where=rt)
        iota16 = iota[:, 0:TOPK]
        best = sb("best", [P, PH, TOPK], where=rt)
        pos = sb("pos", [P, 3, SLOTS], U32, where=rt)
        posf = sb("posf", [P, 2, SLOTS], where=rt)
        slot = sb("slot", [P, 3, SLOTS], where=rt)
        slotT = sb("slotT", [P, 3, P], where=rt)
        gsum = sb("gsum", [P, 2, PH], where=rt)
        rq = sb("rq", [P, 2, NT, HP], where=rt)
        rt.close()
        keys = h2T[:, 0:4, :].rearrange("p a (b k) -> p (a b) k", k=NK)
        spill = h2T[:, 4:6]

        ex = ExitStack()
        ahi0 = sb("ahi0", [P, GROUP, S], F32R, where=ex)
        alo0 = sb("alo0", [P, GROUP, S], F32R, where=ex)
        gmap = sb("gmap", [P, GROUP // 2, S // HALF, 2, HALF], where=ex)
        av = sb("av", [P, 4, S], where=ex)
        vraw = sb("vraw", [P, GROUP, D], where=ex)
        vhi0 = sb("vhi0", [P, GROUP, D], F32R, where=ex)
        vlo0 = sb("vlo0", [P, GROUP, D], F32R, where=ex)
        gel = sb("gel", [P, GROUP, S], where=ex)
        sets = [[vhi0, vlo0, ahi0, alo0]]
        ex.close()
        up_mem.close()
        sets.append([sb("vhi1", [P, GROUP, D], F32R, where=up_mem), sb("vlo1", [P, GROUP, D], F32R, where=up_mem),
                     sb("ahi1", [P, GROUP, S], F32R, where=up_mem), sb("alo1", [P, GROUP, S], F32R, where=up_mem)])
        up_mem.close()
        acc = h2T[:, :, :].rearrange("p a b -> p (a b)").rearrange("p (t d) -> p t d", t=NT)
        n_lev = LEVELS - 1
        sqs = cat

        def number(jobs):
            return {job: n for n, job in enumerate(jobs)}

        a_jobs, d_jobs = [], []
        a_jobs += [("xT", k) for k in range(1, KD, 2)]
        a_jobs += [("f", tt) for tt in range(NT)] + [("hq", h) for h in range(HH)]
        a_jobs += [("hk", h) for h in range(HH)] + [("hi", tt) for tt in range(NT)]
        a_jobs += [("suffix", c) for c in range(NT - 1)]
        for h in range(HH):
            a_jobs += [("A", h), ("side", h, 0), ("side", h, 1)]
            a_jobs += [("o", h - 1)] if h else []
            a_jobs += [("side", h, 2), ("side", h, 3)]
        a_jobs += [("o", HH - 1), ("fcol",)] + [("nF", h) for h in range(FH)]
        extras = [("gate_a", 0), ("gate_a", 1), ("mod", 1, 0), ("mod", 1, 1), ("mod", 1, 2), ("mod", 1, 3),
                  ("gate_f", 0), ("gate_f", 1)]
        ACT_PARTS = 5
        ACT_SCALES, POOL_SUMS = ((0, 1), (2, 3), (4,)), ((1,), (2, 3), (4,))
        extra_at = [3 * e + 5 for e in range(len(extras))]
        assert extra_at[-1] < NT * FH
        for n in range(NT * FH):
            a_jobs += [("pT", n)]
            if n > FH and n % FH == 5:
                a_jobs += [("catT", n // FH - 1, j) for j in range(2)]
        a_jobs += [("catT", NT - 1, j) for j in range(2)]
        a_jobs += [("mix", tt, half) for tt in range(NT) for half in range(2)]
        d_jobs += [("mod",)] + [("xT", k) for k in range(0, KD, 2)] + [("ff",)]
        for h in range(HH):
            d_jobs += [("kv", h)] + [("level", h, lev) for lev in range(LEVELS)]
        d_jobs += [("logits", n) for n in range(NT * FH)]
        d_jobs += [("h2T", tt, j) for tt in range(NT) for j in range(2)]
        a_job, d_job = number(a_jobs), number(d_jobs)
        A_BANKS, D_BANKS, O_BANK, X_BANK = [0, 1, 2], [3, 4, 5], 6, 7
        SCORE_BANKS, SLOT_BANK, G_BANKS = [4, 5], 4, [2, 3, 6, 7]
        UP_BANKS, Y_BANKS = [0, 1], [2, 3, 4, 5]

        def a_bank(job):
            return bank[A_BANKS[a_job[job] % 3]]

        def d_bank(job):
            return bank[D_BANKS[d_job[job] % 3]]

        w_loaded = [sem(f"w_loaded{i}") for i in range(2)]
        w_used = sem("w_used")
        c_loaded = sem("c_loaded")
        early_loaded = sem("early_loaded")
        late_loaded = sem("late_loaded")
        x_loaded = sem("x_loaded")
        keys_loaded = sem("keys_loaded")
        made = sem("made")
        cond_ready = sem("cond_ready")
        a_full = sem("a_full")
        a_done = sem("a_done")
        d_full = sem("d_full")
        d_done = sem("d_done")
        ada_loaded = [sem(f"ada_loaded{i}") for i in range(3)]
        part_ready = sem("part_ready")
        mod_ready = sem("mod_ready")
        scaled_ready = sem("scaled_ready")
        part2_ready = sem("part2_ready")
        part3_ready = sem("part3_ready")
        x_full = sem("x_full")
        x_done = sem("x_done")
        dve_chain = sem("dve_chain")
        act_chain = sem("act_chain")
        sumsq_ready = sem("sumsq_ready")
        root_ready = sem("root_ready")
        xn_ready = sem("xn_ready")
        h2T_ready = sem("h2T_ready")
        f_ready = sem("f_ready")
        logf_ready = sem("logf_ready")
        fz_ready = sem("fz_ready")
        fsoft_ready = sem("fsoft_ready")
        lff_ready = sem("lff_ready")
        kd_ready = sem("kd_ready")
        gam_ready = sem("gam_ready")
        game_ready = sem("game_ready")
        diff_ready = sem("diff_ready")
        dec_ready = sem("dec_ready")
        qe_ready = sem("qe_ready")
        ke_ready = sem("ke_ready")
        alast_ready = sem("alast_ready")
        expA_ready = sem("expA_ready")
        qa_ready = sem("qa_ready")
        st_ready = sem("st_ready")
        hsq_ready = sem("hsq_ready")
        hsum_ready = sem("hsum_ready")
        hroot_ready = sem("hroot_ready")
        hcat_ready = sem("hcat_ready")
        mask_ready = sem("mask_ready")
        rmax_ready = sem("rmax_ready")
        pr_ready = sem("pr_ready")
        pv_done = sem("pv_done")
        fcat_ready = sem("fcat_ready")
        xmix_ready = sem("xmix_ready")
        qsq_ready = sem("qsq_ready")
        qss_done = sem("qss_done")
        qroot_ready = sem("qroot_ready")
        s_full = sem("s_full")
        s_done = sem("s_done")
        gmax_ready = sem("gmax_ready")
        gexp_ready = sem("gexp_ready")
        slot_ready = sem("slot_ready")
        slotT_full = sem("slotT_full")
        slotT_done = sem("slotT_done")
        onehot_ready = sem("onehot_ready")
        g_full = sem("g_full")
        g_done = sem("g_done")
        map_stored = sem("map_stored")
        last_stored = [sem(f"last_stored{i}") for i in range(2)]
        routed = sem("routed")
        hhi_ready = sem("hhi_ready")
        hlo_ready = sem("hlo_ready")
        u_loaded = [sem(f"u_loaded{i}") for i in range(2)]
        v_loaded = [sem(f"v_loaded{i}") for i in range(GROUP)]
        g_loaded = [sem(f"g_loaded{i}") for i in range(GROUP // 2)]
        s_loaded = [sem(f"s_loaded{i}") for i in range(GROUP)]
        spilled = [sem(f"spilled{i}") for i in range(2)]
        uhi_ready = sem("uhi_ready")
        ulo_ready = sem("ulo_ready")
        vhi_ready = sem("vhi_ready")
        vlo_ready = sem("vlo_ready")
        up_full = sem("up_full")
        up_done = sem("up_done")
        av_ready = sem("av_ready")
        ahi_ready = sem("ahi_ready")
        alo_ready = sem("alo_ready")
        y_full = sem("y_full")
        y_done = sem("y_done")
        out_ready = sem("out_ready")
        stored = sem("stored")

        FF = 3 * FH * FD
        HQ, HF, HI, HG = [FF + FH + i * 512 for i in range(4)]
        chunks = [(w_ada, 3 * W)]
        chunks += [(w_in, n) for n in (HF, HQ, HI, 0, 512, 1024, HG)]
        chunks += [(w_ada, n * W) for n in (4, 5, 6, 7, 8, 9, 10, 11)]
        chunks += [(w_out, 0), (w_out, W)]
        early = [(bada[:], b_ada_col), (gains[:], gains_col), (ident[:], const_f[:, 0:P]),
                 (gam[:, 0], hgrn_rows[0].partition_broadcast(P)),
                 (gam[:, 1], hgrn_rows[1].partition_broadcast(P))]
        late = [(wff[:], w_in[:, FF:FF + FH].rearrange("(k p) n -> p k n", p=P)),
                (bfox[:], hgrn_rows[3, 0:FH].partition_broadcast(P)),
                (tri[:], const_f[:, P:2 * P + W]), (lmask[:], const_m),
                (hng[:], hgrn_rows[2].partition_broadcast(P)),
                (gate_a[:], rows[0].partition_broadcast(P)), (post_a[:], rows[2].partition_broadcast(P)),
                (gate_f[:], rows[1].partition_broadcast(P)), (post_f[:], rows[3].partition_broadcast(P)),
                (iota[:], const_f[:, 2 * P + W:3 * P + W])]
        N_FOX = NT * FH
        AFTER_W_IN = 8
        part2 = [gam[:, 0], gam[:, 1]]
        part3 = [gmx[:], hng[:]]

        block = ctx.enter_context(nc.Block())

        @block.sync
        def _(sp):
            sp.dma_start(cond[:, 0], c_col).then_inc(c_loaded, 16)
            for n in range(3):
                sp.dma_start(ada[n], w_ada[:, n * W:(n + 1) * W].rearrange("(k p) n -> p k n", p=P)
                             ).then_inc(ada_loaded[n], 16)
                if n == 0:
                    for tt in range(NT):
                        sp.dma_start(x[:, tt, :], x_in[tt * P:(tt + 1) * P, :]).then_inc(x_loaded, 16)
                sp.wait_ge(ada_loaded[n] if n else x_loaded, 16 if n else 16 * NT)
            for n, (w, c0) in enumerate(chunks):
                if n >= 2:
                    sp.wait_ge(w_used, n - 1)
                sp.dma_start(wring[:, n % 2], w[:, c0:c0 + W].rearrange("(k p) n -> p k n", p=P)
                             ).then_inc(w_loaded[n % 2], 16)
            sp.wait_ge(fcat_ready, NT)
            for n in range(HP):
                if n >= 2:
                    sp.wait_ge(ulo_ready, n - 1)
                sp.dma_start(uraw[:, n % 2], w_q[n]).then_inc(u_loaded[n % 2], 16)
                if n == HP - 1:
                    sp.wait_ge(hlo_ready, 2 * NT)
                    sp.dma_start(keys, keys_t).then_inc(keys_loaded, 16)

            def load_u(n, par):
                sp.wait_ge(ulo_ready, n - 1)
                sp.dma_start(uraw[:, par], u_t[bass.ds(n - HP, 1)].rearrange("a p c e -> p (a c) e")
                             ).then_inc(u_loaded[par], 16)

            def store_gelu(n, par):
                sp.wait_ge(up_done, n + 1)
                sp.dma_start(gelus[bass.ds(n - HP, 1)].rearrange("a e t -> e (a t)"), spill[:, par]
                             ).then_inc(spilled[par], 16)

            for n in range(HP, HP + 4):
                load_u(n, n % 2)
            for what, *at in plan:
                if what == "up":
                    n0, count = at
                    with sp.Fori(0, count // 2) as i:
                        for par in range(2):
                            store_gelu(i * 2 + (n0 + par), par)
                            load_u(i * 2 + (n0 + par + 4), par)
                elif what == "maps":
                    tt, half, n0 = at
                    if (tt, half) == (NT - 1, 1):
                        sp.wait_ge(s_full, NT * (HP // 4))
                        for k in range(GROUP):
                            sp.dma_start(vraw[:, k], v_in[(SPILLED + k) * P:(SPILLED + k + 1) * P, :]
                                         ).then_inc(v_loaded[k], 16)
                    with sp.Fori(0, HALF // STEP) as i:
                        for par in range(2):
                            store_gelu(i * 2 + (n0 + par), par)
                            load_u(i * 2 + (n0 + par + 4), par)
                elif what == "store":
                    c, part = at
                    sp.wait_ge(g_done, (c + 1) * (HALF // QUAD) + len(G_BANKS))
                    tiles = slice(part * NK // 2, (part + 1) * NK // 2)
                    signal = last_stored[part] if c == 2 * NT - 1 else map_stored
                    sp.dma_start(gate_map[c, :, tiles], stage[:, tiles]).then_inc(signal, 16)

            def load_map(tile, pair):
                sp.dma_start(gmap[:, pair].rearrange("p c i t -> p c (i t)"),
                             gate_map[:, :, bass.ds(tile, 2)].rearrange("c j i t -> j c (i t)")
                             ).then_inc(g_loaded[pair], 16)

            def load_v(tile, grp, k):
                sp.wait_ge(vlo_ready, (grp - 1) * GROUP + (k + 1))
                sp.dma_start(vraw[:, k], v_in[bass.ds(tile * P, P), :]).then_inc(v_loaded[k], 16)
                if k % 2:
                    sp.wait_ge(av_ready, (grp - 1) * GROUP + (k + 1))
                    load_map(tile - 1, k // 2)

            load_u(N_UP0 + 4, 0)
            load_u(N_UP0 + 5, 1)
            sp.wait_ge(map_stored, 32 * (2 * NT - 1))
            sp.wait_ge(last_stored[1], 16)
            for pair in range(GROUP // 2):
                load_map(SPILLED + 2 * pair, pair)
            load_u(N_UP0 + 6, 0)
            load_u(N_UP0 + 7, 1)
            for k in range(GROUP):
                load_v(GROUP + SPILLED + k, 1, k)
            with sp.Fori(2, NF) as g:
                for k in range(GROUP):
                    load_u((g - 1) * GROUP + (N_UP0 + k + 4), k % 2)
                    load_v(g * GROUP + (SPILLED + k), g, k)
            sp.wait_ge(last_stored[0], 16)
            with sp.Fori(0, ND) as g:
                for k in range(GROUP):
                    load_v(g * GROUP + k, g + NF, k)
                    sp.wait_ge(av_ready, (g + (NF - 1)) * GROUP + (k + 1))
                    sp.dma_start(gel[:, k], gelus[bass.ds(g * GROUP + k, 1)].rearrange("a e t -> e (a t)")
                                 ).then_inc(s_loaded[k], 16)
            for tt in range(NT):
                sp.wait_ge(out_ready, tt + 1)
                sp.dma_start(out[tt * P:(tt + 1) * P, :], acc[:, tt, :]).then_inc(stored, 16)
            sp.wait_ge(stored, 16 * NT)

        @block.gpsimd
        def _(pool):
            for dst, src in early:
                pool.dma_start(dst, src).then_inc(early_loaded, 16)
            pool.wait_ge(ada_loaded[2], 16)
            for dst, src in late:
                pool.dma_start(dst, src).then_inc(late_loaded, 16)
            pool.wait_ge(a_done, a_job["hk", HH - 1] + 1)
            for h in range(HH):
                for lev in range(1, LEVELS):
                    n = h * n_lev + lev - 1
                    pool.wait_ge(dec_ready, n + 1)
                    if n >= 2:
                        h2, l2 = divmod(n - 2, n_lev)
                        pool.wait_ge(d_full, d_job["level", h2, l2 + 1] + 1)
                    nc.gpsimd.tensor_tensor(ke[:, n % 2], hkT[:, h], dec[:, n % 2], ALU.mult
                                            ).then_inc(ke_ready, 1)
            def mask(n):
                tt = n // FH
                pool.wait_ge(d_done, d_job["logits", n] + 1)
                blk = lg[:, n % FR, tt * P:(tt + 1) * P]
                nc.gpsimd.affine_select(out=blk, in_=blk, compare_op=ALU.is_ge, fill=MASKED, base=0,
                                        pattern=[[-1, P]], channel_multiplier=1).then_inc(mask_ready, 1)

            mask(0)
            pool.wait_ge(ke_ready, HH * n_lev)
            pool.wait_ge(qe_ready, HH * n_lev)
            for n in range(N_FOX):
                if n + 1 < N_FOX:
                    mask(n + 1)
                for k in POOL_SUMS[n % 3] if n < 3 * len(extras) else ():
                    e = n // 3
                    w = wring[:, (e + AFTER_W_IN) % 2]
                    pool.wait_ge(scaled_ready, e * ACT_PARTS + k + 1)
                    if k == 1:
                        if e >= 2:
                            pool.wait_ge(x_full, e - 1)
                        first = w[:, 0]
                    else:
                        pool.wait_ge(part2_ready, e * (ACT_PARTS - 1) + k - 1)
                        first = part2[e % 2]
                    nc.gpsimd.tensor_tensor(part2[e % 2], first, w[:, k], ALU.add).then_inc(part2_ready, 1)

            def split_u(n, par):
                pool.wait_ge(uhi_ready, n + 1)
                nc.gpsimd.tensor_tensor(ulo[:, par], uraw[:, par], uhi[:, par].bitcast(F32), ALU.subtract
                                        ).then_inc(ulo_ready, 1)

            for n in range(HP + 2):
                split_u(n, n % 2)
            for what, *at in plan:
                if what == "up":
                    n0, count = at
                    with pool.Fori(0, count // 2) as i:
                        for par in range(2):
                            split_u(i * 2 + (n0 + par + 2), par)
                elif what == "maps":
                    tt, half, n0 = at
                    with pool.Fori(0, HALF // STEP) as i:
                        for par in range(2):
                            split_u(i * 2 + (n0 + par + 2), par)
            with pool.Fori(0, NF - 1) as g:
                for k in range(GROUP):
                    split_u(g * GROUP + (N_UP0 + k + 2), k % 2)
            for k in range(GROUP - 2):
                split_u((NF - 1) * GROUP + N_UP0 + k + 2, k % 2)

        @block.scalar
        def _(act):
            chain = [0]

            def link(ins):
                chain[0] += 1
                ins.then_inc(act_chain, 1)
                act.wait_ge(act_chain, chain[0])

            def move(job, dst, func=ACT.Copy, cols=W, split=None, **kw):
                act.wait_ge(a_full, a_job[job] + 1)
                src = a_bank(job)[:, 0:cols]
                if split:
                    src = src.rearrange("p (c v) -> p c v", c=split)
                nc.scalar.activation(dst, src, func, **kw).then_inc(a_done, 1)

            n_roots = [0]

            def roots(which, tiles, src, dst):
                for tt in tiles:
                    nc.scalar.activation(dst[:, tt, :], src[:, tt, :], ACT.Square,
                                         accum_out=stat[:, which, 0, tt:tt + 1]).then_inc(sumsq_ready, 1)
                n_roots[0] += len(tiles)
                act.wait_ge(sumsq_ready, n_roots[0])
                ts = slice(tiles[0], tiles[-1] + 1)
                nc.scalar.activation(stat[:, which, 1, ts], stat[:, which, 0, ts], ACT.Sqrt, bias=eps[:],
                                     scale=1.0 / D).then_inc(root_ready, 1)

            act.wait_ge(c_loaded, 16)
            nc.scalar.activation(cond[:, 1], cond[:, 0], ACT.Silu).then_inc(cond_ready, 1)
            act.wait_ge(x_loaded, 16 * NT)
            act.wait_ge(made, 2)
            roots(0, range(NT), x, sqs)
            act.wait_ge(mod_ready, 1)
            for k in range(1, KD, 2):
                move(("xT", k), hT[:, k], ACT.Identity, scale=scale[:, 0, k:k + 1], bias=shift[:, 0, k:k + 1])
            act.wait_ge(gam_ready, 1)
            nc.scalar.activation(gam[:], gam[:], ACT.Exp).then_inc(game_ready, 1)
            for tt in range(NT):
                move(("f", tt), logf[:, tt, :], ACT.Sigmoid)
            for h in range(HH):
                move(("hq", h), hqT[:, h], scale=HD ** -0.5)
            act.wait_ge(fz_ready, 1)
            link(nc.scalar.activation(ff[:, 2], ff[:, 1], ACT.Exp, scale=-1.0))
            nc.scalar.activation(ff[:, 3], ff[:, 2], ACT.Ln, bias=ones[:, 0:1]).then_inc(fsoft_ready, 1)
            act.wait_ge(f_ready, 1)
            nc.scalar.activation(logf[:], logf[:], ACT.Ln).then_inc(logf_ready, 1)
            for h in range(HH):
                move(("hk", h), hkT[:, h])
            for tt in range(NT):
                move(("hi", tt), hi[:, tt, :])
            for c in range(NT - 1):
                move(("suffix", c), cat[:, c, 0:512], ACT.Exp)

            def output_of(h):
                o_h = cat[:, :, 512 + h * HD:512 + (h + 1) * HD]
                move(("o", h), o_h, split=NT)
                act.wait_ge(a_done, a_job["o", h] + 1)
                if h:
                    act.wait_ge(hsum_ready, h)
                nc.scalar.activation(hsq[:].rearrange("p (c v) -> p c v", c=NT), o_h, ACT.Square
                                     ).then_inc(hsq_ready, 1)

            sides = [(fqT, ACT.Copy, FD ** -0.5), (fkT, ACT.Copy, 1.0), (fv, ACT.Copy, 1.0), (hg, ACT.Silu, 1.0)]
            for h in range(HH):
                if h:
                    act.wait_ge(diff_ready, h * n_lev)
                    act.wait_ge(expA_ready, h)
                move(("A", h), AT[:, 0])
                act.wait_ge(a_done, a_job["A", h] + 1)
                if h >= 2:
                    act.wait_ge(st_ready, h - 1)
                nc.scalar.activation(alast[:, h % 2], AT[:, 0].rearrange("p (c t) -> p c t", c=NT)[:, :, P - 1],
                                     ACT.Exp).then_inc(alast_ready, 1)
                dst, func, mul = sides[h]
                for j in range(-1, NT):
                    if j >= 0:
                        move(("side", h, j), dst[:, j], func, scale=mul)
                    for lev in (2 * j + 3, 2 * j + 4):
                        if lev < LEVELS:
                            n = h * n_lev + lev - 1
                            act.wait_ge(diff_ready, n + 1)
                            link(nc.scalar.activation(dec[:, n % 2], dec[:, n % 2], ACT.Abs))
                            nc.scalar.activation(dec[:, n % 2], dec[:, n % 2], ACT.Exp, scale=-1.0
                                                 ).then_inc(dec_ready, 1)
                    if j == 1 and h:
                        output_of(h - 1)
                nc.scalar.activation(AT[:, 1], AT[:, 0], ACT.Exp).then_inc(expA_ready, 1)
            output_of(HH - 1)
            act.wait_ge(hsum_ready, HH)
            nc.scalar.activation(hss[:, 1], hss[:, 0], ACT.Sqrt, bias=eps[:], scale=1.0 / HD
                                 ).then_inc(hroot_ready, 1)
            move(("fcol",), fcol[:].rearrange("p t h -> p (t h)"), cols=NT * FH)
            act.wait_ge(hcat_ready, 1)
            for h in range(FH):
                move(("nF", h), nFb[:, h], scale=-1.0)
            for n in range(N_FOX):
                tt, h = divmod(n, FH)
                w = (tt + 1) * P
                for k in ACT_SCALES[n % 3] if n < 3 * len(extras) else ():
                    e = n // 3
                    ring_slot = (e + AFTER_W_IN) % 2
                    if k == 0:
                        act.wait_ge(w_loaded[ring_slot], 16 * ((e + AFTER_W_IN) // 2 + 1))
                    nc.scalar.activation(wring[:, ring_slot, k], wring[:, ring_slot, k], ACT.Copy,
                                         scale=cond[:, 1, k:k + 1]).then_inc(scaled_ready, 1)
                act.wait_ge(rmax_ready, n + 1)
                nc.scalar.activation(pr[:, n % FR, 0:w], lg[:, n % FR, 0:w], ACT.Exp, bias=rmax[:, tt, h:h + 1],
                                     accum_out=rsum[:, 0, tt, h:h + 1]).then_inc(pr_ready, 1)
                if n >= FR:
                    act.wait_ge(pv_done, n - FR + 1)
                move(("pT", n), prT[:, n % FR, 0:w], cols=w)
                if n > FH and n % FH == 5:
                    for j in range(2):
                        move(("catT", tt - 1, j), hT[:, 4 * j:4 * j + 4, (tt - 1) * P:tt * P], split=4)
            for j in range(2):
                move(("catT", NT - 1, j), hT[:, 4 * j:4 * j + 4, (NT - 1) * P:], split=4)

            def split_input(tt):
                ts = slice(tt * P, (tt + 1) * P)
                for j in range(2):
                    act.wait_ge(h2T_ready, 2 * tt + j + 1)
                    ks = slice(4 * j, 4 * j + 4)
                    nc.scalar.activation(hhi[:, ks, ts], h2T[:, ks, ts], ACT.Copy).then_inc(hhi_ready, 1)

            def split_u(n, par):
                act.wait_ge(u_loaded[par], (n - par) * 8 + 16)
                nc.scalar.activation(uhi[:, par], uraw[:, par], ACT.Copy).then_inc(uhi_ready, 1)

            for tt in range(NT):
                for half in range(2):
                    move(("mix", tt, half), mix[:, tt, half * W:(half + 1) * W])
                act.wait_ge(a_done, a_job["mix", tt, 1] + 1)
                roots(0, [tt], mix, cat)
                if tt:
                    split_input(tt - 1)
                act.wait_ge(xmix_ready, tt + 1)
                roots(1, [tt], x, mix)
                if tt == 2:
                    split_u(0, 0)
                    split_u(1, 1)
            split_input(NT - 1)

            for n in range(HP):
                act.wait_ge(up_full, n + 1)
                nc.scalar.activation(qT[:, n], bank[UP_BANKS[n % 2]][:], ACT.Copy).then_inc(up_done, 1)
                split_u(n + 2, n % 2)
                act.wait_ge(up_done, n + 1)
                if n >= 2:
                    act.wait_ge(qss_done, n - 1)
                nc.scalar.activation(qsq[:, n % 2], qT[:, n], ACT.Square).then_inc(qsq_ready, 1)
            act.wait_ge(qss_done, HP)
            nc.scalar.activation(rq[:, 0], bank[6][:, 0:NT * HP].rearrange("p (t n) -> p t n", t=NT), ACT.Sqrt,
                                 bias=eps[:], scale=1.0 / P).then_inc(qroot_ready, 1)
            act.wait_ge(qroot_ready, 1)
            act.sem_inc(g_done, len(G_BANKS))

            def gelu_spilled(n, par, first=False):
                act.wait_ge(up_full, n + 1)
                if not first:
                    act.wait_ge(spilled[par], (n - (HP + par)) * 8)
                nc.scalar.activation(spill[:, par], bank[UP_BANKS[par]][:], ACT.Gelu).then_inc(up_done, 1)
                split_u(n + 2, par)

            halves_done = 0
            for what, *at in plan:
                if what == "up":
                    n0, count = at
                    start = 0
                    if n0 == HP:
                        act.wait_ge(hlo_ready, 2 * NT)
                        gelu_spilled(HP, 0, first=True)
                        gelu_spilled(HP + 1, 1, first=True)
                        start = 1
                    with act.Fori(start, count // 2) as i:
                        for par in range(2):
                            gelu_spilled(i * 2 + (n0 + par), par)
                elif what == "exp":
                    act.wait_ge(gmax_ready, at[0] + 1)
                    nc.scalar.activation(best[:], best[:], ACT.Exp).then_inc(gexp_ready, 1)
                elif what == "maps":
                    tt, half, n0 = at
                    if halves_done:
                        act.wait_ge(map_stored, 32 * halves_done)
                    halves_done += 1
                    with act.Fori(0, HALF // STEP) as i:
                        for qd in range(SQ):
                            act.wait_ge(g_full, i * SQ + ((2 * tt + half) * (HALF // QUAD) + qd + 1 + OHR))
                            dst = stage[:, :, bass.ds(i * STEP + qd * QUAD, QUAD)].rearrange("p i t -> p t i")
                            nc.scalar.activation(dst, bank[G_BANKS[qd % 4]][:].rearrange("p (t i) -> p t i", t=QUAD),
                                                 ACT.Copy).then_inc(g_done, 1)
                            if qd % (SQ // 2) == SQ // 2 - 1:
                                par = qd // (SQ // 2)
                                gelu_spilled(i * 2 + (n0 + par), par)
            def split_v(grp, k, which):
                act.wait_ge(v_loaded[k], grp * 16 + 16)
                nc.scalar.activation(sets[which][0][:, k], vraw[:, k], ACT.Copy).then_inc(vhi_ready, 1)

            def split_a(grp, k, which):
                act.wait_ge(av_ready, grp * GROUP + (k + 1))
                nc.scalar.activation(sets[which][2][:, k], av[:, k], ACT.Copy).then_inc(ahi_ready, 1)

            def fused(g, last):
                for k in range(GROUP):
                    n = g * GROUP + (N_UP0 + k)
                    act.wait_ge(up_full, n + 1)
                    nc.scalar.activation(gel[:, k], bank[UP_BANKS[k % 2]][:], ACT.Gelu).then_inc(up_done, 1)
                    if not last or k + 2 < GROUP:
                        split_u(n + 2, k % 2)
                    if k == 0:
                        act.wait_ge(y_full, g * 8 + 1)
                    split_v(g, k, 0)
                    split_a(g, k, 0)

            act.wait_ge(routed, 1)
            act.wait_ge(s_full, NT * (HP // 4))
            for k in range(GROUP):
                split_v(0, k, 0)
            for k in range(GROUP):
                n = N_UP0 + k
                act.wait_ge(up_full, n + 1)
                nc.scalar.activation(gel[:, k], bank[UP_BANKS[k % 2]][:], ACT.Gelu).then_inc(up_done, 1)
                split_u(n + 2, k % 2)
            act.wait_ge(last_stored[0], 16)
            for k in range(GROUP):
                split_a(0, k, 0)
            with act.Fori(1, NF - 1) as g:
                fused(g, False)
            fused(NF - 1, True)

            def second_only(grp, which, guard=True):
                for k in range(GROUP):
                    if k == 0 and guard:
                        act.wait_ge(y_full, (grp - 1) * 8 + 1)
                    split_v(grp, k, which)
                    split_a(grp, k, which)

            with act.Fori(0, ND // 2) as i:
                second_only(i * 2 + NF, 1)
                second_only(i * 2 + (NF + 1), 0)
            act.wait_ge(y_done, 8 * (NF + ND) + len(Y_BANKS))
            roots(0, range(NT), acc, vraw)

        @block.vector
        def _(dve):
            chain = [0]

            def link(ins):
                chain[0] += 1
                ins.then_inc(dve_chain, 1)
                dve.wait_ge(dve_chain, chain[0])

            def full(job):
                dve.wait_ge(d_full, d_job[job] + 1)
                return d_bank(job)

            def mod_chunk(i, chs, b):
                n0, n1 = 4 * chs[0], 4 * chs[-1] + 4
                link(nc.vector.tensor_tensor(modt[:, n0:n1], b[:, 0:n1 - n0], bada[:, 24 * i + n0:24 * i + n1],
                                             ALU.add))
                dve.sem_inc(x_done if i else d_done, 1)
                if chs[-1] == 3:
                    nc.vector.scalar_tensor_tensor(scale[:, i], modt[:, KD:2 * KD], 1.0, gains[:, i],
                                                   ALU.add, ALU.mult)
                    link(nc.vector.tensor_copy(shift[:, i], modt[:, 0:KD]))

            def gate_chunk(name, half):
                gate, post = (gate_a, post_a) if name == "gate_a" else (gate_f, post_f)
                b = bank[X_BANK]
                cols = slice(half * W, (half + 1) * W)
                link(nc.vector.tensor_tensor(gate[:, cols], gate[:, cols], b[:], ALU.add))
                nc.vector.tensor_tensor(gate[:, cols], gate[:, cols], post[:, cols], ALU.mult
                                        ).then_inc(x_done, 1)

            nc.vector.memset(eps[:], EPS).then_inc(made, 1)
            nc.vector.memset(ones[:], 1.0).then_inc(made, 1)
            dve.wait_ge(early_loaded, 16 * len(early))
            dve.wait_ge(cond_ready, 1)

            def silu_times(ch):
                if ch < 3:
                    dve.wait_ge(ada_loaded[ch], 16)
                else:
                    dve.wait_ge(w_loaded[0], 16)
                w = ada[ch]
                link(nc.vector.tensor_scalar(part0[:, ch], w[:, 0], cond[:, 1, 0:1], None, ALU.mult))
                for k in range(1, KD):
                    link(nc.vector.scalar_tensor_tensor(part0[:, ch], w[:, k], cond[:, 1, k:k + 1], part0[:, ch],
                                                        ALU.mult, ALU.add))
                dve.sem_inc(part_ready, 1)
                if ch == 3:
                    dve.sem_inc(w_used, 1)

            silu_times(0)
            dve.wait_ge(root_ready, 1)
            link(nc.vector.reciprocal(stat[:, 0, 2], stat[:, 0, 1]))
            for tt in range(NT):
                nc.vector.tensor_scalar(cat[:, tt], x[:, tt], stat[:, 0, 2, tt:tt + 1], None, ALU.mult
                                        ).then_inc(xn_ready, 1)
            for ch in range(1, 4):
                silu_times(ch)
            mod_chunk(0, range(4), full(("mod",)))
            dve.sem_inc(mod_ready, 1)
            for k in range(0, KD, 2):
                b = full(("xT", k))
                nc.vector.tensor_scalar(hT[:, k], b[:], scale[:, 0, k:k + 1], shift[:, 0, k:k + 1],
                                        ALU.mult, ALU.add).then_inc(d_done, 1)
            link(nc.vector.tensor_tensor(gmx[:], gam[:, 0], gam[:, 1], ALU.max))
            nc.vector.tensor_tensor(gam[:, 0], gam[:, 0], gmx[:], ALU.subtract)
            nc.vector.tensor_tensor(gam[:, 1], gam[:, 1], gmx[:], ALU.subtract).then_inc(gam_ready, 1)
            dve.wait_ge(game_ready, 1)
            link(nc.vector.tensor_tensor(gmx[:], gam[:, 0], gam[:, 1], ALU.add))
            link(nc.vector.reciprocal(gmx[:], gmx[:]))
            link(nc.vector.tensor_tensor(gam[:, 0], gam[:, 0], gmx[:], ALU.mult))
            link(nc.vector.tensor_scalar(gam[:, 1], gam[:, 0], -1.0, 1.0, ALU.mult, ALU.add))
            for tt in range(NT):
                dve.wait_ge(a_done, a_job["f", tt] + 1)
                link(nc.vector.tensor_tensor(logf[:, tt], logf[:, tt], gam[:, 1], ALU.mult))
                link(nc.vector.tensor_tensor(logf[:, tt], logf[:, tt], gam[:, 0], ALU.add))
                ins = nc.vector.tensor_scalar(hk[:, tt], logf[:, tt], -1.0, 1.0, ALU.mult, ALU.add)
            ins.then_inc(f_ready, 1)
            dve.wait_ge(late_loaded, 16 * len(late))
            b = full(("ff",))
            link(nc.vector.tensor_tensor(ff[:, 0], b[:, 0:NT * FH].rearrange("p (t h) -> p t h", t=NT),
                                         bfox[:].unsqueeze(1).to_broadcast([P, NT, FH]), ALU.add))
            dve.sem_inc(d_done, 1)
            nc.vector.scalar_tensor_tensor(ff[:, 1], ff[:, 0], -1.0, ff[:, 0], ALU.mult, ALU.max).then_inc(fz_ready, 1)
            dve.wait_ge(fsoft_ready, 1)
            nc.vector.scalar_tensor_tensor(ff[:, 0], ff[:, 0], 0.0, ff[:, 3], ALU.min, ALU.subtract
                                           ).then_inc(lff_ready, 1)
            dve.wait_ge(a_done, a_job["hk", HH - 1] + 1)
            for c in range(NT - 1):
                dve.wait_ge(a_done, a_job["suffix", c] + 1)
                nc.vector.tensor_tensor(hk[:, c], hk[:, c], cat[:, c, 0:512], ALU.mult).then_inc(kd_ready, 1)

            def difference(h, lev):
                n = h * n_lev + lev - 1
                half = 1 << (lev - 1)
                a = AT[:, 0].rearrange("p (g u) -> p g u", u=2 * half)
                mid = a[:, :, half - 1:half].to_broadcast([P, S // (2 * half), 2 * half])
                if n >= 2:
                    dve.wait_ge(ke_ready, n - 1)
                nc.vector.tensor_tensor(dec[:, n % 2].rearrange("p (g u) -> p g u", u=2 * half), a, mid,
                                        ALU.subtract).then_inc(diff_ready, 1)

            def decay_q(h, lev):
                n = h * n_lev + lev - 1
                dve.wait_ge(dec_ready, n + 1)
                nc.vector.tensor_tensor(qe[:, n % 2], hqT[:, h], dec[:, n % 2], ALU.mult).then_inc(qe_ready, 1)

            def next_difference(h, lev):
                if lev < LEVELS:
                    dve.wait_ge(qe_ready, h * n_lev + lev - 2)
                    difference(h, lev)

            def keep(h, lev):
                b = full(("level", h, lev))
                nc.vector.copy_predicated(sc[:, h % 2].rearrange("p (c t) -> p c t", c=NT),
                                          lmask[:, lev].unsqueeze(1).to_broadcast([P, NT, P]),
                                          b[:].rearrange("p (c t) -> p c t", c=NT)).then_inc(d_done, 1)

            def sum_squares(h):
                dve.wait_ge(hsq_ready, h + 1)
                nc.vector.tensor_reduce(hss[:, 0, :, h:h + 1].rearrange("p c o -> p (c o)"),
                                        hsq[:].rearrange("p (c v) -> p c v", c=NT), AX.X, ALU.add
                                        ).then_inc(hsum_ready, 1)

            for h in range(HH):
                dve.wait_ge(a_done, a_job["A", h] + 1)
                difference(h, 1)
                difference(h, 2)
                b = full(("kv", h))
                dve.wait_ge(alast_ready, h + 1)
                if h >= 2:
                    dve.wait_ge(a_full, a_job["o", h - 2] + 1)
                link(nc.vector.memset(sc[:, h % 2], 0.0))
                link(nc.vector.tensor_copy(st[:, h % 2, 0], b[:, 0:HD]))
                link(nc.vector.scalar_tensor_tensor(st[:, h % 2, 1], st[:, h % 2, 0], alast[:, h % 2, 1:2],
                                                    b[:, HD:2 * HD], ALU.mult, ALU.add))
                link(nc.vector.scalar_tensor_tensor(st[:, h % 2, 2], st[:, h % 2, 1], alast[:, h % 2, 2:3],
                                                    b[:, 2 * HD:3 * HD], ALU.mult, ALU.add))
                dve.sem_inc(d_done, 1)
                dve.sem_inc(st_ready, 1)
                decay_q(h, 1)
                next_difference(h, 3)
                for lev in range(LEVELS):
                    full(("level", h, lev))
                    if lev + 2 < LEVELS:
                        decay_q(h, lev + 2)
                        next_difference(h, lev + 4)
                    if lev:
                        dve.wait_ge(d_done, d_job["level", h, lev - 1] + 1)
                    keep(h, lev)
                dve.wait_ge(expA_ready, h + 1)
                nc.vector.tensor_tensor(AT[:, 1], AT[:, 1], hqT[:, h], ALU.mult).then_inc(qa_ready, 1)
                if h:
                    sum_squares(h - 1)
            sum_squares(HH - 1)
            dve.wait_ge(hroot_ready, 1)
            link(nc.vector.reciprocal(hss[:, 0], hss[:, 1]))
            for c in range(NT):
                o_c = cat[:, c, 512:1024].rearrange("p (h v) -> p h v", h=HH)
                nc.vector.tensor_tensor(o_c, o_c, hss[:, 0, c].unsqueeze(2).to_broadcast([P, HH, HD]), ALU.mult)
                ins = nc.vector.tensor_tensor(hg[:, c], hg[:, c], hng[:], ALU.mult)
            link(ins)
            ins = nc.vector.tensor_tensor(cat[:, :, 512:1024], cat[:, :, 512:1024], hg[:], ALU.mult)
            ins.then_inc(hcat_ready, 1)
            def logits(n):
                tt, h = divmod(n, FH)
                w = (tt + 1) * P
                b = full(("logits", n))
                if n >= FR:
                    dve.wait_ge(pr_ready, n - FR + 1)
                nc.vector.scalar_tensor_tensor(lg[:, n % FR, 0:w], nFb[:, h, 0:w], fcol[:, tt, h:h + 1], b[:, 0:w],
                                               ALU.add, ALU.add).then_inc(d_done, 1)

            def fox_out(tt):
                dve.wait_ge(pv_done, (tt + 1) * FH)
                link(nc.vector.reciprocal(rsum[:, 1, tt], rsum[:, 0, tt]))
                nc.vector.tensor_tensor(cat[:, tt, 0:512].rearrange("p (h d) -> p h d", h=FH),
                                        bank[O_BANK][:].rearrange("p (h d) -> p h d", h=FH),
                                        rsum[:, 1, tt].unsqueeze(2).to_broadcast([P, FH, FD]), ALU.mult
                                        ).then_inc(fcat_ready, 1)

            dve.wait_ge(a_done, a_job["nF", FH - 1] + 1)
            logits(0)
            logits(1)
            for n in range(N_FOX):
                tt, h = divmod(n, FH)
                if n + 2 < N_FOX:
                    logits(n + 2)
                dve.wait_ge(mask_ready, n + 1)
                link(nc.vector.tensor_reduce(rmax[:, tt, h:h + 1], lg[:, n % FR, 0:(tt + 1) * P], AX.X, ALU.max))
                nc.vector.tensor_scalar(rmax[:, tt, h:h + 1], rmax[:, tt, h:h + 1], -1.0, None, ALU.mult
                                        ).then_inc(rmax_ready, 1)
                if tt and h == 0:
                    fox_out(tt - 1)
                if n and n % 3 == 0 and n <= 3 * len(extras):
                    dve.wait_ge(part3_ready, n)
                    dve.wait_ge(part2_ready, n // 3 * (ACT_PARTS - 1))
                    dve.sem_inc(w_used, 1)
                if n < 3 * len(extras):
                    e, k = n // 3, ACT_PARTS + n % 3
                    ring_slot = (e + AFTER_W_IN) % 2
                    if n % 3 == 0:
                        dve.wait_ge(w_loaded[ring_slot], 16 * ((e + AFTER_W_IN) // 2 + 1))
                        if e >= 2:
                            dve.wait_ge(x_full, e - 1)
                        nc.vector.tensor_scalar(part3[e % 2], wring[:, ring_slot, k], cond[:, 1, k:k + 1], None,
                                                ALU.mult).then_inc(part3_ready, 1)
                    else:
                        dve.wait_ge(part3_ready, n)
                        nc.vector.scalar_tensor_tensor(part3[e % 2], wring[:, ring_slot, k], cond[:, 1, k:k + 1],
                                                       part3[e % 2], ALU.mult, ALU.add).then_inc(part3_ready, 1)
                if n - 1 in extra_at:
                    e = extra_at.index(n - 1)
                    what, *at = extras[e]
                    dve.wait_ge(x_full, e + 1)
                    mod_chunk(1, at[1:], bank[X_BANK]) if what == "mod" else gate_chunk(what, *at)
            fox_out(NT - 1)
            def residual(tt):
                dve.wait_ge(root_ready, 2 * tt + 2)
                link(nc.vector.reciprocal(stat[:, 0, 2, tt:tt + 1], stat[:, 0, 1, tt:tt + 1]))
                link(nc.vector.scalar_tensor_tensor(mix[:, tt], mix[:, tt], stat[:, 0, 2, tt:tt + 1], gate_a[:],
                                                    ALU.mult, ALU.mult))
                nc.vector.tensor_tensor(x[:, tt], x[:, tt], mix[:, tt], ALU.add).then_inc(xmix_ready, 1)
                if tt:
                    low_part(tt - 1)
                dve.wait_ge(root_ready, 2 * tt + 3)
                link(nc.vector.reciprocal(stat[:, 1, 2, tt:tt + 1], stat[:, 1, 1, tt:tt + 1]))
                nc.vector.tensor_scalar(cat[:, tt], x[:, tt], stat[:, 1, 2, tt:tt + 1], None, ALU.mult
                                        ).then_inc(xn_ready, 1)

            def peer_input(tt):
                ts = slice(tt * P, (tt + 1) * P)
                for j in range(2):
                    b = full(("h2T", tt, j))
                    ks = slice(4 * j, 4 * j + 4)
                    nc.vector.tensor_tensor(h2T[:, ks, ts], b[:].rearrange("p (k t) -> p k t", k=4),
                                            scale[:, 1, ks].unsqueeze(2).to_broadcast([P, 4, P]), ALU.mult
                                            ).then_inc(d_done, 1)
                    dve.wait_ge(d_done, d_job["h2T", tt, j] + 1)
                    nc.vector.tensor_tensor(h2T[:, ks, ts], h2T[:, ks, ts],
                                            shift[:, 1, ks].unsqueeze(2).to_broadcast([P, 4, P]), ALU.add
                                            ).then_inc(h2T_ready, 1)

            def low_part(tt):
                ts = slice(tt * P, (tt + 1) * P)
                for j in range(2):
                    ks = slice(4 * j, 4 * j + 4)
                    dve.wait_ge(hhi_ready, 2 * tt + j + 1)
                    nc.vector.tensor_tensor(hlo[:, ks, ts], h2T[:, ks, ts], hhi[:, ks, ts].bitcast(F32),
                                            ALU.subtract).then_inc(hlo_ready, 1)

            for tt in range(NT):
                if tt:
                    peer_input(tt - 1)
                residual(tt)
            peer_input(NT - 1)
            low_part(NT - 1)

            dve.wait_ge(qroot_ready, 1)
            link(nc.vector.reciprocal(rq[:, 1], rq[:, 0]))
            pairs = [s1, s2, s3]
            c1, c2, c3 = [s[:].rearrange("p n k -> p (n k)").rearrange("p (h a b) -> p h a b", h=PH, a=TOPK)
                          for s in pairs]
            f1, f3 = [s[:].rearrange("p n k -> p (n k)").rearrange("p (h c) -> p h c", h=PH) for s in (s1, s3)]
            halves = top[:].rearrange("p (h two) k -> p h two k", two=2)
            halvesf = topf[:].rearrange("p (h two) k -> p h two k", two=2)
            posk = pos[:, 0].rearrange("p (h k) -> p h k", h=PH)

            def take_scores(tt):
                for q4 in range(HP // 4):
                    dve.wait_ge(s_full, tt * (HP // 4) + (q4 + 1))
                    ns = slice(4 * q4, 4 * q4 + 4)
                    nc.vector.tensor_tensor(s1[:, ns], bank[SCORE_BANKS[q4 % 2]][:].rearrange("p (n k) -> p n k", n=4),
                                            rq[:, 1, tt, ns].unsqueeze(2).to_broadcast([P, 4, NK]), ALU.mult
                                            ).then_inc(s_done, 1)
                dve.wait_ge(s_done, (tt + 1) * (HP // 4))

            take_scores(0)
            for tt in range(NT):
                for n in range(HP):
                    ins = nc.vector.max(top[:, n, 0:8], s1[:, n])
                link(ins)
                for n in range(HP):
                    nc.vector.max_index(topi[:, n, 0:8], top[:, n, 0:8], s1[:, n])
                    ins = nc.vector.match_replace(s2[:, n], top[:, n, 0:8], s1[:, n], MASKED)
                link(ins)
                for n in range(HP):
                    ins = nc.vector.max(top[:, n, 8:16], s2[:, n])
                link(ins)
                for n in range(HP):
                    ins = nc.vector.max_index(topi[:, n, 8:16], top[:, n, 8:16], s2[:, n])
                link(ins)
                nc.vector.tensor_copy(topf[:], topi[:])
                link(nc.vector.tensor_tensor(c3, halves[:, :, 0].unsqueeze(3).to_broadcast([P, PH, TOPK, TOPK]),
                                            halves[:, :, 1].unsqueeze(2).to_broadcast([P, PH, TOPK, TOPK]), ALU.add))
                for h in range(PH):
                    ins = nc.vector.max(best[:, h, 0:8], f3[:, h])
                link(ins)
                for h in range(PH):
                    nc.vector.max_index(posk[:, h, 0:8], best[:, h, 0:8], f3[:, h])
                    ins = nc.vector.match_replace(f1[:, h], best[:, h, 0:8], f3[:, h], MASKED)
                link(ins)
                for h in range(PH):
                    ins = nc.vector.max(best[:, h, 8:16], f1[:, h])
                link(ins)
                for h in range(PH):
                    nc.vector.max_index(posk[:, h, 8:16], best[:, h, 8:16], f1[:, h])
                link(nc.vector.tensor_copy(gsum[:, 0], best[:, :, 0]))
                nc.vector.tensor_tensor(best[:], best[:], gsum[:, 0].unsqueeze(2).to_broadcast([P, PH, TOPK]),
                                        ALU.subtract).then_inc(gmax_ready, 1)
                nc.vector.tensor_scalar(pos[:, 1], pos[:, 0], 4, None, ALU.logical_shift_right)
                link(nc.vector.tensor_scalar(pos[:, 2], pos[:, 0], TOPK - 1, None, ALU.bitwise_and))
                link(nc.vector.tensor_copy(posf[:], pos[:, 1:3]))
                for p, cp in ((0, c1), (1, c2)):
                    ins = nc.vector.tensor_tensor(
                        cp.rearrange("p h a b -> p (h a) b"), posf[:, p].unsqueeze(2).to_broadcast([P, SLOTS, TOPK]),
                        iota16.unsqueeze(1).to_broadcast([P, SLOTS, TOPK]), ALU.is_equal)
                link(ins)
                for p, cp in ((0, c1), (1, c2)):
                    ins = nc.vector.tensor_tensor(cp, cp, halvesf[:, :, p].unsqueeze(2).to_broadcast(
                        [P, PH, TOPK, TOPK]), ALU.mult)
                link(ins)
                for p, cp in ((0, c1), (1, c2)):
                    nc.vector.tensor_reduce(slot[:, p], cp.rearrange("p h a b -> p (h a) b"), AX.X, ALU.add)
                dve.wait_ge(gexp_ready, tt + 1)
                link(nc.vector.tensor_reduce(gsum[:, 0], best[:], AX.X, ALU.add))
                link(nc.vector.reciprocal(gsum[:, 1], gsum[:, 0]))
                nc.vector.tensor_tensor(slot[:, 2].rearrange("p (h k) -> p h k", h=PH), best[:],
                                        gsum[:, 1].unsqueeze(2).to_broadcast([P, PH, TOPK]), ALU.mult
                                        ).then_inc(slot_ready, 1)
                dve.wait_ge(slotT_full, tt + 1)
                nc.vector.tensor_copy(slotT[:].rearrange("p a t -> p (a t)"), bank[SLOT_BANK][:, 0:3 * P]
                                      ).then_inc(slotT_done, 1)
                dve.wait_ge(slotT_done, tt + 1)
                for half in range(2):
                    with dve.Fori(0, HALF // STEP) as i:
                        for qd in range(SQ):
                            dve.wait_ge(g_full, i * SQ + ((2 * tt + half) * (HALF // QUAD) + qd + 1))
                            o = (qd % OHR) * QUAD
                            ts = bass.ds(i * STEP + (half * HALF + qd * QUAD), QUAD)
                            nc.vector.tensor_tensor(ohB[:, o:o + QUAD], iota[:].unsqueeze(1).to_broadcast([P, QUAD, P]),
                                                    slotT[:, 1, ts].unsqueeze(2).to_broadcast([P, QUAD, P]),
                                                    ALU.is_equal)
                            for j in range(QUAD):
                                t = bass.ds(i * STEP + (half * HALF + qd * QUAD + j), 1)
                                ins = nc.vector.tensor_scalar(ohA[:, o + j], iota[:], slotT[:, 0, t],
                                                              slotT[:, 2, t], ALU.is_equal, ALU.mult)
                            ins.then_inc(onehot_ready, 1)
                    if half == 0 and tt + 1 < NT:
                        take_scores(tt + 1)
            dve.wait_ge(onehot_ready, S // QUAD)
            dve.sem_inc(routed, 1)

            for par in range(2):
                dve.wait_ge(spilled[par], SPILLED * 8)
            dve.wait_ge(s_full, NT * (HP // 4))
            link(nc.vector.memset(h2T[:], 0.0))
            dve.sem_inc(y_done, len(Y_BANKS))

            def weigh(grp, k):
                dve.wait_ge(g_loaded[k // 2], grp * 16 + 16)
                nc.vector.tensor_tensor(av[:, k].rearrange("p (c t) -> p c t", t=HALF),
                                        gel[:, k].rearrange("p (c t) -> p c t", t=HALF),
                                        gmap[:, k // 2, :, k % 2], ALU.mult).then_inc(av_ready, 1)

            def split_v(grp, k, which):
                hi_, lo_ = sets[which][0:2]
                dve.wait_ge(vhi_ready, grp * GROUP + (k + 1))
                nc.vector.tensor_tensor(lo_[:, k], vraw[:, k], hi_[:, k].bitcast(F32), ALU.subtract
                                        ).then_inc(vlo_ready, 1)

            def split_a(grp, k, which):
                hi_, lo_ = sets[which][2:4]
                dve.wait_ge(ahi_ready, grp * GROUP + (k + 1))
                nc.vector.tensor_tensor(lo_[:, k], av[:, k], hi_[:, k].bitcast(F32), ALU.subtract
                                        ).then_inc(alo_ready, 1)

            def add_y(grp, blk):
                dve.wait_ge(y_full, grp * 8 + (blk + 2))
                a = acc[:, blk // 2, (blk % 2) * W:(blk % 2 + 1) * W]
                nc.vector.tensor_tensor(a, a, bank[Y_BANKS[blk % 4]][:], ALU.add).then_inc(y_done, 1)

            def fused(g):
                for blk in range(4, 8):
                    add_y(g - 1, blk)
                for k in range(GROUP):
                    dve.wait_ge(up_done, g * GROUP + (N_UP0 + k + 1))
                    weigh(g, k)
                    split_v(g, k, 0)
                    split_a(g, k, 0)
                for blk in range(4):
                    add_y(g, blk)

            def second_only(g, grp, which, blocks):
                for k in range(GROUP):
                    dve.wait_ge(s_loaded[k], g * 16 + 16)
                    weigh(grp, k)
                    split_v(grp, k, which)
                    split_a(grp, k, which)
                    for blk in blocks[k]:
                        add_y(grp - 1, blk)

            for k in range(GROUP):
                split_v(0, k, 0)
            dve.wait_ge(last_stored[1], 16)
            for k in range(GROUP):
                dve.wait_ge(up_done, N_UP0 + k + 1)
                weigh(0, k)
            dve.wait_ge(last_stored[0], 16)
            for k in range(GROUP):
                split_a(0, k, 0)
            for blk in range(4):
                add_y(0, blk)
            with dve.Fori(1, NF) as g:
                fused(g)
            second_only(0, NF, 1, [[4], [5], [6], [7]])
            second_only(1, NF + 1, 0, [[0, 1], [2, 3], [4, 5], [6, 7]])
            with dve.Fori(1, ND // 2) as i:
                second_only(i * 2, i * 2 + NF, 1, [[0, 1], [2, 3], [4, 5], [6, 7]])
                second_only(i * 2 + 1, i * 2 + (NF + 1), 0, [[0, 1], [2, 3], [4, 5], [6, 7]])
            for blk in range(8):
                add_y(NF + ND - 1, blk)
            dve.wait_ge(root_ready, 2 * NT + 2)
            link(nc.vector.reciprocal(stat[:, 0, 2], stat[:, 0, 1]))
            for tt in range(NT):
                ins = nc.vector.scalar_tensor_tensor(acc[:, tt], acc[:, tt], stat[:, 0, 2, tt:tt + 1], gate_f[:],
                                                     ALU.mult, ALU.mult)
            link(ins)
            for tt in range(NT):
                nc.vector.tensor_tensor(acc[:, tt], acc[:, tt], x[:, tt], ALU.add).then_inc(out_ready, 1)

        @block.tensor
        def _(pe):
            mm = nc.tensor.matmul

            def a_open(job):
                if a_job[job] >= 3:
                    pe.wait_ge(a_done, a_job[job] - 2)
                return a_bank(job)

            def d_open(job):
                if d_job[job] >= 3:
                    pe.wait_ge(d_done, d_job[job] - 2)
                return d_bank(job)

            chunk = [1]

            def weights():
                n = chunk[0]
                pe.wait_ge(w_loaded[n % 2], 16 * (n // 2 + 1))
                return wring[:, n % 2]

            def used(ins):
                ins.then_inc(w_used, 1)
                chunk[0] += 1

            def by_feature(w, b, m, src):
                for k in range(KD):
                    ins = mm(b[:], w[:, k, m * P:(m + 1) * P], src[:, k], start=k == 0, stop=k == KD - 1)
                return ins

            def by_token(w, b, tt, src):
                for k in range(KD):
                    ins = mm(b[:], src[:, k, tt * P:(tt + 1) * P], w[:, k], start=k == 0, stop=k == KD - 1)
                return ins

            def by_columns(b, m0, parts):
                for m in range(4):
                    for i, part in enumerate(parts):
                        ins = mm(b[:, m0 + m:m0 + m + 1], part[:, m * P:(m + 1) * P], ones[:, 0:1],
                                 start=i == 0, stop=i == len(parts) - 1)
                return ins

            def finish(ins, full, n):
                ins.then_inc(full, 1)
                pe.wait_ge(full, n)
                pe.sem_inc(w_used, 1)
                chunk[0] += 1

            def transposes(b, src, n):
                for i in range(n):
                    ins = nc.tensor.transpose(b[:, i * P:(i + 1) * P], src(i), ident[:])
                return ins

            pe.wait_ge(made, 2)
            b = d_open(("mod",))
            for ch in range(4):
                pe.wait_ge(part_ready, ch + 1)
                ins = by_columns(b, 4 * ch, [part0[:, ch]])
            ins.then_inc(d_full, 1)
            pe.wait_ge(early_loaded, 16 * len(early))
            pe.wait_ge(xn_ready, NT)
            for k in range(KD):
                b, full = (a_open(("xT", k)), a_full) if k % 2 else (d_open(("xT", k)), d_full)
                transposes(b, lambda tt: cat[:, tt, k * P:(k + 1) * P], NT).then_inc(full, 1)
            pe.wait_ge(d_done, d_job["xT", KD - 2] + 1)
            pe.wait_ge(a_done, a_job["xT", KD - 1] + 1)
            w = weights()
            for tt in range(NT):
                ins = by_token(w, a_open(("f", tt)), tt, hT)
                if tt < NT - 1:
                    ins.then_inc(a_full, 1)
            finish(ins, a_full, a_job["f", NT - 1] + 1)
            w = weights()
            for h in range(HH):
                ins = by_feature(w, a_open(("hq", h)), h, hT)
                if h < HH - 1:
                    ins.then_inc(a_full, 1)
            finish(ins, a_full, a_job["hq", HH - 1] + 1)
            pe.wait_ge(late_loaded, 16 * len(late))
            b = d_open(("ff",))
            for tt in range(NT):
                for k in range(KD):
                    ins = mm(b[:, tt * FH:(tt + 1) * FH], hT[:, k, tt * P:(tt + 1) * P], wff[:, k],
                             start=k == 0, stop=k == KD - 1)
            ins.then_inc(d_full, 1)
            pe.wait_ge(f_ready, 1)
            for h in range(HH):
                transposes(a_open(("hk", h)), lambda c: hk[:, c, h * HD:(h + 1) * HD], NT).then_inc(a_full, 1)
            w = weights()
            for tt in range(NT):
                ins = by_token(w, a_open(("hi", tt)), tt, hT)
                if tt < NT - 1:
                    ins.then_inc(a_full, 1)
            finish(ins, a_full, a_job["hi", NT - 1] + 1)
            pe.wait_ge(logf_ready, 1)
            for c in range(NT - 1):
                mm(a_open(("suffix", c))[:], tri[:, W:W + P], logf[:, c], start=True, stop=True).then_inc(a_full, 1)

            def output_of(h):
                b = a_open(("o", h))
                pe.wait_ge(d_done, d_job["level", h, LEVELS - 1] + 1)
                pe.wait_ge(st_ready, h + 1)
                pe.wait_ge(qa_ready, h + 1)
                for c in range(NT):
                    cs = slice(c * P, (c + 1) * P)
                    ins = mm(b[:, cs], sc[:, h % 2, cs], hi[:, c, h * HD:(h + 1) * HD], start=True, stop=c == 0)
                    if c:
                        ins = mm(b[:, cs], AT[:, 1, cs], st[:, h % 2, c - 1], start=False, stop=True)
                ins.then_inc(a_full, 1)

            for h in range(HH):
                hs = slice(h * HD, (h + 1) * HD)
                b = a_open(("A", h))
                for c in range(NT):
                    ins = mm(b[:, c * P:(c + 1) * P], logf[:, c, hs], tri[:, 0:P], start=True, stop=True)
                ins.then_inc(a_full, 1)
                b = d_open(("kv", h))
                pe.wait_ge(kd_ready, NT - 1)
                pe.wait_ge(a_done, a_job["hi", NT - 1] + 1)
                for c in range(NT - 1):
                    ins = mm(b[:, c * HD:(c + 1) * HD], hk[:, c, hs], hi[:, c, hs], start=True, stop=True)
                ins.then_inc(d_full, 1)
                w = weights()
                for j in range(NT):
                    b = a_open(("side", h, j))
                    ins = by_feature(w, b, j, hT) if h < 2 else by_token(w, b, j, hT)
                    if j < NT - 1:
                        ins.then_inc(a_full, 1)
                    else:
                        finish(ins, a_full, a_job["side", h, j] + 1)
                    if j == 1 and h:
                        output_of(h - 1)
                    for lev in (2 * j, 2 * j + 1):
                        b = d_open(("level", h, lev))
                        n = h * n_lev + lev - 1
                        if lev:
                            pe.wait_ge(qe_ready, n + 1)
                            pe.wait_ge(ke_ready, n + 1)
                        for c in range(NT):
                            cs = slice(c * P, (c + 1) * P)
                            ins = mm(b[:, cs], ke[:, n % 2, cs] if lev else hkT[:, h, cs],
                                     qe[:, n % 2, cs] if lev else hqT[:, h, cs], start=True, stop=True)
                        ins.then_inc(d_full, 1)
            output_of(HH - 1)
            pe.wait_ge(lff_ready, 1)
            b = a_open(("fcol",))
            for tt in range(NT):
                for c in range(tt + 1):
                    ins = mm(b[:, tt * FH:(tt + 1) * FH], tri[:, 0:P] if c == tt else tri[:, P:2 * P], ff[:, 0, c],
                             start=c == 0, stop=c == tt)
            ins.then_inc(a_full, 1)
            for h in range(FH):
                b = a_open(("nF", h))
                for c in range(NT):
                    ins = mm(b[:, c * P:W], ff[:, 0, c, h:h + 1].to_broadcast([P, P]), tri[:, 0:W - c * P],
                             start=c == 0, stop=c == NT - 1)
                ins.then_inc(a_full, 1)

            def logits(n):
                tt, h = divmod(n, FH)
                ps = slice(FD * (h % 2), FD * (h % 2) + FD)
                mm(d_open(("logits", n))[:, 0:(tt + 1) * P], fqT[ps, h // 2, tt * P:(tt + 1) * P],
                   fkT[ps, h // 2, 0:(tt + 1) * P], start=True, stop=True).then_inc(d_full, 1)

            def values(n):
                tt, h = divmod(n, FH)
                pe.wait_ge(a_done, a_job["pT", n] + 1)
                if tt and h == 0:
                    pe.wait_ge(fcat_ready, tt)
                o = bank[O_BANK]
                for c in range(tt + 1):
                    ins = mm(o[:, h * FD:(h + 1) * FD], prT[:, n % FR, c * P:(c + 1) * P],
                             fv[:, c, h * FD:(h + 1) * FD], start=c == 0, stop=c == tt)
                ins.then_inc(pv_done, 1)

            def cat_transposes(tt):
                pe.wait_ge(fcat_ready, tt + 1)
                pe.wait_ge(hcat_ready, 1)
                for j in range(2):
                    transposes(a_open(("catT", tt, j)), lambda i: cat[:, tt, (4 * j + i) * P:(4 * j + i + 1) * P], 4
                               ).then_inc(a_full, 1)

            for n in range(3):
                logits(n)
            for n in range(N_FOX):
                if n + 3 < N_FOX:
                    logits(n + 3)
                if n in extra_at:
                    e = extra_at.index(n)
                    parts = [part2[e % 2], part3[e % 2]]
                    pe.wait_ge(part2_ready, (ACT_PARTS - 1) * (e + 1))
                    pe.wait_ge(part3_ready, (KD - ACT_PARTS) * (e + 1))
                    if e:
                        pe.wait_ge(x_done, e)
                    if extras[e][0] == "mod":
                        ins = by_columns(bank[X_BANK], 0, parts)
                    else:
                        mm(bank[X_BANK][:], ones[:], parts[0], start=True, stop=False)
                        ins = mm(bank[X_BANK][:], ones[:], parts[1], start=False, stop=True)
                    ins.then_inc(x_full, 1)
                    chunk[0] += 1
                pe.wait_ge(pr_ready, n + 1)
                transposes(a_open(("pT", n)), lambda c: pr[:, n % FR, c * P:(c + 1) * P], n // FH + 1
                           ).then_inc(a_full, 1)
                if n:
                    values(n - 1)
                if n > FH and n % FH == 5:
                    cat_transposes(n // FH - 1)
            values(N_FOX - 1)
            cat_transposes(NT - 1)
            n = chunk[0]
            pe.wait_ge(w_loaded[n % 2], 16 * (n // 2 + 1))
            pe.wait_ge(w_loaded[(n + 1) % 2], 16 * ((n + 1) // 2 + 1))

            def input_transposes(tt):
                pe.wait_ge(xn_ready, NT + tt + 1)
                for j in range(2):
                    transposes(d_open(("h2T", tt, j)), lambda i: cat[:, tt, (4 * j + i) * P:(4 * j + i + 1) * P], 4
                               ).then_inc(d_full, 1)

            def up(n, par):
                pe.wait_ge(ulo_ready, n + 1)
                pe.wait_ge(up_done, n - 1)
                b = bank[UP_BANKS[par]]
                for c in range(KD):
                    mm(b[:], uhi[:, par, c], hhi[:, c], start=c == 0, stop=False)
                    mm(b[:], uhi[:, par, c], hlo[:, c], start=False, stop=False)
                    ins = mm(b[:], ulo[:, par, c], hhi[:, c], start=False, stop=c == KD - 1)
                ins.then_inc(up_full, 1)

            def up_part(n, ts):
                pe.wait_ge(ulo_ready, n + 1)
                for c in range(KD):
                    mm(bank[UP_BANKS[n]][:, ts], uhi[:, n, c], hhi[:, c, ts], start=c == 0, stop=False)
                    mm(bank[UP_BANKS[n]][:, ts], uhi[:, n, c], hlo[:, c, ts], start=False, stop=False)
                    ins = mm(bank[UP_BANKS[n]][:, ts], ulo[:, n, c], hhi[:, c, ts], start=False, stop=c == KD - 1)
                return ins

            for tt in range(NT):
                pe.wait_ge(a_done, a_job["catT", tt, 1] + 1)
                by_token(wring[:, n % 2], a_open(("mix", tt, 0)), tt, hT).then_inc(a_full, 1)
                b = a_open(("mix", tt, 1))
                for k in range(KD):
                    if tt and k == 5:
                        input_transposes(tt - 1)
                    ins = mm(b[:], hT[:, k, tt * P:(tt + 1) * P], wring[:, (n + 1) % 2, k],
                             start=k == 0, stop=k == KD - 1)
                ins.then_inc(a_full, 1)
            pe.wait_ge(a_done, a_job["mix", NT - 1, 1] + 1)
            pe.wait_ge(hlo_ready, NT)
            for n in range(2):
                up_part(n, slice(0, S // 2))
            input_transposes(NT - 1)
            pe.wait_ge(hlo_ready, 2 * NT)
            for n in range(2):
                up_part(n, slice(S // 2, S)).then_inc(up_full, 1)

            def square_sums(n):
                pe.wait_ge(qsq_ready, n + 1)
                for tt in range(NT):
                    ins = mm(bank[6][:, tt * HP + n:tt * HP + n + 1], qsq[:, n % 2, tt * P:(tt + 1) * P], ones[:, 0:1],
                             start=True, stop=True)
                ins.then_inc(qss_done, 1)

            for n in range(1, HP):
                if n > 1:
                    up(n, n % 2)
                square_sums(n - 1)
            square_sums(HP - 1)

            def scores(tt):
                if tt:
                    pe.wait_ge(slotT_done, tt)
                for q4 in range(HP // 4):
                    done = tt * (HP // 4) + q4 - 1
                    if done > 0:
                        pe.wait_ge(s_done, done)
                    for n in range(4 * q4, 4 * q4 + 4):
                        ins = mm(bank[SCORE_BANKS[q4 % 2]][:, (n % 4) * NK:(n % 4 + 1) * NK],
                                 qT[:, n, tt * P:(tt + 1) * P], keys[:, n], start=True, stop=True)
                    ins.then_inc(s_full, 1)

            pe.wait_ge(keys_loaded, 16)
            scores(0)
            pe.sem_inc(g_full, OHR)
            for what, *at in plan:
                if what == "up":
                    n0, count = at
                    with pe.Fori(0, count // 2) as i:
                        for par in range(2):
                            up(i * 2 + (n0 + par), par)
                elif what == "slots":
                    tt, = at
                    pe.wait_ge(slot_ready, tt + 1)
                    transposes(bank[SLOT_BANK], lambda a: slot[:, a], 3).then_inc(slotT_full, 1)
                elif what == "maps":
                    tt, half, n0 = at
                    with pe.Fori(0, HALF // STEP) as i:
                        for qd in range(SQ):
                            idx = i * SQ + ((2 * tt + half) * (HALF // QUAD) + qd)
                            pe.wait_ge(onehot_ready, idx + 1)
                            pe.wait_ge(g_done, idx + 1)
                            for j in range(QUAD):
                                o = (qd % OHR) * QUAD + j
                                ins = mm(bank[G_BANKS[qd % 4]][:, j * NK:(j + 1) * NK], ohB[:, o], ohA[:, o],
                                         start=True, stop=True)
                            ins.then_inc(g_full, 1)
                            if qd % (SQ // 2) == SQ // 2 - 1:
                                par = qd // (SQ // 2)
                                up(i * 2 + (n0 + par), par)
                    if half == 0 and tt + 1 < NT:
                        scores(tt + 1)

            pe.sem_inc(y_full, 1)

            def down(b, blk, k, which):
                vhi, vlo, ahi, alo = sets[which]
                ts = slice(blk // 2 * P, (blk // 2 + 1) * P)
                ds = slice(blk % 2 * W, (blk % 2 + 1) * W)
                mm(b[:], ahi[:, k, ts], vhi[:, k, ds], start=k == 0, stop=False)
                mm(b[:], ahi[:, k, ts], vlo[:, k, ds], start=False, stop=False)
                return mm(b[:], alo[:, k, ts], vhi[:, k, ds], start=False, stop=k == GROUP - 1)

            def second(grp, which):
                pe.wait_ge(vlo_ready, grp * GROUP + (GROUP - 1))
                pe.wait_ge(alo_ready, grp * GROUP + (GROUP - 1))
                for blk in range(2):
                    pe.wait_ge(y_done, grp * 8 + (blk + 1))
                    for k in range(GROUP - 1):
                        down(bank[Y_BANKS[blk]], blk, k, which)
                pe.wait_ge(vlo_ready, grp * GROUP + GROUP)
                pe.wait_ge(alo_ready, grp * GROUP + GROUP)
                for blk in range(2):
                    down(bank[Y_BANKS[blk]], blk, GROUP - 1, which).then_inc(y_full, 1)
                for blk in range(2, 8):
                    pe.wait_ge(y_done, grp * 8 + (blk + 1))
                    for k in range(GROUP):
                        ins = down(bank[Y_BANKS[blk % 4]], blk, k, which)
                    ins.then_inc(y_full, 1)

            with pe.Fori(0, NF) as g:
                for k in range(GROUP):
                    up(g * GROUP + (N_UP0 + k), k % 2)
                second(g, 0)
            with pe.Fori(0, ND // 2) as i:
                second(i * 2 + NF, 1)
                second(i * 2 + (NF + 1), 0)


def kernel(x, c, w_ada, b_ada, pre_mix_g, post_mix_g, w_in, b_fox_f, hgrn_gamma, hgrn_norm_g, w_out,
           pre_ffn_g, post_ffn_g, peer_w_q, peer_sub_keys, peer_u, peer_v):
    import concourse.bacc as _bacc
    import numpy as np
    from concourse.bass_utils import run_bass_kernel_spmd as _run

    D = x.shape[-1]
    S = x.shape[1]
    n_keys = peer_sub_keys.shape[3]

    def arr(a):
        return np.ascontiguousarray(np.asarray(a))

    def columns(v):
        return arr(np.asarray(v).reshape(-1, P).T)

    s = np.arange(P)
    const_f = np.concatenate([
        np.eye(P), (s[:, None] <= s[None, :]), np.ones((P, 3 * P)), (s[:, None] > s[None, :]),
        np.broadcast_to(s[None, :], (P, P))], axis=1).astype(np.float32)
    masks = [s[:, None] == s[None, :]]
    for lev in range(1, 8):
        half = 1 << (lev - 1)
        same = s[:, None] // (2 * half) == s[None, :] // (2 * half)
        masks.append(same & (s[:, None] % (2 * half) < half) & (s[None, :] % (2 * half) >= half))
    const_m = arr(np.stack(masks, axis=1).astype(np.int32))

    b = np.asarray(b_ada)[0].reshape(6, D)
    width = hgrn_gamma.shape[1]
    fox = np.concatenate([np.asarray(b_fox_f)[0], np.zeros(width - b_fox_f.shape[1], np.float32)])
    arrays = {
        "x_in": arr(np.asarray(x)[0]),
        "c_col": columns(np.asarray(c)[0]),
        "w_ada": arr(np.asarray(w_ada)[0]),
        "b_ada_col": columns(np.asarray(b_ada)[0]),
        "gains_col": arr(np.stack([columns(np.asarray(pre_mix_g)[0]), columns(np.asarray(pre_ffn_g)[0])], axis=1)),
        "rows": arr(np.stack([b[2], b[5], np.asarray(post_mix_g)[0], np.asarray(post_ffn_g)[0]])),
        "w_in": arr(np.asarray(w_in)[0]),
        "hgrn_rows": arr(np.concatenate([np.asarray(hgrn_gamma), np.asarray(hgrn_norm_g), fox[None]])),
        "w_out": arr(np.asarray(w_out)[0]),
        "w_q": arr(np.asarray(peer_w_q)[0].reshape(D // P, P, -1, P).transpose(2, 1, 0, 3)),
        "keys_t": arr(np.asarray(peer_sub_keys)[0].reshape(-1, n_keys, P).transpose(2, 0, 1)),
        "u_t": arr(np.asarray(peer_u)[0].reshape(n_keys, n_keys, D // P, P).transpose(0, 3, 2, 1)),
        "v_in": arr(np.asarray(peer_v)[0]),
        "const_f": const_f,
        "const_m": const_m,
    }
    nc = _bacc.Bacc("TRN2", target_bir_lowering=False, num_devices=1)
    args = [nc.dram_tensor(n, a.shape, mybir.dt.from_np(a.dtype), kind="ExternalInput").ap()
            for n, a in arrays.items()]
    gate_map = nc.dram_tensor("gate_map", (8, P, n_keys, S // 8), F32, kind="Internal").ap()
    gelus = nc.dram_tensor("gelus", (n_keys, P, S), F32, kind="Internal").ap()
    out = nc.dram_tensor("y_out", (S, D), F32, kind="ExternalOutput").ap()
    hybrid_block(nc, *args, gate_map, gelus, out)
    r = _run(nc, [arrays], core_ids=[0])
    return r.results[0]["y_out"].reshape(1, S, D)
```
